# Optimizing a Trainium2 kernel written in Bass

```python
import jax, jax.numpy as jnp
from jax import lax
import numpy as np

D_MODEL = 1024
BATCH = 1
SEQ = 512
DEPTH = 1
DEC_BATCH = 8
DEC_SEQ = 16
PAST_LEN = 512

CHUNK = 64
N_HEADS = 8
HEAD_DIM = 64
ATTN_WIDTH = N_HEADS * HEAD_DIM
CONV_WIDTH = 512
CONV_K = 3
Q_BLOCK = 128
N_GROUPS = 4
EXPERTS_PER_GROUP = 4
N_EXPERTS = N_GROUPS * EXPERTS_PER_GROUP
TOP_K = 2
D_EXPERT = 512
PLE_DIM = 256
EPS = 1e-6
IN_SIZES = (ATTN_WIDTH, ATTN_WIDTH, ATTN_WIDTH, CONV_WIDTH, CONV_WIDTH, CONV_WIDTH, D_MODEL, D_MODEL)
IN_TOTAL = sum(IN_SIZES)

kernel_name = "stickbreak_shortconv_hmoe_stream_step"

def rmsnorm(x, g):
    xf = x.astype(jnp.float32)
    y = xf * lax.rsqrt(jnp.mean(xf * xf, axis=-1, keepdims=True) + EPS) * g.astype(jnp.float32)
    return y.astype(x.dtype)

def mix_projections(x, ln_mix, w_in, q_norm, k_norm):
    h = rmsnorm(x, ln_mix)
    z = h @ w_in
    cuts = np.cumsum(IN_SIZES)[:-1].tolist()
    q, k, v, cb, cc, cx, ga, gb = jnp.split(z, cuts, axis=-1)
    hs = x.shape[:-1] + (N_HEADS, HEAD_DIM)
    q = rmsnorm(q.reshape(hs), q_norm)
    k = rmsnorm(k.reshape(hs), k_norm)
    v = v.reshape(hs)
    u = cc * cx
    return q, k, v, cb, u, ga, gb

def stick_breaking(q, k, v, q_pos, k_pos):
    z = jnp.einsum('bqhd,bkhd->bhqk', q.astype(jnp.float32), k.astype(jnp.float32)) * (HEAD_DIM ** -0.5)
    mask = k_pos[None, :] < q_pos[:, None]
    log_keep = jnp.where(mask, jax.nn.log_sigmoid(-z), 0.0)
    after = lax.cumsum(log_keep, axis=3, reverse=True) - log_keep
    a = jnp.where(mask, jnp.exp(jax.nn.log_sigmoid(z) + after), 0.0)
    return jnp.einsum('bhqk,bkhd->bqhd', a, v.astype(jnp.float32)).astype(v.dtype)

def stick_breaking_blocked(q, k, v):
    b, s = q.shape[0], q.shape[1]
    k_pos = jnp.arange(s)

    def one_block(i):
        qs = lax.dynamic_slice_in_dim(q, i * Q_BLOCK, Q_BLOCK, axis=1)
        return stick_breaking(qs, k, v, i * Q_BLOCK + jnp.arange(Q_BLOCK), k_pos)

    out = lax.map(one_block, jnp.arange(s // Q_BLOCK))
    return out.transpose(1, 0, 2, 3, 4).reshape(b, s, N_HEADS, HEAD_DIM)

def short_conv(u, u_past, conv_w):
    t = u.shape[1]
    ext = jnp.concatenate([u_past.astype(u.dtype), u], axis=1)
    y = sum(conv_w[j] * ext[:, j:j + t, :] for j in range(CONV_K))
    return y, ext[:, -(CONV_K - 1):, :]

def hier_moe(h, w_rg, b_rg, w_re, b_re, w_eg, w_eu, w_ed):
    lg = (h @ w_rg + b_rg).astype(jnp.float32)
    pg = jax.nn.softmax(lg, axis=-1)
    g_sel = jnp.argmax(lg, axis=-1)
    p_sel = jnp.max(pg, axis=-1)
    le = (h @ w_re + b_re).astype(jnp.float32).reshape(h.shape[:-1] + (N_GROUPS, EXPERTS_PER_GROUP))
    le_sel = jnp.take_along_axis(le, g_sel[..., None, None], axis=-2)[..., 0, :]
    vals, idx = lax.top_k(le_sel, TOP_K)
    w2 = jax.nn.softmax(vals, axis=-1)
    eidx = g_sel[..., None] * EXPERTS_PER_GROUP + idx
    gate = p_sel[..., None] * jnp.sum(jax.nn.one_hot(eidx, N_EXPERTS, dtype=jnp.float32) * w2[..., None], axis=-2)
    gate = gate.astype(h.dtype)
    out = jnp.zeros_like(h)
    for e in range(N_EXPERTS):
        y = (jax.nn.silu(h @ w_eg[e]) * (h @ w_eu[e])) @ w_ed[e]
        out = out + gate[..., e:e + 1] * y
    return out

def merge_and_channel(x, attn_out, cb, conv_y, ga, gb, p, lw):
    ya = attn_out.reshape(attn_out.shape[:-2] + (ATTN_WIDTH,)) @ lw['w_attn_branch']
    yb = (cb * conv_y) @ lw['w_conv_branch']
    m = jax.nn.sigmoid(ga) * ya + jax.nn.sigmoid(gb) * yb
    x = x + m @ lw['w_out']
    x = x + hier_moe(rmsnorm(x, lw['ln_ffn']), lw['w_router_group'], lw['b_router_group'],
                     lw['w_router_expert'], lw['b_router_expert'],
                     lw['w_exp_gate'], lw['w_exp_up'], lw['w_exp_down'])
    gate = jax.nn.sigmoid(rmsnorm(x, lw['ln_ple']) @ lw['w_ple_gate'])
    return x + gate * (p @ lw['w_ple_proj'])

def setup_inputs(seed: int = 0) -> dict:
    key = jax.random.key(seed)
    ks = jax.random.split(key, 32)

    def nrm(k, shape, scale=1.0):
        return jax.random.normal(k, shape, jnp.float32) * scale

    L = DEPTH
    return {
        'x_prompt': nrm(ks[0], (BATCH, SEQ, D_MODEL)),
        'x_sample': nrm(ks[1], (DEC_BATCH, DEC_SEQ, D_MODEL)),
        'cache_k': nrm(ks[2], (L, DEC_BATCH, PAST_LEN, N_HEADS, HEAD_DIM)),
        'cache_v': nrm(ks[3], (L, DEC_BATCH, PAST_LEN, N_HEADS, HEAD_DIM)),
        'state_conv': nrm(ks[4], (L, DEC_BATCH, CONV_K - 1, CONV_WIDTH)),
        'p_prompt': nrm(ks[5], (L, BATCH, SEQ, PLE_DIM)),
        'p_sample': nrm(ks[6], (L, DEC_BATCH, DEC_SEQ, PLE_DIM)),
        'ln_mix': 1.0 + nrm(ks[7], (L, D_MODEL), 0.05),
        'w_in': nrm(ks[8], (L, D_MODEL, IN_TOTAL), D_MODEL ** -0.5),
        'q_norm': 1.0 + nrm(ks[9], (L, HEAD_DIM), 0.05),
        'k_norm': 1.0 + nrm(ks[10], (L, HEAD_DIM), 0.05),
        'conv_w': nrm(ks[11], (L, CONV_K, CONV_WIDTH), CONV_K ** -0.5),
        'w_attn_branch': nrm(ks[12], (L, ATTN_WIDTH, D_MODEL), ATTN_WIDTH ** -0.5),
        'w_conv_branch': nrm(ks[13], (L, CONV_WIDTH, D_MODEL), CONV_WIDTH ** -0.5),
        'w_out': nrm(ks[14], (L, D_MODEL, D_MODEL), D_MODEL ** -0.5),
        'ln_ffn': 1.0 + nrm(ks[15], (L, D_MODEL), 0.05),
        'w_router_group': nrm(ks[16], (L, D_MODEL, N_GROUPS), D_MODEL ** -0.5),
        'b_router_group': nrm(ks[17], (L, N_GROUPS), 0.01),
        'w_router_expert': nrm(ks[18], (L, D_MODEL, N_EXPERTS), D_MODEL ** -0.5),
        'b_router_expert': nrm(ks[19], (L, N_EXPERTS), 0.01),
        'w_exp_gate': nrm(ks[20], (L, N_EXPERTS, D_MODEL, D_EXPERT), D_MODEL ** -0.5),
        'w_exp_up': nrm(ks[21], (L, N_EXPERTS, D_MODEL, D_EXPERT), D_MODEL ** -0.5),
        'w_exp_down': nrm(ks[22], (L, N_EXPERTS, D_EXPERT, D_MODEL), D_EXPERT ** -0.5),
        'ln_ple': 1.0 + nrm(ks[23], (L, D_MODEL), 0.05),
        'w_ple_gate': nrm(ks[24], (L, D_MODEL, D_MODEL), D_MODEL ** -0.5),
        'w_ple_proj': nrm(ks[25], (L, PLE_DIM, D_MODEL), PLE_DIM ** -0.5),
    }

def reference(x_prompt, x_sample, cache_k, cache_v, state_conv, p_prompt, p_sample,
              ln_mix, w_in, q_norm, k_norm, conv_w, w_attn_branch, w_conv_branch, w_out,
              ln_ffn, w_router_group, b_router_group, w_router_expert, b_router_expert,
              w_exp_gate, w_exp_up, w_exp_down, ln_ple, w_ple_gate, w_ple_proj):
    xp, xs = x_prompt, x_sample
    kp_l, vp_l, cp_l, ks_l, vs_l, cs_l = [], [], [], [], [], []
    for i in range(DEPTH):
        lw = dict(w_attn_branch=w_attn_branch[i], w_conv_branch=w_conv_branch[i], w_out=w_out[i],
                  ln_ffn=ln_ffn[i], w_router_group=w_router_group[i], b_router_group=b_router_group[i],
                  w_router_expert=w_router_expert[i], b_router_expert=b_router_expert[i],
                  w_exp_gate=w_exp_gate[i], w_exp_up=w_exp_up[i], w_exp_down=w_exp_down[i],
                  ln_ple=ln_ple[i], w_ple_gate=w_ple_gate[i], w_ple_proj=w_ple_proj[i])

        q, k, v, cb, u, ga, gb = mix_projections(xp, ln_mix[i], w_in[i], q_norm[i], k_norm[i])
        attn = stick_breaking_blocked(q, k, v)
        u0 = jnp.zeros((u.shape[0], CONV_K - 1, CONV_WIDTH), u.dtype)
        conv_y, conv_new = short_conv(u, u0, conv_w[i])
        xp = merge_and_channel(xp, attn, cb, conv_y, ga, gb, p_prompt[i], lw)
        kp_l.append(k); vp_l.append(v); cp_l.append(conv_new)

        q, k, v, cb, u, ga, gb = mix_projections(xs, ln_mix[i], w_in[i], q_norm[i], k_norm[i])
        past = cache_k.shape[2]
        t = xs.shape[1]
        k_all = jnp.concatenate([cache_k[i].astype(k.dtype), k], axis=1)
        v_all = jnp.concatenate([cache_v[i].astype(v.dtype), v], axis=1)
        attn = stick_breaking(q, k_all, v_all, past + jnp.arange(t), jnp.arange(past + t))
        conv_y, conv_new = short_conv(u, state_conv[i], conv_w[i])
        xs = merge_and_channel(xs, attn, cb, conv_y, ga, gb, p_sample[i], lw)
        ks_l.append(k); vs_l.append(v); cs_l.append(conv_new)

    new_k_prompt = jnp.stack(kp_l)
    new_v_prompt = jnp.stack(vp_l)
    new_conv_prompt = jnp.stack(cp_l)
    new_k_sample = jnp.stack(ks_l)
    new_v_sample = jnp.stack(vs_l)
    new_conv_sample = jnp.stack(cs_l)
    return (xp, xs, new_k_prompt, new_v_prompt, new_conv_prompt, new_k_sample, new_v_sample, new_conv_sample)


_drawn_inputs = setup_inputs


def setup_inputs(seed=0):
    import zlib

    import numpy as np

    out = dict(_drawn_inputs(seed))
    spreads = {}
    factors = {'q_norm': 4.24, 'b_router_group': 11.064, 'b_router_expert': 5.901, 'ln_ple': 7.294}
    for name, (base, spread) in spreads.items():
        noise = np.random.default_rng([zlib.crc32(name.encode()), seed]).standard_normal(out[name].shape)
        drawn = base * np.exp(spread * noise) if base else spread * noise
        out[name] = __import__('jax').numpy.asarray(drawn.astype(out[name].dtype))
    for name, factor in factors.items():
        out[name] = (out[name] * factor).astype(out[name].dtype)
    return out
```

```python
from contextlib import ExitStack

import numpy as np
import concourse.bass as bass
from concourse import mybir

F32, F32R, BF16, I32 = mybir.dt.float32, mybir.dt.float32r, mybir.dt.bfloat16, mybir.dt.int32
ACT, ALU, AX = mybir.ActivationFunctionType, mybir.AluOpType, mybir.AxisListType

P = 128
D = 1024
KD = D // P
TP, B, TS = 512, 8, 16
T = TP + B * TS
NT = T // P
W = 512
KW = W // P
H, HD = 8, 64
HP = H // 2
PAST = 512
KB = PAST // P
NG, EG = 4, 4
NE = NG * EG
FE = 512
PLE = 256
EPS = 1e-6
C = 128
OV_TILES = (T - C) // P
RING = 4

W_IN_COLS = [0, 1, 2, 4, 5, 3]
U_A, U_C, U_D, U_P, U_M, U_G = 0, 24, 48, 56, 58, 250
CH_A, CH_C, CH_D, CH_P, CH_G = 0, 6, 14, 16, 18
NSTREAM = 12
G_X, G_STATE, G_QK, G_CONV, G_PLE, G_R, G_F = 0, 10, 11, 21, 22, 27, 37


class Unit:

    def __init__(self, c, stride=0, k=0):
        self.c, self.stride, self.k, self.slot = c, stride, k, c % RING

    def plus(self, n):
        return Unit(self.c + n, self.stride, self.k)

    def count(self, less=0):
        return (self.c + 1 - less) + self.stride * self.k

    def turn16(self):
        return 16 * (self.c // RING + 1) + 16 * (self.stride // RING) * self.k

    def mm(self, less=0):
        return 5 * (self.c + 1 - less) + 5 * self.stride * self.k


def program(nc, I, O):
    ctx = ExitStack()
    with ctx:
        base = 16512
        cursor = [base]

        def at(name, shape, dt, off):
            return nc.alloc_sbuf_tensor_at(name, shape, dt, offset=off)

        def size(shape, dt=F32):
            n = 2 if dt == BF16 else 4
            for s in shape[1:]:
                n *= s
            return (n + 31) // 32 * 32

        def sb(name, shape, dt=F32):
            t = at(name, shape, dt, cursor[0])
            cursor[0] += size(shape, dt)
            return t

        class Region:
            def __init__(self, nbytes):
                self.start = cursor[0]
                self.end = self.start + nbytes
                cursor[0] += nbytes

            def lay(self, *specs):
                off, out = self.start, []
                for name, shape, dt in specs:
                    out.append(at(name, shape, dt, off))
                    off += size(shape, dt)
                assert off <= self.end, (specs, off, self.end)
                return out if len(out) > 1 else out[0]

        ident = sb("ident", [P, P])
        um = sb("um", [P, P])
        neg = sb("neg", [P, P])
        before = sb("before", [P, P], BF16)
        onesb = sb("onesb", [P, P], BF16)
        ones1 = sb("ones1", [P, 1])
        zero = sb("zero", [P, P])
        mhalf = sb("mhalf", [P, 8])
        lnb_off = cursor[0]
        lnb = sb("lnb", [P, D])
        qkg = sb("qkg", [P, 2, HD])
        convw = sb("convw", [P, 3, KW])
        rbias = sb("rbias", [P, NG + NE])
        wr = sb("wr", [P, KD, NG + NE])
        ss = sb("ss", [P, 3 * NT])
        rms = sb("rms", [P, 3 * NT])
        rr = sb("rr", [P, 3 * NT])
        ssq = sb("ssq", [P, 10, H])
        msq = sb("msq", [P, 10, H])
        rq = sb("rq", [P, 10, H])
        cpk = sb("cpk", [P, KW, 2 + 2 * B])
        lg = sb("lg", [P, NT, NG + NE])
        desc = sb("desc", [P, 4])
        eidx = sb("eidx", [P, NE])
        gmax, cm1, v1, v2, vdiff, vexp, vsum, gsum = [
            sb(name, [P, NT]) for name in ("gmax", "cm1", "v1", "v2", "vdiff", "vexp", "vsum", "gsum")]
        gdiff, gexp, lsel2 = [sb(name, [P, NT, 4]) for name in ("gdiff", "gexp", "lsel2")]
        ovm = sb("ovm", [P, 1])
        free_ = sb("free_", [P, 1])
        og = sb("og", [P, NT, 4])
        ok = sb("ok", [P, 2, NT, 4])
        cand = sb("cand", [P, NT, 4])
        lsel = sb("lsel", [P, NT, 4])
        prod = sb("prod", [P, NT, 4, 4])
        Mk = sb("Mk", [P, 2, NT, NE])
        Mb = sb("Mb", [P, NT, NE], BF16)
        rk = sb("rk", [P, NT, NE])
        mr = sb("mr", [P, 2, NT, NE])
        slotf = sb("slotf", [P, 4, 2, NT])
        gate = sb("gate", [P, 2, NT])
        slot = sb("slot", [P, 2, NT], I32)
        flag = sb("flag", [1, 1], I32)
        spn = sb("spn", [TS, P])
        tmpn = sb("tmpn", [TS, P])
        an = sb("an", [TS, 2, P])
        qbd = sb("qbd", [P, 2, HP, 2 * TS])
        ktn = sb("ktn", [P, 2, HP, TS])
        af = sb("af", [P, HP, P])
        raw = sb("raw", [P, RING, 2, W])
        whi = sb("whi", [P, RING, 2, W], F32R)
        wlo = sb("wlo", [P, RING, 2, W], F32R)

        XR = Region(NT * D * 4)
        HT = Region(2 * KD * T * 4)
        CT = Region(2 * KW * T * 4)
        AT = Region(2 * KW * T * 4)
        QK = Region(2 * KW * T * 4)
        VV = Region(NT * W * 4)
        TAIL = Region(229344 - cursor[0])

        x = XR.lay(("x", [P, NT, D], F32))
        hh, hl = HT.lay(("hh", [P, KD, T], F32R), ("hl", [P, KD, T], F32R))
        ch, cl = CT.lay(("ch", [P, KW, T], F32R), ("cl", [P, KW, T], F32R))
        ah, al = AT.lay(("ah", [P, KW, T], F32R), ("al", [P, KW, T], F32R))
        qT, kT = QK.lay(("qT", [P, KW, T], F32), ("kT", [P, KW, T], F32))
        v = VV.lay(("v", [P, NT, W], F32))
        hn, zb, sqb, qn1, qn2 = AT.lay(("hn", [P, 2, D], F32), ("zb", [P, 2, W], F32), ("sqb", [P, 1, W], F32),
                                       ("qn1", [P, 1, W], F32), ("qn2", [P, 2, W], F32))
        junk = TAIL.lay(("junk", [P, D], F32))
        ccT, yc = XR.lay(("ccT", [P, KW, T], F32), ("yc", [P, KW, T], F32))
        up, us = TAIL.lay(("up", [P, KW, 2 + TP], F32), ("us", [P, KW, B, 2 + TS], F32))
        ncv = at("ncv", [2 + 2 * B, W], F32, AT.start)
        st = at("st", [2 * B, W], F32, VV.start)
        tm0, tm1, sp0, sp1 = XR.lay(("tm0", [P, 1280], F32), ("tm1", [P, 1280], F32),
                                    ("sp0", [P, 1280], F32), ("sp1", [P, 1280], F32))
        a0, a1 = TAIL.lay(("a0", [P, 1280], F32), ("a1", [P, 1280], F32))
        tmp1280, sp1280, a1280 = [tm0, tm1], [sp0, sp1], [a0, a1]
        vc, tms, sps = XR.lay(("vc", [P, 2, KB, W], F32), ("tms", [P, W], F32), ("sps", [P, W], F32))
        kc, as0 = TAIL.lay(("kc", [P, KB, W], F32), ("as0", [P, W], F32))
        ktc, as1 = VV.lay(("ktc", [P, KB, HP, P], F32), ("as1", [P, W], F32))
        vn = at("vn", [TS, 2, W], F32, lnb_off)
        a_s = [as0, as1]
        m = QK.lay(("m", [P, KD, T], F32))
        sg = VV.lay(("sg", [P, KW, T], F32))
        mt = TAIL.lay(("mt", [P, KW, T], F32))
        h2 = QK.lay(("h2", [P, NT, D], F32))
        h2T = at("h2T", [P, KD, T], F32, VV.start)
        praw, junk2 = CT.lay(("praw", [P, NT, PLE], F32), ("junk2", [P, D], F32))
        ph, pl = [at(n, [P, 2, T], F32R, CT.start + KW * T * 4 + i * 2 * T * 4) for i, n in enumerate(("ph", "pl"))]
        pp = AT.lay(("pp", [P, NT, D], F32))
        xe, xh, xl, si, hm, mh, ml, y = HT.lay(
            ("xe", [P, 2, D], F32), ("xh", [P, KD, P], F32R), ("xl", [P, KD, P], F32R), ("si", [P, FE], F32),
            ("hm", [P, FE], F32), ("mh", [P, FE // P, P], F32R), ("ml", [P, FE // P, P], F32R), ("y", [P, 2, D], F32))
        oxT, omT = CT.lay(("oxT", [P, KD, P], F32), ("omT", [P, FE // P, P], F32))
        NYG = 4
        yg = at("yg", [P, NYG, D], F32, VV.start)
        hn3, eo = QK.lay(("hn3", [P, 2, D], F32), ("eo", [P, 4, W], F32))

        bank = [ctx.enter_context(nc.psum_tensor(f"bank{i}", [P, 512], F32)) for i in range(8)]
        Xd = nc.dram_tensor("moe_rows", ((NE * C) + NE * OV_TILES * P, D), F32, kind="Internal").ap()
        Yd = nc.dram_tensor("moe_out", ((NE * C) + NE * OV_TILES * P, D), F32, kind="Internal").ap()

        def sem(name):
            return ctx.enter_context(nc.semaphore(name))

        s_const = sem("constants_loaded")
        s_ln = sem("norm_weights_loaded")
        s_x = [sem(f"x_loaded{t}") for t in range(NT)]
        s_made = sem("constants_made")
        s_pc = sem("pool_step")
        s_vc = sem("vector_step")
        s_raw = [sem(f"raw_loaded{i}") for i in range(RING)]
        s_hi = sem("weights_hi")
        s_lo = sem("weights_lo")
        s_mm = sem("products_done")
        s_free = sem("banks_read")
        s_sq = sem("squares_summed")
        s_r = sem("rms_ready")
        s_hn = sem("rows_normed")
        s_tr = sem("transposed")
        s_trh = sem("transposed_hi")
        s_trf = sem("transposed_read")
        s_qsq = sem("head_squares")
        s_ssq = sem("head_sums")
        s_rq = sem("head_rms")
        s_qn1 = sem("head_scaled")
        s_qn2 = sem("head_normed")
        s_ko = [sem(f"k_stored{i}") for i in range(2)]
        s_vout = sem("v_stored")
        s_state = sem("conv_state_loaded")
        s_ch = sem("gated_conv_hi")
        s_cl = sem("gated_conv_lo")
        s_cpk = sem("last_inputs_packed")
        s_ncvo = sem("conv_state_stored")
        s_zero = sem("rows_zeroed")
        s_z = sem("scores")
        s_ln1 = sem("log_terms")
        s_spr = sem("softplus")
        s_sp = sem("softplus_masked")
        s_acc = sem("log_sums")
        s_ea = sem("weights_exp")
        s_am = sem("weights_masked")
        s_av = sem("head_pairs_summed")
        s_ah = sem("attn_hi")
        s_al = sem("attn_lo")
        s_kc = sem("cache_k_loaded")
        s_vcl = [sem(f"cache_v_loaded{i}") for i in range(2)]
        s_qb = sem("queries_placed")
        s_kt = sem("cache_k_transposed")
        s_kta = sem("cache_kT_scalar")
        s_ktv = sem("cache_kT_vector")
        s_zs = sem("sample_scores")
        s_lns = sem("sample_log_terms")
        s_sps = sem("sample_softplus")
        s_spn = sem("sample_softplus_masked")
        s_accs = sem("sample_log_sums")
        s_eas = sem("sample_weights_exp")
        s_ams = sem("sample_weights_masked")
        s_avs = sem("sample_values")
        s_af = sem("sample_attn_kept")
        s_m = sem("merged")
        s_mh = sem("merged_hi")
        s_ml = sem("merged_lo")
        s_xr = sem("x_reloaded")
        s_ple = sem("ple_rows_loaded")
        s_rt = sem("router_logits")
        s_rx = sem("router_exps")
        s_d = sem("router_differences")
        s_M = sem("choices")
        s_rk = sem("ranks")
        s_slot = sem("slots")
        s_ovm = sem("overflow_rows_marked")
        s_ov = sem("overflow_sum")
        s_flag = sem("overflow_flag")
        s_scat = sem("rows_scattered")
        s_xe = [sem(f"expert_rows_loaded{i}") for i in range(2)]
        s_xt = sem("expert_rows_transposed")
        s_xh = sem("expert_rows_hi")
        s_xl = sem("expert_rows_lo")
        s_si = sem("silu")
        s_hm = sem("hidden")
        s_ht = sem("hidden_transposed")
        s_hth = sem("hidden_hi")
        s_htl = sem("hidden_lo")
        s_y = sem("expert_outputs")
        s_yo = [sem(f"expert_outputs_stored{i}") for i in range(2)]
        s_o_x = sem("overflow_rows_loaded")
        s_o_raw = [sem(f"overflow_raw_loaded{i}") for i in range(RING)]
        s_o_free = sem("overflow_output_free")
        s_o_pe = sem("overflow_products")
        s_o_act = sem("overflow_scalar")
        s_o_dve = sem("overflow_vector")
        s_o_st = sem("overflow_stored")
        s_yg = [sem(f"outputs_gathered{i}") for i in range(NYG)]
        s_yu = sem("outputs_added")
        s_eo = sem("result_tile")
        s_out = [sem(f"result_stored{i}") for i in range(4)]

        block = ctx.enter_context(nc.Block())


        def load_unit(sp, u, src):
            if u.c >= RING:
                sp.wait_ge(s_lo, u.count(RING))
            sp.dma_start(raw[:, u.slot], src).then_inc(s_raw[u.slot], 16)

        def split_hi(act, u):
            act.wait_ge(s_raw[u.slot], u.turn16())
            if u.c >= RING:
                act.wait_ge(s_mm, u.mm(RING))
            nc.scalar.activation(whi[:, u.slot], raw[:, u.slot], ACT.Copy).then_inc(s_hi, 1)

        def split_lo(dve, u):
            dve.wait_ge(s_hi, u.count())
            nc.vector.tensor_tensor(out=wlo[:, u.slot], in0=raw[:, u.slot], in1=whi[:, u.slot].bitcast(F32),
                                    op=ALU.subtract).then_inc(s_lo, 1)

        def three(pe, out, a_hi, a_lo, b_hi, b_lo, first, last):
            pe.matmul(out, a_hi, b_hi, start=first, stop=False, skip_group_check=True)
            pe.matmul(out, a_lo, b_hi, start=False, stop=False, skip_group_check=True)
            return pe.matmul(out, a_hi, b_lo, start=False, stop=last, skip_group_check=True)

        def ring_bank(g):
            return bank[5 + g % 3]

        def rows(w, k0, col):
            return w[k0 * P:(k0 + 2) * P, col:col + W].rearrange("(k p) c -> p k c", p=P)

        def flat(name):
            return I[name].rearrange("o k n -> (o k) n")

        @block.sync
        def _(sp):
            sp.dma_start(lnb[:, :], I["ln_mix"].to_broadcast([P, D])).then_inc(s_ln, 16)
            xp = I["x_prompt"].rearrange("o (t p) d -> p (o t) d", p=P)
            xs = I["x_sample"].rearrange("b s d -> (b s) d")
            w_in = flat("w_in")
            for t in range(NT):
                sp.dma_start(x[:, t], xp[:, t] if t < NT - 1 else xs).then_inc(s_x[t], 16)
                if t < RING:
                    load_unit(sp, Unit(t), rows(w_in, 2 * t, 0))
            sp.dma_start(st[:, :], I["state_conv"].rearrange("o b j c -> (o b j) c")).then_inc(s_state, 16)
            for c in range(1, 6):
                for i in range(4):
                    load_unit(sp, Unit(4 * c + i), rows(w_in, 2 * i, W * W_IN_COLS[c]))
            for i in range(4):
                load_unit(sp, Unit(U_C + i), rows(w_in, 2 * i, 6 * W))

            ck = I["cache_k"].rearrange("o b (kb p) h d -> p (o b) kb (h d)", p=P)
            cv = I["cache_v"].rearrange("o b (kb p) h d -> p (o b) kb (h d)", p=P)
            vnew = O[6].rearrange("o b s h d -> (o b) s (h d)")

            def cache(b, par, reuse):
                if reuse > 0:
                    sp.wait_ge(s_kt, 4 * b)
                sp.dma_start(kc[:, :, :], ck[:, bass.ds(b, 1)].rearrange("p o kb c -> p (o kb) c")).then_inc(s_kc, 16)
                if reuse > 1:
                    sp.wait_ge(s_avs, b - 1)
                sp.dma_start(vc[:, par], cv[:, bass.ds(b, 1)].rearrange("p o kb c -> p (o kb) c")).then_inc(s_vcl[par], 16)
                sp.dma_start(vn[:, par], vnew[bass.ds(b, 1)].rearrange("o s c -> s (o c)")).then_inc(s_vcl[par], 16)

            sp.wait_ge(s_vout, 16 * NT)
            sp.wait_ge(s_hn, NT)
            sp.wait_ge(s_av, H)
            cache(0, 0, 0)
            cache(1, 1, 1)
            with sp.Fori(1, 4) as i:
                cache(2 * i, 0, 2)
                cache(2 * i + 1, 1, 2)

            part_w = {"wab": flat("w_attn_branch"), "wcb": flat("w_conv_branch")}
            u = U_C + 4
            for n in range(2):
                for part in ("ga", "wab", "gb", "wcb"):
                    if (n, part) == (0, "ga"):
                        continue
                    for i in range(4 if part[0] == "g" else 2):
                        load_unit(sp, Unit(u), rows(w_in, 2 * i, (6 + n + 2 * (part == "gb")) * W) if part[0] == "g"
                                  else rows(part_w[part], 2 * i, n * W))
                        u += 1
                if n == 0:
                    sp.wait_ge(s_al, HP + 1)
                    for t in range(NT):
                        sp.dma_start(x[:, t], xp[:, t] if t < NT - 1 else xs).then_inc(s_xr, 16)
                    sp.dma_start(lnb[:, :], I["ln_ffn"].to_broadcast([P, D])).then_inc(s_ln, 16)
            for n in range(2):
                for i in range(4):
                    if (n, i) == (0, 3):
                        sp.wait_ge(s_mm, 5 * U_D)
                        sp.dma_start(praw[:, 0:NT - 1], I["p_prompt"].rearrange("o b (t p) c -> p (o b t) c", p=P)
                                     ).then_inc(s_ple, 16)
                        sp.dma_start(praw[:, NT - 1], I["p_sample"].rearrange("o b s c -> (o b s) c")).then_inc(s_ple, 16)
                    load_unit(sp, Unit(u), rows(flat("w_out"), 2 * i, n * W))
                    u += 1
            for n in range(2):
                load_unit(sp, Unit(u), rows(flat("w_ple_proj"), 0, n * W))
                u += 1
            assert u == U_M

            gup = [I[n].rearrange("o e (k p) f -> p (o e) k f", p=P) for n in ("w_exp_gate", "w_exp_up")]
            dwn = I["w_exp_down"].rearrange("o e (k p) f -> p (o e) k f", p=P)

            def gate_up_src(e, j):
                return gup[j // 4][:, bass.ds(e, 1), 2 * (j % 4):2 * (j % 4) + 2].rearrange("p o k f -> p (o k) f")

            def down_src(e, j):
                return dwn[:, bass.ds(e, 1), 2 * (j % 2):2 * (j % 2) + 2,
                           (j // 2) * W:(j // 2 + 1) * W].rearrange("p o k f -> p (o k) f")

            for j in range(4):
                load_unit(sp, Unit(U_M + j), gate_up_src(0, j))
            sp.wait_ge(s_scat, 16 * 2 * NT)
            for e in range(2):
                sp.dma_start(xe[:, e], Xd[e * C:(e + 1) * C, :]).then_inc(s_xe[e], 16)
            for j in range(4, 8):
                load_unit(sp, Unit(U_M + j), gate_up_src(0, j))

            def expert_loads(e, par, rows_next=True):
                for j in range(4):
                    load_unit(sp, Unit(U_M - 4 + j, NSTREAM, e), gate_up_src(e, j))
                if rows_next:
                    sp.wait_ge(s_xt, 2 * e)
                    sp.dma_start(xe[:, 1 - par], Xd[bass.ds((e + 1) * C, C), :]).then_inc(s_xe[1 - par], 16)
                for j in range(4, 8):
                    load_unit(sp, Unit(U_M - 4 + j, NSTREAM, e), gate_up_src(e, j))
                for j in range(4):
                    load_unit(sp, Unit(U_M + 4 + j, NSTREAM, e), down_src(e - 1, j))

            with sp.Fori(0, NE // 2 - 1) as i:
                expert_loads(2 * i + 1, 1)
                expert_loads(2 * i + 2, 0)
            expert_loads(NE - 1, 1, rows_next=False)
            for j in range(4):
                load_unit(sp, Unit(U_G - 4 + j), down_src(NE - 1, j))

            sp.wait_ge(s_flag, 1)
            over = sp.value_load(flag[0:1, 0:1], min_val=0, max_val=1)
            with sp.If(over > 0):
                with sp.Fori(0, NE) as e:
                    with sp.Fori(0, OV_TILES) as o:
                        n = e * OV_TILES + o
                        sp.wait_ge(s_o_act, 3 * n + 3)
                        sp.dma_start(xe[:, 0], Xd[bass.ds(NE * C + n * P, P), :]).then_inc(s_o_x, 16)
                        for j in range(12):
                            if j >= RING:
                                sp.wait_ge(s_o_pe, 14 * n + j - 2)
                            sp.dma_start(raw[:, j % RING], gate_up_src(e, j) if j < 8 else down_src(e, j - 8)
                                         ).then_inc(s_o_raw[j % RING], 16)
            sp.dma_start(lnb[:, :], I["ln_ple"].to_broadcast([P, D])).then_inc(s_ln, 16)
            for i in range(8):
                load_unit(sp, Unit(U_G + i), rows(flat("w_ple_gate"), 2 * (i % 4), (i // 4) * W))
            for i in range(2 * NT):
                n, t = i // NT, i % NT
                dst = (O[0].rearrange("o (t p) d -> p (o t) d", p=P)[:, t] if t < NT - 1
                       else O[1].rearrange("b s d -> (b s) d"))
                sp.wait_ge(s_eo, i + 1)
                sp.dma_start(dst[:, n * W:(n + 1) * W], eo[:, i % 4]).then_inc(s_out[i % 4], 16)
            for i in range(4):
                sp.wait_ge(s_out[i], 16 * len(range(i, 2 * NT, 4)))
            sp.wait_ge(s_ko[0], 16 * 2)
            sp.wait_ge(s_ko[1], 16 * 3)
            sp.wait_ge(s_vout, 16 * NT)
            sp.wait_ge(s_ncvo, 32)

        @block.gpsimd
        def _(pool):
            pl_ = nc.gpsimd
            for tile, value in ((ident, 0.0), (um, -1.0), (neg, -1.0), (before, 1.0), (onesb, 1.0), (ones1, 1.0),
                                (mhalf, -0.5), (zero, 0.0)):
                pl_.memset(tile[:], value).then_inc(s_made, 1)
            pl_.memset(qbd[:], 0.0).then_inc(s_made, 1)
            pl_.iota(desc[:], pattern=[[-1, 4]], base=4, channel_multiplier=0,
                     allow_small_or_imprecise_dtypes=True).then_inc(s_made, 1)
            pl_.iota(eidx[:], pattern=[[1, NE]], base=0, channel_multiplier=0,
                     allow_small_or_imprecise_dtypes=True).then_inc(s_made, 1)
            pool.wait_ge(s_made, 11)
            pl_.affine_select(out=ident[:], in_=ident[:], compare_op=ALU.not_equal, fill=1.0, base=0,
                              pattern=[[-1, P]], channel_multiplier=1).then_inc(s_made, 1)
            pl_.affine_select(out=um[:], in_=um[:], compare_op=ALU.is_ge, fill=0.0, base=0,
                              pattern=[[-1, P]], channel_multiplier=1).then_inc(s_made, 1)
            pl_.affine_select(out=before[:], in_=before[:], compare_op=ALU.is_gt, fill=0.0, base=0,
                              pattern=[[1, P]], channel_multiplier=-1).then_inc(s_made, 1)
            with nc.allow_non_contiguous_dma(reason="small weights"):
                pool.dma_start(qkg[:, 0], I["q_norm"].to_broadcast([P, HD])).then_inc(s_const, 16)
                pool.dma_start(qkg[:, 1], I["k_norm"].to_broadcast([P, HD])).then_inc(s_const, 16)

            step = [0]

            def link(ins):
                step[0] += 1
                ins.then_inc(s_pc, 1)
                pool.wait_ge(s_pc, step[0])

            def row_rms(i):
                pool.wait_ge(s_sq, i + 1)
                link(pl_.tensor_scalar(rms[:, i:i + 1], ss[:, i:i + 1], 1.0 / D, EPS, ALU.mult, ALU.add))
                pl_.tensor_tensor(rr[:, i:i + 1], rms[:, i:i + 1], mhalf[:, 0:1], ALU.pow).then_inc(s_r, 1)

            for t in range(NT):
                row_rms(t)
            pool.wait_ge(s_const, 32)
            link(pl_.tensor_scalar(qkg[:, 0], qkg[:, 0], HD ** -0.5, 1.0, ALU.mult, ALU.mult))
            with nc.allow_non_contiguous_dma(reason="small weights"):
                for j in range(3):
                    pool.dma_start(convw[:, j], I["conv_w"][0, j].rearrange("(c p) -> p c", p=P)).then_inc(s_const, 16)
                pool.dma_start(rbias[:, 0:NG], I["b_router_group"].to_broadcast([P, NG])).then_inc(s_const, 16)
                pool.dma_start(rbias[:, NG:], I["b_router_expert"].to_broadcast([P, NE])).then_inc(s_const, 16)
                pool.dma_start(wr[:, :, 0:NG], flat("w_router_group").rearrange("(k p) n -> p k n", p=P)
                               ).then_inc(s_const, 16)
                pool.dma_start(wr[:, :, NG:], flat("w_router_expert").rearrange("(k p) n -> p k n", p=P)
                               ).then_inc(s_const, 16)
            pl_.memset(up[:, :, 0:2], 0.0).then_inc(s_made, 1)

            kp = O[2].rearrange("o b (t p) h d -> p (o b t) (h d)", p=P)
            ks = O[5].rearrange("o b s h d -> (o b s) (h d)")
            vp = O[3].rearrange("o b (t p) h d -> p (o b t) (h d)", p=P)
            vs = O[6].rearrange("o b s h d -> (o b s) (h d)")

            def store_k(n):
                t = n - NT
                pool.wait_ge(s_qn2, n + 1)
                pool.dma_start(kp[:, t] if t < NT - 1 else ks, qn2[:, n % 2]).then_inc(s_ko[n % 2], 16)

            for n in range(2 * NT):
                pool.wait_ge(s_free, n + 1)
                if n:
                    pool.wait_ge(s_ssq, n)
                pl_.tensor_tensor(sqb[:, 0], zb[:, n % 2], zb[:, n % 2], ALU.mult).then_inc(s_qsq, 1)
                pool.wait_ge(s_ssq, n + 1)
                link(pl_.tensor_scalar(msq[:, n], ssq[:, n], 1.0 / HD, EPS, ALU.mult, ALU.add))
                pl_.tensor_tensor(rq[:, n], msq[:, n], mhalf[:, :], ALU.pow).then_inc(s_rq, 1)
                if n > NT:
                    store_k(n - 1)
            store_k(2 * NT - 1)
            for t in range(NT):
                pool.wait_ge(s_free, 2 * NT + t + 1)
                pool.dma_start(vp[:, t] if t < NT - 1 else vs, v[:, t]).then_inc(s_vout, 16)
            with pool.Fori(0, NE) as e:
                pool.dma_start(Xd[bass.ds(e * C, C), :].rearrange("r (a b) -> r a b", b=P),
                               zero[:, None, :].to_broadcast([P, D // P, P])).then_inc(s_zero, 16)
            pool.wait_ge(s_free, 5 * 5)
            pl_.tensor_copy(cpk[:, :, 0:2], up[:, :, TP:TP + 2]).then_inc(s_cpk, 1)
            for j in range(KW):
                pl_.tensor_copy(cpk[:, j, 2:].rearrange("p (b s) -> p b s", s=2), us[:, j, :, TS:TS + 2]).then_inc(s_cpk, 1)
            pool.wait_ge(s_trf, G_CONV + 1)
            pool.dma_start(O[4].rearrange("o b j c -> (o b j) c"), ncv[0:2]).then_inc(s_ncvo, 16)
            pool.dma_start(O[7].rearrange("o b j c -> (o b j) c"), ncv[2:]).then_inc(s_ncvo, 16)

            diag = (0, 512, 1024, 896)
            for h in range(H + 1):
                if h < H:
                    pool.wait_ge(s_spr, 3 * h + 3)
                    for i in range(4):
                        blk = sp1280[h % 2][:, diag[i]:diag[i] + P]
                        pl_.affine_select(out=blk, in_=blk, compare_op=ALU.is_gt, fill=0.0, base=0,
                                          pattern=[[1, P]], channel_multiplier=-1).then_inc(s_sp, 1)
                if h > 0:
                    pool.wait_ge(s_ea, 3 * h)
                    for i in range(4):
                        blk = a1280[(h - 1) % 2][:, diag[i]:diag[i] + P]
                        pl_.affine_select(out=blk, in_=blk, compare_op=ALU.is_gt, fill=0.0, base=0,
                                          pattern=[[1, P]], channel_multiplier=-1).then_inc(s_am, 1)

            def mask_softplus(b):
                pool.wait_ge(s_sps, 2 * b + 2)
                pl_.affine_select(out=spn[:], in_=spn[:], compare_op=ALU.is_gt, fill=0.0, base=0,
                                  pattern=[[0, H], [1, TS]], channel_multiplier=-1).then_inc(s_spn, 1)

            def mask_weights(b, par):
                pool.wait_ge(s_eas, 2 * b + 2)
                pl_.affine_select(out=an[:, par], in_=an[:, par], compare_op=ALU.is_gt, fill=0.0, base=0,
                                  pattern=[[0, H], [1, TS]], channel_multiplier=-1).then_inc(s_ams, 1)

            mask_softplus(0)
            mask_softplus(1)
            mask_weights(0, 0)
            for b in range(2, B):
                mask_softplus(b)
                mask_weights(b - 1, 1 - b % 2)
            mask_weights(7, 1)

            for t in range(NT):
                row_rms(NT + t)

            pool.wait_ge(s_flag, 1)
            over = pool.value_load(flag[0:1, 0:1], min_val=0, max_val=1)
            pool.wait_ge(s_zero, 16 * NE)
            with pool.If(over > 0):
                with pool.Fori(0, NE * OV_TILES) as o:
                    pool.dma_start(Xd[bass.ds(NE * C + o * P, P), :].rearrange("r (a b) -> r a b", b=P),
                                   zero[:, None, :].to_broadcast([P, D // P, P])).then_inc(s_zero, 16)
                pool.wait_ge(s_zero, 16 * (NE + NE * OV_TILES))
            pool.wait_ge(s_slot, 1)
            for t in range(NT):
                for k in range(2):
                    pool.indirect_dma_start(out=Xd[:, :], out_offset=bass.IndirectOffsetOnAxis(
                        ap=slot[:, k, t:t + 1], axis=0), in_=h2[:, t, :], in_offset=None).then_inc(s_scat, 16)

            def store_y(e, par):
                pool.wait_ge(s_y, 2 * e + 2)
                pool.dma_start(Yd[bass.ds(e * C, C), :], y[:, par]).then_inc(s_yo[par], 16)

            with pool.Fori(0, NE // 2) as i:
                store_y(2 * i, 0)
                store_y(2 * i + 1, 1)
            with pool.If(over > 0):
                pl_.tensor_tensor(free_[0:1], ones1[0:1], ones1[0:1], ALU.add).then_inc(s_o_free, 1)
                with pool.Fori(0, NE * OV_TILES) as o:
                    pool.wait_ge(s_o_act, 3 * o + 6)
                    pool.dma_start(Yd[bass.ds(NE * C + o * P, P), :], y[:, 0]).then_inc(s_o_st, 16)
                    pool.wait_ge(s_o_st, 16 * o + 16)
                    pl_.tensor_tensor(free_[0:1], ones1[0:1], ones1[0:1], ALU.add).then_inc(s_o_free, 1)
            pool.wait_ge(s_yo[0], 16 * NE // 2)
            pool.wait_ge(s_yo[1], 16 * NE // 2)

            def gather(i, n_rows):
                if i >= 2 * NT:
                    return
                if i >= NYG:
                    pool.wait_ge(s_yu, i - NYG + 1)
                pool.indirect_dma_start(out=yg[:, i % NYG, :], out_offset=None, in_=Yd[0:n_rows, :],
                                        in_offset=bass.IndirectOffsetOnAxis(ap=slot[:, i % 2, i // 2:i // 2 + 1], axis=0)
                                        ).then_inc(s_yg[i % NYG], 16)

            def gather_all(n_rows):
                for i in range(NYG):
                    gather(i, n_rows)
                for t in range(NT):
                    gather(NYG + 2 * t, n_rows)
                    gather(NYG + 2 * t + 1, n_rows)
                    row_rms(2 * NT + t)

            at_step = step[0]
            with pool.If(over > 0):
                gather_all(NE * C + NE * OV_TILES * P)
            step[0] = at_step
            with pool.Else():
                gather_all(NE * C)

        @block.scalar
        def _(act):
            sc = nc.scalar
            hi = lambda u: split_hi(act, Unit(u))

            def square(i, out, wait_sem, value):
                act.wait_ge(wait_sem, value)
                if i % NT:
                    act.wait_ge(s_sq, i)
                sc.activation(out[:, :], x[:, i % NT], ACT.Square, accum_out=ss[:, i:i + 1]).then_inc(s_sq, 1)

            for t in range(NT):
                square(t, junk, s_x[t], 16)
                if t < RING:
                    hi(t)

            def norm_hi(g, t, half):
                act.wait_ge(s_tr, g + 1)
                sc.activation(hh[:, 4 * half:4 * half + 4, t * P:(t + 1) * P],
                              ring_bank(g)[:, :].rearrange("p (k t) -> p k t", k=4), ACT.Copy).then_inc(s_trh, 1)

            for t in range(NT):
                for half in range(2):
                    norm_hi(G_X + 2 * t + half, t, half)

            for c in range(3):
                for i in range(4, 7):
                    hi(4 * c + i)
                for t in range(NT):
                    n = c * NT + t
                    act.wait_ge(s_mm, 5 * (4 * c + 3) + t + 1)
                    if c < 2:
                        if n >= 2:
                            act.wait_ge(s_qn1, n - 1)
                        sc.activation(zb[:, n % 2], bank[t][:, :], ACT.Copy).then_inc(s_free, 1)
                    else:
                        act.wait_ge(s_trf, G_STATE + 1)
                        sc.activation(v[:, t], bank[t][:, :], ACT.Copy).then_inc(s_free, 1)
                hi(4 * c + 7)
            for i in range(4, 7):
                hi(12 + i)
            for j in range(NT):
                act.wait_ge(s_mm, 5 * 16 if j >= 3 else 5 * 15 + j + 1)
                act.wait_ge(s_hn, NT)
                if j < KW:
                    sc.activation(ccT[:, j, 0:TP], bank[j][:, :], ACT.Copy).then_inc(s_free, 1)
                else:
                    sc.activation(ccT[:, :, TP:T], bank[4][:, :].rearrange("p (j t) -> p j t", j=KW), ACT.Copy
                                  ).then_inc(s_free, 1)
            hi(19)
            for u in range(20, 28):
                hi(u)
            for j in range(NT):
                act.wait_ge(s_free, 5 * CH_C - NT + j + 1)
                cols = (slice(j, j + 1), slice(0, TP)) if j < KW else (slice(0, KW), slice(TP, T))
                sc.activation(ch[:, cols[0], cols[1]], ccT[:, cols[0], cols[1]], ACT.Copy).then_inc(s_ch, 1)

            act.wait_ge(s_cl, NT)
            act.wait_ge(s_cpk, 1 + KW)
            act.wait_ge(s_ncvo, 32)
            for h in range(H + 1):
                if h < H:
                    tmp, zb3 = tmp1280[h % 2], bank[3 * (h % 2):3 * (h % 2) + 3]
                    act.wait_ge(s_z, h + 1)
                    if h >= 2:
                        act.wait_ge(s_spr, 3 * (h - 1))
                    for i, width in enumerate((512, 512, 256)):
                        sc.activation(tmp[:, 512 * i:512 * i + width], zb3[i][:, 0:width], ACT.Abs).then_inc(s_ln1, 1)
                    act.wait_ge(s_ln1, 5 * h + 3)
                    sc.activation(tmp[:, :], tmp[:, :], ACT.Exp, scale=-1.0).then_inc(s_ln1, 1)
                    act.wait_ge(s_ln1, 5 * h + 4)
                    sc.activation(tmp[:, :], tmp[:, :], ACT.Ln, bias=1.0).then_inc(s_ln1, 1)
                if h > 0:
                    a, zb3 = a1280[(h - 1) % 2], bank[3 * ((h - 1) % 2):3 * ((h - 1) % 2) + 3]
                    act.wait_ge(s_acc, h)
                    if h >= 3:
                        act.wait_ge(s_av, h - 2)
                    for i, width in enumerate((512, 512, 256)):
                        sc.activation(a[:, 512 * i:512 * i + width], zb3[i][:, 0:width], ACT.Exp).then_inc(s_ea, 1)
                if h in (3, 5, 7):
                    pair = (h - 3) // 2
                    act.wait_ge(s_av, 2 * pair + 2)
                    sc.activation(ah[:, pair, 0:TP], bank[6 + pair % 2][:, :], ACT.Copy).then_inc(s_ah, 1)
            act.wait_ge(s_av, H)
            sc.activation(ah[:, HP - 1, 0:TP], bank[6 + (HP - 1) % 2][:, :], ACT.Copy).then_inc(s_ah, 1)

            def keys_out(b):
                for kb in range(2):
                    act.wait_ge(s_kt, 4 * b + kb + 1)
                    act.wait_ge(s_zs, b)
                    sc.activation(ktc[:, kb], bank[kb][:, :].rearrange("p (h t) -> p h t", h=HP), ACT.Copy).then_inc(s_kta, 1)

            def logs(b, par):
                zs, zn = bank[4 + par][:, :], bank[6 + par][0:TS, 0:P]
                act.wait_ge(s_zs, b + 1)
                act.wait_ge(s_sps, 2 * b)
                sc.activation(tms[:], zs, ACT.Abs).then_inc(s_lns, 1)
                sc.activation(tmpn[:], zn, ACT.Abs).then_inc(s_lns, 1)
                act.wait_ge(s_lns, 6 * b + 2)
                sc.activation(tms[:], tms[:], ACT.Exp, scale=-1.0).then_inc(s_lns, 1)
                sc.activation(tmpn[:], tmpn[:], ACT.Exp, scale=-1.0).then_inc(s_lns, 1)
                act.wait_ge(s_lns, 6 * b + 4)
                sc.activation(tms[:], tms[:], ACT.Ln, bias=1.0).then_inc(s_lns, 1)
                sc.activation(tmpn[:], tmpn[:], ACT.Ln, bias=1.0).then_inc(s_lns, 1)

            def weights(b, par):
                act.wait_ge(s_accs, b + 1)
                act.wait_ge(s_avs, b)
                sc.activation(a_s[par][:], bank[4 + par][:, :], ACT.Exp).then_inc(s_eas, 1)
                sc.activation(an[:, par], bank[6 + par][0:TS, 0:P], ACT.Exp).then_inc(s_eas, 1)

            keys_out(0)
            logs(0, 0)
            keys_out(1)
            logs(1, 1)
            weights(0, 0)
            with act.Fori(1, 4) as i:
                keys_out(2 * i)
                logs(2 * i, 0)
                weights(2 * i - 1, 1)
                keys_out(2 * i + 1)
                logs(2 * i + 1, 1)
                weights(2 * i, 0)
            weights(7, 1)
            act.wait_ge(s_af, 2 * B)
            sc.activation(ah[:, :, TP:T], af[:, :, :], ACT.Copy).then_inc(s_ah, 1)

            for n in range(2):
                for q, nu in enumerate((4, 2, 4, 2)):
                    u0 = U_C + 12 * n + (0, 4, 6, 10)[q]
                    d = CH_C + 4 * n + q
                    for i in range(4, nu + 3):
                        hi(u0 + i)
                    if q % 2 == 0:
                        act.wait_ge(s_free, 5 * d)
                        for j in range(NT):
                            act.wait_ge(s_mm, 5 * (u0 + nu) if j >= 3 else 5 * (u0 + nu - 1) + j + 1)
                            if j < KW:
                                sc.activation(sg[:, j, 0:TP], bank[j][:, :], ACT.Sigmoid).then_inc(s_free, 1)
                            else:
                                sc.activation(sg[:, :, TP:T], bank[4][:, :].rearrange("p (j t) -> p j t", j=KW),
                                              ACT.Sigmoid).then_inc(s_free, 1)
                    hi(u0 + nu + 3)
                    if (n, q) == (1, 2):
                        for k in range(KW):
                            act.wait_ge(s_mm, 5 * (U_C + 22))
                            sc.activation(hh[:, k], m[:, k], ACT.Copy).then_inc(s_mh, 1)
            for k in range(KW, KD):
                act.wait_ge(s_m, k + 1)
                sc.activation(hh[:, k], m[:, k], ACT.Copy).then_inc(s_mh, 1)
            for n in range(2):
                u0 = U_D + 4 * n
                for i in range(4, 8):
                    hi(u0 + i)
                if n == 0:
                    for t in range(NT):
                        act.wait_ge(s_tr, G_PLE + t + 1)
                        sc.activation(ph[:, :, t * P:(t + 1) * P], ring_bank(G_PLE + t)[:, 0:2 * P].rearrange(
                            "p (k t) -> p k t", k=2), ACT.Copy).then_inc(s_trh, 1)
            for t in range(NT):
                square(NT + t, junk2, s_free, 5 * (CH_D + 1) + t + 1)
            for n in range(2):
                for t in range(NT):
                    act.wait_ge(s_mm, 5 * (U_P + n) + t + 1)
                    sc.activation(pp[:, t, n * W:(n + 1) * W], bank[t][:, :], ACT.Copy).then_inc(s_free, 1)
                hi(U_P + n + 4)
                if n == 0:
                    act.wait_ge(s_d, 1)
                    sc.activation(gexp[:], gdiff[:], ACT.Exp).then_inc(s_rx, 1)
                    act.wait_ge(s_d, 2)
                    sc.activation(vexp[:], vdiff[:], ACT.Exp).then_inc(s_rx, 1)

            def rows_hi(e):
                for half in range(2):
                    act.wait_ge(s_xt, 2 * e + half + 1)
                    sc.activation(xh[:, 4 * half:4 * half + 4], bank[4 + half][:, :].rearrange("p (k t) -> p k t", k=4),
                                  ACT.Copy).then_inc(s_xh, 1)

            def silu(e, last_gate_unit):
                act.wait_ge(s_mm, last_gate_unit.mm())
                act.wait_ge(s_hm, e)
                sc.activation(si[:, :], bank[0][:, :], ACT.Silu).then_inc(s_si, 1)

            def hidden_hi(e):
                act.wait_ge(s_ht, e + 1)
                sc.activation(mh[:, :, :], bank[6][:, :].rearrange("p (k t) -> p k t", k=4), ACT.Copy).then_inc(s_hth, 1)

            def out_rows(n, e, par, turn, unit):
                act.wait_ge(s_mm, unit.mm())
                act.wait_ge(s_yo[par], 16 * turn)
                sc.activation(y[:, par, n * W:(n + 1) * W], bank[2 + n][:, :], ACT.Copy).then_inc(s_y, 1)

            rows_hi(0)
            for j in range(4, 8):
                hi(U_M + j)
            silu(0, Unit(U_M + 3))
            for j in range(8, 12):
                hi(U_M + j)
            rows_hi(1)

            def expert_scalar(e, par, turn, rows_next=True):
                u = lambda j: Unit(U_M - 4 + j, NSTREAM, e)
                for j in range(4, 8):
                    split_hi(act, u(j))
                hidden_hi(e - 1)
                silu(e, u(3))
                for j in range(8, 12):
                    split_hi(act, u(j))
                if rows_next:
                    rows_hi(e + 1)
                split_hi(act, u(12))
                split_hi(act, u(13))
                out_rows(0, e - 1, 1 - par, turn, u(9))
                split_hi(act, u(14))
                split_hi(act, u(15))
                out_rows(1, e - 1, 1 - par, turn, u(11))

            expert_scalar(1, 1, 0)
            expert_scalar(2, 0, 0)
            with act.Fori(1, NE // 2 - 1) as i:
                expert_scalar(2 * i + 1, 1, i)
                expert_scalar(2 * i + 2, 0, i)
            expert_scalar(NE - 1, 1, NE // 2 - 1, rows_next=False)
            hidden_hi(NE - 1)
            out_rows(0, NE - 1, 1, NE // 2 - 1, Unit(U_G - 3))
            out_rows(1, NE - 1, 1, NE // 2 - 1, Unit(U_G - 1))

            act.wait_ge(s_flag, 1)
            over = act.value_load(flag[0:1, 0:1], min_val=0, max_val=1)
            with act.If(over > 0):
                act.wait_ge(s_yo[0], 16 * NE // 2)
                act.wait_ge(s_hm, NE)
                sc.activation(si[:, 0:1], ss[:, 0:1], ACT.Copy).then_inc(s_o_act, 3)
                act.wait_ge(s_o_act, 3)
                with act.Fori(0, NE * OV_TILES) as o:
                    act.wait_ge(s_o_pe, 14 * o + 5)
                    sc.activation(si[:, :], bank[0][:, :], ACT.Silu).then_inc(s_o_act, 1)
                    act.wait_ge(s_o_free, o + 1)
                    for n in range(2):
                        act.wait_ge(s_o_pe, 14 * o + 12 + 2 * n)
                        sc.activation(y[:, 0, n * W:(n + 1) * W], bank[2 + n][:, :], ACT.Copy).then_inc(s_o_act, 1)

            for i in range(4):
                hi(U_G + i)
            for t in range(NT):
                square(2 * NT + t, junk2, s_yu, 2 * t + 2)
                for half in range(2):
                    norm_hi(G_F + 2 * t + half, t, half)
            for n in range(2):
                if n == 0:
                    for i in range(4, 7):
                        hi(U_G + i)
                for t in range(NT):
                    i = n * NT + t
                    act.wait_ge(s_mm, 5 * (U_G + 4 * n + 3) + t + 1)
                    if i >= 4:
                        act.wait_ge(s_out[i % 4], 16 * (i // 4))
                    sc.activation(eo[:, i % 4], bank[t][:, :], ACT.Sigmoid).then_inc(s_free, 1)
                if n == 0:
                    hi(U_G + 7)

        @block.vector
        def _(dve):
            ve = nc.vector
            lo = lambda u: split_lo(dve, Unit(u))
            step = [0]

            def link(ins):
                step[0] += 1
                ins.then_inc(s_vc, 1)
                dve.wait_ge(s_vc, step[0])

            def tt(out, a, b, op):
                return ve.tensor_tensor(out=out, in0=a, in1=b, op=op)

            def norm_rows(i, out):
                dve.wait_ge(s_r, i + 1)
                return ve.scalar_tensor_tensor(out=out, in0=x[:, i % NT], scalar=rr[:, i:i + 1], in1=lnb[:, :],
                                               op0=ALU.mult, op1=ALU.mult)

            def norm_lo(g, t, half):
                dve.wait_ge(s_trh, trh(g))
                dst = (slice(4 * half, 4 * half + 4), slice(t * P, (t + 1) * P))
                tt(hl[:, dst[0], dst[1]], ring_bank(g)[:, :].rearrange("p (k t) -> p k t", k=4),
                   hh[:, dst[0], dst[1]].bitcast(F32), ALU.subtract).then_inc(s_trf, 1)

            def trh(g):
                return g + 1 if g < 10 else 10 + g - G_PLE + 1 if g < G_R else 15 + g - G_F + 1

            dve.wait_ge(s_ln, 16)
            for t in range(NT):
                if t >= 2:
                    dve.wait_ge(s_tr, 2 * (t - 2) + 2)
                norm_rows(t, hn[:, t % 2]).then_inc(s_hn, 1)
                if t < RING:
                    lo(t)
                if t >= 1:
                    norm_lo(2 * t - 2, t - 1, 0)
                    norm_lo(2 * t - 1, t - 1, 1)
            norm_lo(8, 4, 0)
            norm_lo(9, 4, 1)
            dve.wait_ge(s_sq, NT)
            dve.wait_ge(s_tr, G_STATE + 1)
            ve.tensor_copy(us[:, :, :, 0:2], ring_bank(G_STATE)[:, 0:KW * 2 * B].rearrange(
                "p (j b s) -> p j b s", j=KW, s=2)).then_inc(s_trf, 1)

            def head_sums(n):
                dve.wait_ge(s_qsq, n + 1)
                ve.tensor_reduce(out=ssq[:, n], in_=sqb[:, 0].rearrange("p (h d) -> p h d", h=H), axis=AX.X,
                                 op=ALU.add).then_inc(s_ssq, 1)
                dve.wait_ge(s_rq, n + 1)
                if n:
                    dve.wait_ge(s_qn2, n)
                tt(qn1[:, 0].rearrange("p (h d) -> p h d", h=H), zb[:, n % 2].rearrange("p (h d) -> p h d", h=H),
                   rq[:, n, :, None].to_broadcast([P, H, HD]), ALU.mult).then_inc(s_qn1, 1)

            def head_normed(n):
                if n >= 2:
                    dve.wait_ge(s_tr, G_QK + n - 1)
                if n >= NT + 2:
                    dve.wait_ge(s_ko[n % 2], 16 * ((n - NT) // 2))
                dve.wait_ge(s_qn1, n + 1)
                tt(qn2[:, n % 2].rearrange("p (h d) -> p h d", h=H), qn1[:, 0].rearrange("p (h d) -> p h d", h=H),
                   qkg[:, n // NT, None, :].to_broadcast([P, H, HD]), ALU.mult).then_inc(s_qn2, 1)

            def qk_out(n):
                g = G_QK + n
                dve.wait_ge(s_tr, g + 1)
                dst = (qT if n < NT else kT)[:, :, (n % NT) * P:(n % NT + 1) * P]
                ve.tensor_copy(dst, ring_bank(g)[:, :].rearrange("p (j t) -> p j t", j=KW)).then_inc(s_trf, 1)

            for c in range(3):
                for i in range(4, 7):
                    lo(4 * c + i)
                if c < 2:
                    n = c * NT
                    if c == 1:
                        qk_out(n - 2)
                        qk_out(n - 1)
                    head_sums(n)
                    head_normed(n)
                    head_sums(n + 1)
                    head_normed(n + 1)
                    head_sums(n + 2)
                    lo(4 * c + 7)
                    qk_out(n)
                    head_normed(n + 2)
                    head_sums(n + 3)
                    qk_out(n + 1)
                    head_normed(n + 3)
                    head_sums(n + 4)
                    qk_out(n + 2)
                    head_normed(n + 4)
                else:
                    qk_out(8)
                    qk_out(9)
                    lo(4 * c + 7)

            for u in range(16, 23):
                lo(u)
            dve.wait_ge(s_free, 5 * 4)
            for j in range(NT):
                dve.wait_ge(s_mm, 5 * 20 if j >= 3 else 5 * 19 + j + 1)
                if j < KW:
                    tt(up[:, j, 2:2 + TP], bank[j][:, :], ccT[:, j, 0:TP], ALU.mult).then_inc(s_free, 1)
                else:
                    for jj in range(KW):
                        ins = tt(us[:, jj, :, 2:2 + TS], bank[4][:, jj * P:(jj + 1) * P].rearrange("p (b s) -> p b s", b=B),
                                 ccT[:, jj, TP:T].rearrange("p (b s) -> p b s", b=B), ALU.mult)
                    ins.then_inc(s_free, 1)
            lo(23)
            dve.wait_ge(s_free, 5 * 5)
            dve.wait_ge(s_made, 15)
            dve.wait_ge(s_const, 16 * 9)

            def conv(j):
                outs = (yc[:, j, 0:TP], yc[:, j, TP:T].rearrange("p (b s) -> p b s", b=B))
                ins_ = (lambda s: up[:, j, s:s + TP], lambda s: us[:, j, :, s:s + TS])
                for s in range(3):
                    for n in range(2):
                        if s == 0:
                            ins = ve.tensor_scalar(outs[n], ins_[n](0), convw[:, 0, j:j + 1], None, ALU.mult)
                        else:
                            ins = ve.scalar_tensor_tensor(out=outs[n], in0=ins_[n](s), scalar=convw[:, s, j:j + 1],
                                                          in1=outs[n], op0=ALU.mult, op1=ALU.add)
                    link(ins)

            for j in range(KW):
                conv(j)
                if j < 3:
                    lo(24 + j)
            for j in range(NT):
                dve.wait_ge(s_mm, 5 * 24 if j >= 3 else 5 * 23 + j + 1)
                if j < KW:
                    tt(ccT[:, j, 0:TP], bank[j][:, :], yc[:, j, 0:TP], ALU.mult).then_inc(s_free, 1)
                else:
                    tt(ccT[:, :, TP:T], bank[4][:, :].rearrange("p (j t) -> p j t", j=KW), yc[:, :, TP:T],
                       ALU.mult).then_inc(s_free, 1)
            lo(27)
            for j in range(NT):
                dve.wait_ge(s_ch, j + 1)
                cols = (slice(j, j + 1), slice(0, TP)) if j < KW else (slice(0, KW), slice(TP, T))
                tt(cl[:, cols[0], cols[1]], ccT[:, cols[0], cols[1]], ch[:, cols[0], cols[1]].bitcast(F32),
                   ALU.subtract).then_inc(s_cl, 1)
            dve.wait_ge(s_tr, G_CONV + 1)
            ve.tensor_copy(ncv[:, :], ring_bank(G_CONV)[0:2 + 2 * B, :]).then_inc(s_trf, 1)

            dve.wait_ge(s_cl, NT)
            for h in range(H):
                tmp, out, zb3 = tmp1280[h % 2], sp1280[h % 2], bank[3 * (h % 2):3 * (h % 2) + 3]
                dve.wait_ge(s_ln1, 5 * h + 5)
                if h >= 2:
                    dve.wait_ge(s_acc, h - 1)
                for i, width in enumerate((512, 512, 256)):
                    ve.scalar_tensor_tensor(out=out[:, 512 * i:512 * i + width], in0=zb3[i][:, 0:width], scalar=0.0,
                                            in1=tmp[:, 512 * i:512 * i + width], op0=ALU.max, op1=ALU.add
                                            ).then_inc(s_spr, 1)
                if h in (3, 5, 7):
                    pair = (h - 3) // 2
                    dve.wait_ge(s_ah, pair + 1)
                    tt(al[:, pair, 0:TP], bank[6 + pair % 2][:, :], ah[:, pair, 0:TP].bitcast(F32), ALU.subtract
                       ).then_inc(s_al, 1)
            dve.wait_ge(s_ah, HP)
            tt(al[:, HP - 1, 0:TP], bank[6 + (HP - 1) % 2][:, :], ah[:, HP - 1, 0:TP].bitcast(F32), ALU.subtract
               ).then_inc(s_al, 1)

            def keys_out(b):
                for kb in (2, 3):
                    dve.wait_ge(s_kt, 4 * b + kb + 1)
                    dve.wait_ge(s_zs, b)
                    ve.tensor_copy(ktc[:, kb], bank[kb][:, :].rearrange("p (h t) -> p h t", h=HP)).then_inc(s_ktv, 1)

            def softplus(b, par):
                dve.wait_ge(s_lns, 6 * b + 6)
                dve.wait_ge(s_accs, b)
                for out, z, tmp in ((sps, bank[4 + par][:, :], tms), (spn, bank[6 + par][0:TS, 0:P], tmpn)):
                    ve.scalar_tensor_tensor(out=out[:], in0=z, scalar=0.0, in1=tmp[:], op0=ALU.max, op1=ALU.add
                                            ).then_inc(s_sps, 1)

            def keep(b, par):
                dve.wait_ge(s_avs, b + 1)
                o = bank[6 + par][:, P:2 * P].rearrange("p (h q) -> p h q", h=HP)
                ve.tensor_copy(af[0:HD, :, bass.ds(b * TS, TS)], o[0:HD, :, 0:TS]).then_inc(s_af, 1)
                ve.tensor_copy(af[HD:P, :, bass.ds(b * TS, TS)], o[HD:P, :, TS:]).then_inc(s_af, 1)

            def place(b, par, reuse):
                if reuse:
                    dve.wait_ge(s_zs, b - 1)
                q_b = qT[:, :, bass.ds(b * TS + TP, TS)]
                ve.tensor_copy(qbd[0:HD, par, :, 0:TS], q_b[0:HD]).then_inc(s_qb, 1)
                ve.tensor_copy(qbd[HD:P, par, :, TS:], q_b[HD:P]).then_inc(s_qb, 1)
                ve.tensor_copy(ktn[:, par], kT[:, :, bass.ds(b * TS + TP, TS)]).then_inc(s_qb, 1)

            place(0, 0, False)
            keys_out(0)
            softplus(0, 0)
            place(1, 1, False)
            keys_out(1)
            softplus(1, 1)
            keep(0, 0)
            with dve.Fori(1, 4) as i:
                place(2 * i, 0, True)
                keys_out(2 * i)
                softplus(2 * i, 0)
                keep(2 * i - 1, 1)
                place(2 * i + 1, 1, True)
                keys_out(2 * i + 1)
                softplus(2 * i + 1, 1)
                keep(2 * i, 0)
            keep(7, 1)
            dve.wait_ge(s_ah, HP + 1)
            tt(al[:, :, TP:T], af[:, :, :], ah[:, :, TP:T].bitcast(F32), ALU.subtract).then_inc(s_al, 1)

            def merged_lo(k):
                dve.wait_ge(s_mh, k + 1)
                tt(hl[:, k], m[:, k], hh[:, k].bitcast(F32), ALU.subtract).then_inc(s_ml, 1)

            for n in range(2):
                for q, nu in enumerate((4, 2, 4, 2)):
                    u0 = U_C + 12 * n + (0, 4, 6, 10)[q]
                    d = CH_C + 4 * n + q
                    for i in range(4, nu + 3):
                        lo(u0 + i)
                    if q % 2:
                        dve.wait_ge(s_free, 5 * d)
                        for j in range(NT):
                            dve.wait_ge(s_mm, 5 * (u0 + nu) if j >= 3 else 5 * (u0 + nu - 1) + j + 1)
                            dst, row = (m, 4 * n) if q == 1 else (mt, 0)
                            if j < KW:
                                tt(dst[:, row + j, 0:TP], bank[j][:, :], sg[:, j, 0:TP], ALU.mult).then_inc(s_free, 1)
                            else:
                                tt(dst[:, row:row + KW, TP:T], bank[4][:, :].rearrange("p (j t) -> p j t", j=KW),
                                   sg[:, :, TP:T], ALU.mult).then_inc(s_free, 1)
                    if q == 3:
                        dve.wait_ge(s_free, 5 * d + 5)
                        for j in range(KW):
                            tt(m[:, 4 * n + j], m[:, 4 * n + j], mt[:, j], ALU.add).then_inc(s_m, 1)
                        dve.wait_ge(s_m, 4 * n + 4)
                    lo(u0 + nu + 3)
                    if (n, q) == (1, 2):
                        for k in range(KW):
                            merged_lo(k)
            for k in range(KW, KD):
                merged_lo(k)

            for n in range(2):
                u0 = U_D + 4 * n
                for i in range(4, 7):
                    lo(u0 + i)
                dve.wait_ge(s_xr, 16 * NT)
                for t in range(NT):
                    dve.wait_ge(s_mm, 5 * (u0 + 3) + t + 1)
                    tt(x[:, t, n * W:(n + 1) * W], x[:, t, n * W:(n + 1) * W], bank[t][:, :], ALU.add).then_inc(s_free, 1)
                lo(u0 + 7)
                if n == 0:
                    for t in range(NT):
                        g = G_PLE + t
                        dve.wait_ge(s_trh, trh(g))
                        tt(pl[:, :, t * P:(t + 1) * P], ring_bank(g)[:, 0:2 * P].rearrange("p (k t) -> p k t", k=2),
                           ph[:, :, t * P:(t + 1) * P].bitcast(F32), ALU.subtract).then_inc(s_trf, 1)

            def h2_out(t):
                for half in range(2):
                    g = G_R + 2 * t + half
                    dve.wait_ge(s_tr, g + 1)
                    ve.tensor_copy(h2T[:, 4 * half:4 * half + 4, t * P:(t + 1) * P],
                                   ring_bank(g)[:, :].rearrange("p (k t) -> p k t", k=4)).then_inc(s_trf, 1)

            dve.wait_ge(s_ln, 32)
            for t in range(NT):
                norm_rows(NT + t, h2[:, t]).then_inc(s_hn, 1)
                if t:
                    h2_out(t - 1)
            h2_out(NT - 1)

            def bc(a, n):
                return a[:, :, None].to_broadcast([P, NT, n])

            def top(logits, vmax, choice):
                link(ve.tensor_reduce(out=vmax[:], in_=logits, axis=AX.X, op=ALU.max))
                link(tt(cand[:], logits, bc(vmax, 4), ALU.is_ge))
                link(tt(cand[:], cand[:], desc[:, None, :].to_broadcast([P, NT, 4]), ALU.mult))
                link(ve.tensor_reduce(out=cm1[:], in_=cand[:], axis=AX.X, op=ALU.max))
                link(tt(choice, cand[:], bc(cm1, 4), ALU.is_equal))

            dve.wait_ge(s_rt, 1)
            link(tt(lg[:], bank[6][:, 0:NT * (NG + NE)].rearrange("p (t n) -> p t n", t=NT),
                    rbias[:, None, :].to_broadcast([P, NT, NG + NE]), ALU.add))
            top(lg[:, :, 0:NG], gmax, og[:])
            tt(gdiff[:], lg[:, :, 0:NG], bc(gmax, NG), ALU.subtract).then_inc(s_d, 1)
            link(tt(prod[:], lg[:, :, NG:].rearrange("p t (g j) -> p t j g", g=NG),
                    og[:, :, None, :].to_broadcast([P, NT, EG, NG]), ALU.mult))
            link(ve.tensor_reduce(out=lsel[:], in_=prod[:], axis=AX.X, op=ALU.add))
            top(lsel[:], v1, ok[:, 0])
            link(ve.scalar_tensor_tensor(out=lsel2[:], in0=ok[:, 0], scalar=-3.0e38, in1=lsel[:], op0=ALU.mult,
                                         op1=ALU.add))
            top(lsel2[:], v2, ok[:, 1])
            tt(vdiff[:], v2[:], v1[:], ALU.subtract).then_inc(s_d, 1)
            for k in range(2):
                ins = tt(Mk[:, k].rearrange("p t (g j) -> p t g j", g=NG), og[:, :, :, None].to_broadcast([P, NT, NG, EG]),
                         ok[:, k, :, None, :].to_broadcast([P, NT, NG, EG]), ALU.mult)
            link(ins)
            tt(Mb[:], Mk[:, 0], Mk[:, 1], ALU.add).then_inc(s_M, 1)
            dve.wait_ge(s_rx, 2)
            ve.tensor_reduce(out=gsum[:], in_=gexp[:], axis=AX.X, op=ALU.add)
            link(ve.tensor_scalar(vsum[:], vexp[:], 1.0, None, ALU.add))
            link(tt(gsum[:], gsum[:], vsum[:], ALU.mult))
            link(ve.reciprocal(gate[:, 0], gsum[:]))
            link(tt(gate[:, 1], gate[:, 0], vexp[:], ALU.mult))
            dve.wait_ge(s_rk, 1)
            link(ve.tensor_copy(rk[:], bank[6][:, P:P + NT * NE].rearrange("p (t e) -> p t e", t=NT)))
            for k in range(2):
                ins = tt(mr[:, k], Mk[:, k], rk[:], ALU.mult)
            link(ins)
            link(ve.tensor_reduce(out=slotf[:, 0], in_=mr[:], axis=AX.X, op=ALU.add))
            link(tt(mr[:].rearrange("p k t e -> p (k t) e"), Mk[:].rearrange("p k t e -> p (k t) e"),
                    eidx[:, None, :].to_broadcast([P, 2 * NT, NE]), ALU.mult))
            link(ve.tensor_reduce(out=slotf[:, 1], in_=mr[:], axis=AX.X, op=ALU.add))
            link(ve.tensor_scalar(slotf[:, 2], slotf[:, 0], float(C), None, ALU.is_ge))
            ve.tensor_reduce(out=ovm[:], in_=slotf[:, 2], axis=AX.XY, op=ALU.max).then_inc(s_ovm, 1)
            link(ve.tensor_scalar(slotf[:, 3], slotf[:, 1], float(T - 2 * C), float((NE - 1) * C), ALU.mult, ALU.add))
            link(tt(slotf[:, 3], slotf[:, 3], slotf[:, 2], ALU.mult))
            link(ve.scalar_tensor_tensor(out=slotf[:, 0], in0=slotf[:, 1], scalar=float(C), in1=slotf[:, 0],
                                         op0=ALU.mult, op1=ALU.add))
            tt(slot[:], slotf[:, 0], slotf[:, 3], ALU.add).then_inc(s_slot, 1)
            dve.wait_ge(s_ov, 1)
            ve.tensor_scalar(flag[0:1, 0:1], bank[7][0:1, 0:1], 1.0, None, ALU.min).then_inc(s_flag, 1)
            lo(60)
            lo(61)

            def rows_lo(e):
                for half in range(2):
                    dve.wait_ge(s_xh, 2 * e + half + 1)
                    tt(xl[:, 4 * half:4 * half + 4], bank[4 + half][:, :].rearrange("p (k t) -> p k t", k=4),
                       xh[:, 4 * half:4 * half + 4].bitcast(F32), ALU.subtract).then_inc(s_xl, 1)

            def hidden(e, last_up_unit):
                dve.wait_ge(s_mm, last_up_unit.mm())
                dve.wait_ge(s_si, e + 1)
                dve.wait_ge(s_ht, e)
                tt(hm[:, :], bank[1][:, :], si[:, :], ALU.mult).then_inc(s_hm, 1)

            def hidden_lo(e):
                dve.wait_ge(s_hth, e + 1)
                tt(ml[:, :, :], bank[6][:, :].rearrange("p (k t) -> p k t", k=4), mh[:, :, :].bitcast(F32),
                   ALU.subtract).then_inc(s_htl, 1)

            rows_lo(0)
            for j in range(4, 11):
                lo(U_M + j)
            hidden(0, Unit(U_M + 7))
            lo(U_M + 11)
            rows_lo(1)

            def expert_vector(e, rows_next=True):
                u = lambda j: Unit(U_M - 4 + j, NSTREAM, e)
                for j in range(4, 8):
                    split_lo(dve, u(j))
                hidden_lo(e - 1)
                for j in range(8, 11):
                    split_lo(dve, u(j))
                hidden(e, u(7))
                split_lo(dve, u(11))
                if rows_next:
                    rows_lo(e + 1)
                last = 16 if rows_next else 16
                for j in range(12, last):
                    split_lo(dve, u(j))

            with dve.Fori(1, NE - 1) as e:
                expert_vector(e)
            expert_vector(NE - 1, rows_next=False)
            hidden_lo(NE - 1)

            dve.wait_ge(s_flag, 1)
            over = dve.value_load(flag[0:1, 0:1], min_val=0, max_val=1)
            with dve.If(over > 0):
                ve.memset(cm1[:], 0.0).then_inc(s_o_dve, 3)
                with dve.Fori(0, NE * OV_TILES) as o:
                    dve.wait_ge(s_o_pe, 14 * o + 1)
                    for half in range(2):
                        ins = ve.tensor_copy(oxT[:, 4 * half:4 * half + 4],
                                             bank[4 + half][:, :].rearrange("p (k t) -> p k t", k=4))
                    ins.then_inc(s_o_dve, 1)
                    dve.wait_ge(s_o_pe, 14 * o + 9)
                    dve.wait_ge(s_o_act, 3 * o + 4)
                    tt(hm[:, :], bank[1][:, :], si[:, :], ALU.mult).then_inc(s_o_dve, 1)
                    dve.wait_ge(s_o_pe, 14 * o + 10)
                    ve.tensor_copy(omT[:, :, :], bank[6][:, :].rearrange("p (k t) -> p k t", k=4)).then_inc(s_o_dve, 1)

            for i in range(4):
                lo(U_G + i)
            dve.wait_ge(s_ln, 48)
            for t in range(NT):
                for k in range(2):
                    i = 2 * t + k
                    dve.wait_ge(s_yg[i % NYG], 16 * (i // NYG + 1))
                    dve.wait_ge(s_yu, i)
                    ve.scalar_tensor_tensor(out=x[:, t], in0=yg[:, i % NYG], scalar=gate[:, k, t:t + 1], in1=x[:, t],
                                            op0=ALU.mult, op1=ALU.add).then_inc(s_yu, 1)
                if t >= 2:
                    dve.wait_ge(s_tr, G_F + 2 * (t - 2) + 2)
                norm_rows(2 * NT + t, hn3[:, t % 2]).then_inc(s_hn, 1)
                if t:
                    for half in range(2):
                        norm_lo(G_F + 2 * (t - 1) + half, t - 1, half)
            for half in range(2):
                norm_lo(G_F + 2 * (NT - 1) + half, NT - 1, half)
            for n in range(2):
                if n == 0:
                    for i in range(4, 7):
                        lo(U_G + i)
                for t in range(NT):
                    i = n * NT + t
                    cols = slice(n * W, (n + 1) * W)
                    dve.wait_ge(s_free, 5 * CH_G + i + 1)
                    link(tt(eo[:, i % 4], eo[:, i % 4], pp[:, t, cols], ALU.mult))
                    tt(eo[:, i % 4], eo[:, i % 4], x[:, t, cols], ALU.add).then_inc(s_eo, 1)
                if n == 0:
                    lo(U_G + 7)

        @block.tensor
        def _(pe):
            def tr(g, pairs):
                if g >= 3:
                    pe.wait_ge(s_trf, g - 2)
                for out, src, idn in pairs:
                    ins = pe.transpose(out, src, idn)
                ins.then_inc(s_tr, 1)

            def tr_rows(g, src, n=4):
                tr(g, [(ring_bank(g)[:, q * P:(q + 1) * P], src[:, q * P:(q + 1) * P], ident[:, :]) for q in range(n)])

            def natural(u0, nu, d, a_hi, a_lo, before_unit=None, before_tile=None, free=True):
                for i in range(nu):
                    u = Unit(u0 + i)
                    pe.wait_ge(s_lo, u.count())
                    if before_unit:
                        before_unit(i)
                    for t in range(NT):
                        if i == 0 and d > 0:
                            pe.wait_ge(s_free, 5 * (d - 1) + t + 1)
                        if before_tile:
                            before_tile(i, t)
                        for kk in range(2):
                            k = 2 * i + kk
                            a = (slice(0, P), k, slice(t * P, (t + 1) * P))
                            ins = three(pe, bank[t][:, :], a_hi[a], a_lo[a], whi[:, u.slot, kk], wlo[:, u.slot, kk],
                                        i == 0 and kk == 0, i == nu - 1 and kk == 1)
                        ins.then_inc(s_mm, 1)

            def transposed(u0, nu, d5, b_hi, b_lo):
                for i in range(nu):
                    u = u0.plus(i)
                    pe.wait_ge(s_lo, u.count())
                    if i == 0:
                        pe.wait_ge(s_free, d5)
                    for j in range(KW):
                        for kk in range(2):
                            k = 2 * i + kk
                            first = i == 0 and kk == 0
                            w_hi = whi[:, u.slot, kk, j * P:(j + 1) * P]
                            w_lo = wlo[:, u.slot, kk, j * P:(j + 1) * P]
                            outs = (bank[j][:, :], bank[4][:, j * P:(j + 1) * P])
                            rows_ = (slice(0, TP), slice(TP, T))
                            for w, r in ((w_hi, b_hi), (w_hi, b_lo), (w_lo, b_hi)):
                                for s in range(2):
                                    ins = pe.matmul(outs[s], w, r[:, k, rows_[s]],
                                                    start=first and w is w_hi and r is b_hi and (s == 0 or j == 0),
                                                    stop=i == nu - 1 and kk == 1 and w is w_lo, skip_group_check=True)
                        ins.then_inc(s_mm, 2 if j == KW - 1 else 1)

            def x_rows(t):
                pe.wait_ge(s_hn, t + 1)
                for half in range(2):
                    tr_rows(G_X + 2 * t + half, hn[:, t % 2, half * W:(half + 1) * W])

            pe.wait_ge(s_made, 14)
            x_rows(0)

            def q_tile(i, t):
                if i == 0:
                    if t + 1 < NT:
                        x_rows(t + 1)
                    pe.wait_ge(s_trf, 2 * t + 2)

            natural(0, 4, 0, hh, hl, before_tile=q_tile)
            pe.wait_ge(s_state, 16)
            tr(G_STATE, [(ring_bank(G_STATE)[:, j * 2 * B:(j + 1) * 2 * B], st[:, j * P:(j + 1) * P],
                          ident[0:2 * B, 0:2 * B]) for j in range(KW)])

            def qk_rows(first):
                def before(i, t):
                    if t == 0 and i >= 2:
                        for n in ((0, 1), (2, 3))[i - 2]:
                            pe.wait_ge(s_qn2, first + n + 1)
                            tr_rows(G_QK + first + n, qn2[:, (first + n) % 2])
                return before

            def qk_last(first):
                pe.wait_ge(s_qn2, first + NT)
                tr_rows(G_QK + first + NT - 1, qn2[:, (first + NT - 1) % 2])

            natural(4, 4, 1, hh, hl, before_tile=qk_rows(0))
            qk_last(0)
            natural(8, 4, 2, hh, hl, before_tile=qk_rows(NT))
            qk_last(NT)
            with pe.Fori(3, 6) as c:
                transposed(Unit(0, 4, c), 4, 5 * c, hh, hl)
            pe.wait_ge(s_cpk, 1 + KW)
            tr(G_CONV, [(ring_bank(G_CONV)[0:2 + 2 * B, j * P:(j + 1) * P], cpk[:, j], ident[:, :]) for j in range(KW)])

            region = {0: (0, 0), 1: (1, 0), 2: (2, 0), 3: (1, 384)}
            off = {0: 0, 1: 512, 2: 1024, 3: 896}
            width = [TP - i * P for i in range(4)]

            def zreg(h, i, skip=0):
                bk, o = region[i]
                return bank[3 * (h % 2) + bk][:, o + skip:o + width[i]]

            def scores(h):
                r = HD * (h % 2)
                if h >= 2:
                    pe.wait_ge(s_ea, 3 * (h - 1))
                for i in (0, 1, 3, 2):
                    ins = pe.matmul(zreg(h, i), kT[r:r + HD, h // 2, i * P:(i + 1) * P],
                                    qT[r:r + HD, h // 2, i * P:TP], start=i != 3, stop=False, skip_group_check=True)
                ins.then_inc(s_z, 1)

            def log_sums(h):
                t = sp1280[h % 2]
                pe.wait_ge(s_sp, 4 * h + 4)
                for i in range(4):
                    ins = pe.matmul(zreg(h, i), um[:, :], t[:, off[i]:off[i] + width[i]], start=False, stop=False,
                                    skip_group_check=True)
                    for later in range(i + 1, 4):
                        ins = pe.matmul(zreg(h, i, (later - i) * P), neg[:, :], t[:, off[later]:off[later] + width[later]],
                                        start=False, stop=later == 3, skip_group_check=True)
                ins.then_inc(s_acc, 1)

            def values(h):
                r, pair = HD * (h % 2), h // 2
                pe.wait_ge(s_am, 4 * h + 4)
                if pair >= 2:
                    pe.wait_ge(s_al, pair - 1)
                for i in range(4):
                    ins = pe.matmul(bank[6 + pair % 2][r:r + HD, i * P:TP], v[:, i, h * HD:(h + 1) * HD],
                                    a1280[h % 2][:, off[i]:off[i] + width[i]], start=i == 0, stop=i == 3,
                                    skip_group_check=True)
                ins.then_inc(s_av, 1)

            pe.wait_ge(s_trf, G_CONV + 1)
            pe.wait_ge(s_free, 5 * CH_C)
            scores(0)
            for h in range(H):
                if h + 1 < H:
                    scores(h + 1)
                log_sums(h)
                if h:
                    values(h - 1)
            values(H - 1)

            def keys_scores(b, par, reuse):
                pe.wait_ge(s_kc, 16 * b + 16)
                if reuse > 0:
                    pe.wait_ge(s_kta, 2 * b)
                    pe.wait_ge(s_ktv, 2 * b)
                for kb in range(KB):
                    for hp in range(HP):
                        ins = pe.transpose(bank[kb][:, hp * P:(hp + 1) * P], kc[:, kb, hp * P:(hp + 1) * P], ident[:, :])
                    ins.then_inc(s_kt, 1)
                pe.wait_ge(s_kta, 2 * b + 2)
                pe.wait_ge(s_ktv, 2 * b + 2)
                pe.wait_ge(s_qb, 3 * b + 3)
                if reuse > 1:
                    pe.wait_ge(s_af, 2 * b - 2)
                for kb in range(KB):
                    for hp in range(HP):
                        pe.matmul(bank[4 + par][:, kb * P + hp * 2 * TS:kb * P + (hp + 1) * 2 * TS], ktc[:, kb, hp],
                                  qbd[:, par, hp], start=kb == 0 and hp == 0, stop=False, skip_group_check=True)
                for hp in range(HP):
                    ins = pe.matmul(bank[6 + par][0:TS, hp * 2 * TS:(hp + 1) * 2 * TS], ktn[:, par, hp],
                                    qbd[:, par, hp], start=hp == 0, stop=False, skip_group_check=True)
                ins.then_inc(s_zs, 1)

            def sums_values(b, par, turn):
                pe.wait_ge(s_spn, b + 1)
                z = bank[4 + par]
                pe.matmul(z[:, :], um[:, :], sps[:, :], start=False, stop=False, skip_group_check=True)
                for kb in range(1, KB):
                    pe.matmul(z[:, 0:kb * P], neg[:, :], sps[:, None, kb * P:(kb + 1) * P].to_broadcast([P, kb, P]),
                              start=False, stop=False, skip_group_check=True)
                pe.matmul(z[:, :], neg[0:TS, :], spn[:, None, :].to_broadcast([TS, KB, P]), start=False, stop=True,
                          skip_group_check=True)
                pe.matmul(bank[6 + par][0:TS, 0:P], um[0:TS, 0:TS], spn[:, :], start=False, stop=True,
                          skip_group_check=True).then_inc(s_accs, 1)
                pe.wait_ge(s_eas, 2 * b + 2)
                pe.wait_ge(s_ams, b + 1)
                pe.wait_ge(s_vcl[par], 32 * turn + 32)
                for hp in range(HP):
                    out = bank[6 + par][:, P + hp * 2 * TS:P + (hp + 1) * 2 * TS]
                    for kb in range(KB):
                        pe.matmul(out, vc[:, par, kb, hp * P:(hp + 1) * P],
                                  a_s[par][:, kb * P + hp * 2 * TS:kb * P + (hp + 1) * 2 * TS],
                                  start=kb == 0, stop=False, skip_group_check=True)
                    ins = pe.matmul(out, vn[:, par, hp * P:(hp + 1) * P], an[:, par, hp * 2 * TS:(hp + 1) * 2 * TS],
                                    start=False, stop=True, skip_group_check=True)
                ins.then_inc(s_avs, 1)

            pe.wait_ge(s_al, HP)
            keys_scores(0, 0, 0)
            keys_scores(1, 1, 1)
            sums_values(0, 0, 0)
            with pe.Fori(1, 4) as i:
                keys_scores(2 * i, 0, 2)
                sums_values(2 * i - 1, 1, i - 1)
                keys_scores(2 * i + 1, 1, 2)
                sums_values(2 * i, 0, i)
            sums_values(7, 1, 3)

            pe.wait_ge(s_al, HP + 1)
            pe.wait_ge(s_cl, NT)
            with pe.Fori(0, 2) as n:
                for q, (nu, b_hi, b_lo) in enumerate(((4, hh, hl), (2, ah, al), (4, hh, hl), (2, ch, cl))):
                    transposed(Unit(U_C + (0, 4, 6, 10)[q], 12, n), nu, 5 * (CH_C + q) + 20 * n, b_hi, b_lo)

            natural(U_D, 4, CH_D, hh, hl, before_unit=lambda i: pe.wait_ge(s_ml, 2 * i + 2))
            pe.wait_ge(s_ple, 32)
            for t in range(NT):
                tr_rows(G_PLE + t, praw[:, t], n=2)
            natural(U_D + 4, 4, CH_D + 1, hh, hl)
            for t in range(NT):
                pe.wait_ge(s_hn, NT + t + 1)
                for half in range(2):
                    tr_rows(G_R + 2 * t + half, h2[:, t, half * W:(half + 1) * W])
            pe.wait_ge(s_trf, G_F)
            for t in range(NT):
                for k in range(KD):
                    ins = pe.matmul(bank[6][:, t * (NG + NE):(t + 1) * (NG + NE)], h2T[:, k, t * P:(t + 1) * P],
                                    wr[:, k], start=k == 0, stop=k == KD - 1, skip_group_check=True)
            ins.then_inc(s_rt, 1)
            natural(U_P, 1, CH_P, ph, pl)
            pe.wait_ge(s_M, 1)
            for t in range(NT):
                out = bank[6][:, P + t * NE:P + (t + 1) * NE]
                ins = pe.matmul(out, before[:, :], Mb[:, t], start=True, stop=t == 0, skip_group_check=True)
                for s in range(t):
                    ins = pe.matmul(out, onesb[:, :], Mb[:, s], start=False, stop=s == t - 1, skip_group_check=True)
            ins.then_inc(s_rk, 1)
            natural(U_P + 1, 1, CH_P + 1, ph, pl)
            pe.wait_ge(s_ovm, 1)
            pe.matmul(bank[7][0:1, 0:1], ovm[:, 0:1], ones1[:, 0:1], start=True, stop=True).then_inc(s_ov, 1)

            def expert_rows(e, par, turn):
                pe.wait_ge(s_xe[par], 16 * turn + 16)
                for half in range(2):
                    if not (isinstance(e, int) and e == 0):
                        pe.wait_ge(s_xl, 2 * e - 1 + half)
                    for q in range(4):
                        ins = pe.transpose(bank[4 + half][:, q * P:(q + 1) * P],
                                           xe[:, par, (4 * half + q) * P:(4 * half + q + 1) * P], ident[:, :])
                    ins.then_inc(s_xt, 1)

            def product(u, out, a_hi, a_lo, k0, first, last):
                pe.wait_ge(s_lo, u.count())
                for kk in range(2):
                    ins = three(pe, out, a_hi[:, k0 + kk], a_lo[:, k0 + kk], whi[:, u.slot, kk], wlo[:, u.slot, kk],
                                first and kk == 0, last and kk == 1)
                ins.then_inc(s_mm, 5)

            def gate_or_up(u, e, which):
                if which == 0:
                    pe.wait_ge(s_xl, 2 * e + 2)
                    pe.wait_ge(s_si, e)
                else:
                    pe.wait_ge(s_hm, e)
                for i in range(4):
                    product(u.plus(i), bank[which][:, :], xh, xl, 2 * i, i == 0, i == 3)

            def hidden_rows(e):
                pe.wait_ge(s_hm, e + 1)
                pe.wait_ge(s_htl, e)
                for q in range(4):
                    ins = pe.transpose(bank[6][:, q * P:(q + 1) * P], hm[:, q * P:(q + 1) * P], ident[:, :])
                ins.then_inc(s_ht, 1)

            def down(u, e):
                pe.wait_ge(s_htl, e + 1)
                for n in range(2):
                    pe.wait_ge(s_y, 2 * e)
                    for i in range(2):
                        product(u.plus(2 * n + i), bank[2 + n][:, :], mh, ml, 2 * i, i == 0, i == 1)

            pe.wait_ge(s_free, 5 * CH_G)
            expert_rows(0, 0, 0)
            gate_or_up(Unit(U_M), 0, 0)
            gate_or_up(Unit(U_M + 4), 0, 1)
            expert_rows(1, 1, 0)

            def expert(e, par, turn, rows_next=True):
                u = Unit(U_M - 4, NSTREAM, e)
                gate_or_up(u, e, 0)
                hidden_rows(e - 1)
                gate_or_up(u.plus(4), e, 1)
                if rows_next:
                    expert_rows(e + 1, 1 - par, turn)
                down(u.plus(8), e - 1)

            with pe.Fori(0, NE // 2 - 1) as i:
                expert(2 * i + 1, 1, i + 1)
                expert(2 * i + 2, 0, i + 1)
            expert(NE - 1, 1, 0, rows_next=False)
            hidden_rows(NE - 1)
            down(Unit(U_G - 4), NE - 1)

            pe.wait_ge(s_flag, 1)
            over = pe.value_load(flag[0:1, 0:1], min_val=0, max_val=1)
            with pe.If(over > 0):
                with pe.Fori(0, NE * OV_TILES) as o:
                    pe.wait_ge(s_o_dve, 3 * o + 3)
                    pe.wait_ge(s_o_act, 3 * o + 3)
                    pe.wait_ge(s_o_x, 16 * o + 16)
                    for k in range(KD):
                        ins = pe.transpose(bank[4 + k // 4][:, (k % 4) * P:(k % 4 + 1) * P], xe[:, 0, k * P:(k + 1) * P],
                                           ident[:, :])
                    ins.then_inc(s_o_pe, 1)
                    pe.wait_ge(s_o_dve, 3 * o + 4)
                    for j in range(12):
                        if j == 8:
                            pe.wait_ge(s_o_dve, 3 * o + 5)
                            for q in range(4):
                                ins = pe.transpose(bank[6][:, q * P:(q + 1) * P], hm[:, q * P:(q + 1) * P], ident[:, :])
                            ins.then_inc(s_o_pe, 1)
                            pe.wait_ge(s_o_dve, 3 * o + 6)
                        pe.wait_ge(s_o_raw[j % RING], 48 * o + 16 * (j // RING) + 16)
                        a, k0, nk = (oxT, 2 * (j % 4), KD) if j < 8 else (omT, 2 * (j % 2), FE // P)
                        out = bank[j // 4] if j < 8 else bank[2 + (j - 8) // 2]
                        for kk in range(2):
                            ins = pe.matmul(out[:, :], a[:, k0 + kk], raw[:, j % RING, kk], start=k0 + kk == 0,
                                            stop=k0 + kk == nk - 1)
                        ins.then_inc(s_o_pe, 1)

            def rows3(t):
                pe.wait_ge(s_hn, 2 * NT + t + 1)
                for half in range(2):
                    tr_rows(G_F + 2 * t + half, hn3[:, t % 2, half * W:(half + 1) * W])

            def g_tile(i, t):
                if i == 0:
                    if t == 0:
                        rows3(0)
                    if t + 1 < NT:
                        rows3(t + 1)
                    pe.wait_ge(s_trf, G_F + 2 * t + 2)

            natural(U_G, 4, CH_G, hh, hl, before_tile=g_tile)
            natural(U_G + 4, 4, CH_G + 1, hh, hl)


def kernel(**inputs):
    import concourse.bacc as bacc
    from concourse.bass_utils import run_bass_kernel_spmd

    nc = bacc.Bacc("TRN2", target_bir_lowering=False, num_devices=1)
    arrays, I = {}, {}
    for name, a in inputs.items():
        a = np.ascontiguousarray(a)
        arrays["in_" + name] = a
        I[name] = nc.dram_tensor("in_" + name, a.shape, mybir.dt.from_np(a.dtype), kind="ExternalInput").ap()
    shapes = [(1, TP, D), (B, TS, D), (1, 1, TP, H, HD), (1, 1, TP, H, HD), (1, 1, 2, W),
              (1, B, TS, H, HD), (1, B, TS, H, HD), (1, B, 2, W)]
    O = [nc.dram_tensor(f"out_{i}", s, F32, kind="ExternalOutput").ap() for i, s in enumerate(shapes)]
    program(nc, I, O)
    r = run_bass_kernel_spmd(nc, [arrays], core_ids=[0])
    return tuple(r.results[0][f"out_{i}"] for i in range(len(shapes)))
```

```python
from contextlib import ExitStack

import numpy as np
import concourse.bass as bass
from concourse import mybir

F32, F32R, BF16, I32 = mybir.dt.float32, mybir.dt.float32r, mybir.dt.bfloat16, mybir.dt.int32
ACT, ALU, AX = mybir.ActivationFunctionType, mybir.AluOpType, mybir.AxisListType

P = 128
D = 1024
KD = D // P
TP, B, TS = 512, 8, 16
T = TP + B * TS
NT = T // P
W = 512
KW = W // P
H, HD = 8, 64
HP = H // 2
PAST = 512
KB = PAST // P
NG, EG = 4, 4
NE = NG * EG
FE = 512
PLE = 256
EPS = 1e-6
C = 128
OV_TILES = (T - C) // P
RING = 4

HALF = T // 2
NB = 2 * KD
U_CC = 3 * KD // 2
U_C = U_CC + 3 * KW
U_D = U_C + 2 * NB
U_P, U_M = U_D + KD, U_D + KD + 2
F_CC = 3 * NT
F_D = F_CC + 3 * 2 * KW
F_P, F_G = F_D + 2 * NT, F_D + 4 * NT
NSTREAM = 12
U_G = U_M + NE * NSTREAM
G_X, G_STATE, G_QK, G_CONV, G_PLE, G_R, G_F = 0, 10, 11, 21, 22, 27, 37


class Unit:

    def __init__(self, c, stride=0, k=0):
        self.c, self.stride, self.k, self.slot = c, stride, k, c % RING

    def plus(self, n):
        return Unit(self.c + n, self.stride, self.k)

    def count(self, less=0):
        return (self.c + 1 - less) + self.stride * self.k

    def turn16(self):
        return 16 * (self.c // RING + 1) + 16 * (self.stride // RING) * self.k

    def mm(self, less=0):
        return 5 * (self.c + 1 - less) + 5 * self.stride * self.k

    def half(self, h):
        return 5 * self.c + (2, 5)[h] + 5 * self.stride * self.k


def program(nc, I, O):
    ctx = ExitStack()
    with ctx:
        base = 16512
        cursor = [base]

        def at(name, shape, dt, off):
            return nc.alloc_sbuf_tensor_at(name, shape, dt, offset=off)

        def size(shape, dt=F32):
            n = 2 if dt == BF16 else 4
            for s in shape[1:]:
                n *= s
            return (n + 31) // 32 * 32

        def sb(name, shape, dt=F32):
            t = at(name, shape, dt, cursor[0])
            cursor[0] += size(shape, dt)
            return t

        class Region:
            def __init__(self, nbytes):
                self.start = cursor[0]
                self.end = self.start + nbytes
                cursor[0] += nbytes

            def lay(self, *specs):
                off, out = self.start, []
                for name, shape, dt in specs:
                    out.append(at(name, shape, dt, off))
                    off += size(shape, dt)
                assert off <= self.end, (specs, off, self.end)
                return out if len(out) > 1 else out[0]

        ident = sb("ident", [P, P])
        um = sb("um", [P, P])
        neg = sb("neg", [P, P])
        before = sb("before", [P, P], BF16)
        onesb = sb("onesb", [P, P], BF16)
        ones1 = sb("ones1", [P, 1])
        zero = sb("zero", [P, P])
        mhalf = sb("mhalf", [P, 8])
        lnb_off = cursor[0]
        lnb = sb("lnb", [P, D])
        qkg = sb("qkg", [P, 2, HD])
        convw = sb("convw", [P, 3, KW])
        rbias = sb("rbias", [P, NG + NE])
        wr = sb("wr", [P, KD, NG + NE])
        ss = sb("ss", [P, 3 * NT])
        rms = sb("rms", [P, 3 * NT])
        rr = sb("rr", [P, 3 * NT])
        ssq = sb("ssq", [P, 10, H])
        msq = sb("msq", [P, 10, H])
        rq = sb("rq", [P, 10, H])
        cpk = sb("cpk", [P, KW, 2 + 2 * B])
        lg = sb("lg", [P, NT, NG + NE])
        desc = sb("desc", [P, 4])
        eidx = sb("eidx", [P, NE])
        gmax, cm1, v1, v2, vdiff, vexp, vsum, gsum = [
            sb(name, [P, NT]) for name in ("gmax", "cm1", "v1", "v2", "vdiff", "vexp", "vsum", "gsum")]
        gdiff, gexp, lsel2 = [sb(name, [P, NT, 4]) for name in ("gdiff", "gexp", "lsel2")]
        ovm = sb("ovm", [P, 1])
        free_ = sb("free_", [P, 1])
        og = sb("og", [P, NT, 4])
        ok = sb("ok", [P, 2, NT, 4])
        cand = sb("cand", [P, NT, 4])
        lsel = sb("lsel", [P, NT, 4])
        prod = sb("prod", [P, NT, 4, 4])
        Mk = sb("Mk", [P, 2, NT, NE])
        Mb = sb("Mb", [P, NT, NE], BF16)
        rk = sb("rk", [P, NT, NE])
        mr = sb("mr", [P, 2, NT, NE])
        slotf = sb("slotf", [P, 4, 2, NT])
        gate = sb("gate", [P, 2, NT])
        slot = sb("slot", [P, 2, NT], I32)
        flag = sb("flag", [1, 1], I32)
        spn = sb("spn", [TS, P])
        tmpn = sb("tmpn", [TS, P])
        an = sb("an", [TS, P])
        qbd = sb("qbd", [P, 2, HP, 2 * TS])
        ktb = sb("ktb", [P, 2, HP, TS])
        af = sb("af", [P, HP, P])
        raw = sb("raw", [P, RING, 2, W])
        whi = sb("whi", [P, RING, 2, W], F32R)
        wlo = sb("wlo", [P, RING, 2, W], F32R)

        XR = Region(NT * D * 4)
        HT = Region(2 * KD * T * 4)
        CT = Region(2 * KW * T * 4)
        AT = Region(2 * KW * T * 4)
        QK = Region(2 * KW * T * 4)
        VV = Region(NT * W * 4)
        TAIL = Region(229344 - cursor[0])

        x = XR.lay(("x", [P, NT, D], F32))
        hh, hl = HT.lay(("hh", [P, KD, T], F32R), ("hl", [P, KD, T], F32R))
        ch, cl = CT.lay(("ch", [P, KW, T], F32R), ("cl", [P, KW, T], F32R))
        ah, al = AT.lay(("ah", [P, KW, T], F32R), ("al", [P, KW, T], F32R))
        qT, kT = QK.lay(("qT", [P, KW, T], F32), ("kT", [P, KW, T], F32))
        v = VV.lay(("v", [P, NT, W], F32))
        hn, zb, sqb, qn1, qn2 = AT.lay(("hn", [P, 2, D], F32), ("zb", [P, 2, W], F32), ("sqb", [P, 1, W], F32),
                                       ("qn1", [P, 1, W], F32), ("qn2", [P, 2, W], F32))
        junk = TAIL.lay(("junk", [P, D], F32))
        ccT, yc = XR.lay(("ccT", [P, KW, T], F32), ("yc", [P, KW, T], F32))
        up, us = TAIL.lay(("up", [P, KW, 2 + TP], F32), ("us", [P, KW, B, 2 + TS], F32))
        ncv = at("ncv", [2 + 2 * B, W], F32, AT.start)
        st = at("st", [2 * B, W], F32, VV.start)
        tm0, tm1, sp0, sp1 = XR.lay(("tm0", [P, 1280], F32), ("tm1", [P, 1280], F32),
                                    ("sp0", [P, 1280], F32), ("sp1", [P, 1280], F32))
        a0, a1 = TAIL.lay(("a0", [P, 1280], F32), ("a1", [P, 1280], F32))
        tmp1280, sp1280, a1280 = [tm0, tm1], [sp0, sp1], [a0, a1]
        vc, tms, sps = XR.lay(("vc", [P, KB, W], F32), ("tms", [P, W], F32), ("sps", [P, W], F32))
        kc, sg = TAIL.lay(("kc", [P, KB, W], F32), ("sg", [P, T], F32))
        ktc, qs, ks, a_s = VV.lay(("ktc", [P, 2, HP, P], F32), ("qs", [P, HP, P], F32), ("ks", [P, HP, P], F32),
                                  ("a_s", [P, W], F32))
        vn = at("vn", [TS, W], F32, lnb_off)
        m = QK.lay(("m", [P, KD, T], F32))
        mt = TAIL.lay(("mt", [P, T], F32))
        h2 = QK.lay(("h2", [P, NT, D], F32))
        h2T = at("h2T", [P, KD, T], F32, VV.start)
        praw, junk2 = CT.lay(("praw", [P, NT, PLE], F32), ("junk2", [P, D], F32))
        ph, pl = [at(n, [P, 2, T], F32R, CT.start + KW * T * 4 + i * 2 * T * 4) for i, n in enumerate(("ph", "pl"))]
        pp = AT.lay(("pp", [P, NT, D], F32))
        xe, xh, xl, si, hm, mh, ml, y = HT.lay(
            ("xe", [P, 2, D], F32), ("xh", [P, KD, P], F32R), ("xl", [P, KD, P], F32R), ("si", [P, FE], F32),
            ("hm", [P, FE], F32), ("mh", [P, FE // P, P], F32R), ("ml", [P, FE // P, P], F32R), ("y", [P, 2, D], F32))
        oxT, omT = CT.lay(("oxT", [P, KD, P], F32), ("omT", [P, FE // P, P], F32))
        NYG = 4
        yg = at("yg", [P, NYG, D], F32, VV.start)
        hn3, eo = QK.lay(("hn3", [P, 2, D], F32), ("eo", [P, 4, W], F32))

        bank = [ctx.enter_context(nc.psum_tensor(f"bank{i}", [P, 512], F32)) for i in range(8)]
        Xd = nc.dram_tensor("moe_rows", ((NE * C) + NE * OV_TILES * P, D), F32, kind="Internal").ap()
        Yd = nc.dram_tensor("moe_out", ((NE * C) + NE * OV_TILES * P, D), F32, kind="Internal").ap()

        def sem(name):
            return ctx.enter_context(nc.semaphore(name))

        s_const = sem("constants_loaded")
        s_ln = sem("norm_weights_loaded")
        s_x = [sem(f"x_loaded{t}") for t in range(NT)]
        s_made = sem("constants_made")
        s_pc = sem("pool_step")
        s_vc = sem("vector_step")
        s_raw = [sem(f"raw_loaded{i}") for i in range(RING)]
        s_hi = sem("weights_hi")
        s_lo = sem("weights_lo")
        s_mm = sem("products_done")
        s_free = sem("banks_read")
        s_sq = sem("squares_summed")
        s_r = sem("rms_ready")
        s_hn = sem("rows_normed")
        s_tr = sem("transposed")
        s_trh = sem("transposed_hi")
        s_trf = sem("transposed_read")
        s_qsq = sem("head_squares")
        s_ssq = sem("head_sums")
        s_rq = sem("head_rms")
        s_qn1 = sem("head_scaled")
        s_qn2 = sem("head_normed")
        s_ko = [sem(f"k_stored{i}") for i in range(2)]
        s_vout = sem("v_stored")
        s_state = sem("conv_state_loaded")
        s_ch = sem("gated_conv_hi")
        s_cl = sem("gated_conv_lo")
        s_cpk = sem("last_inputs_packed")
        s_ncvo = sem("conv_state_stored")
        s_zero = sem("rows_zeroed")
        s_z = sem("scores")
        s_ln1 = sem("log_terms")
        s_spr = sem("softplus")
        s_sp = sem("softplus_masked")
        s_acc = sem("log_sums")
        s_ea = sem("weights_exp")
        s_am = sem("weights_masked")
        s_av = sem("head_pairs_summed")
        s_ah = sem("attn_hi")
        s_al = sem("attn_lo")
        s_kc = [sem(f"cache_k_loaded{i}") for i in range(2)]
        s_vcl = sem("cache_v_loaded")
        s_qb = sem("queries_placed")
        s_qs = sem("sample_rows_moved")
        s_kt = sem("cache_k_transposed")
        s_kta = sem("cache_kT_scalar")
        s_ktv = sem("cache_kT_vector")
        s_zs = sem("sample_scores")
        s_lns = sem("sample_log_terms")
        s_sps = sem("sample_softplus")
        s_spn = sem("sample_softplus_masked")
        s_accs = sem("sample_log_sums")
        s_eas = sem("sample_weights_exp")
        s_ams = sem("sample_weights_masked")
        s_avs = sem("sample_values")
        s_af = sem("sample_attn_kept")
        s_gate = sem("gate_sigmoids")
        s_br = sem("branches_gated")
        s_m = sem("merged")
        s_mh = sem("merged_hi")
        s_ml = sem("merged_lo")
        s_xr = sem("x_reloaded")
        s_ple = sem("ple_rows_loaded")
        s_rt = sem("router_logits")
        s_rx = sem("router_exps")
        s_d = sem("router_differences")
        s_M = sem("choices")
        s_rk = sem("ranks")
        s_slot = sem("slots")
        s_ovm = sem("overflow_rows_marked")
        s_ov = sem("overflow_sum")
        s_flag = sem("overflow_flag")
        s_scat = sem("rows_scattered")
        s_xe = [sem(f"expert_rows_loaded{i}") for i in range(2)]
        s_xt = sem("expert_rows_transposed")
        s_xh = sem("expert_rows_hi")
        s_xl = sem("expert_rows_lo")
        s_si = sem("silu")
        s_hm = sem("hidden")
        s_ht = sem("hidden_transposed")
        s_hth = sem("hidden_hi")
        s_htl = sem("hidden_lo")
        s_y = sem("expert_outputs")
        s_yo = [sem(f"expert_outputs_stored{i}") for i in range(2)]
        s_o_x = sem("overflow_rows_loaded")
        s_o_raw = [sem(f"overflow_raw_loaded{i}") for i in range(RING)]
        s_o_free = sem("overflow_output_free")
        s_o_pe = sem("overflow_products")
        s_o_act = sem("overflow_scalar")
        s_o_dve = sem("overflow_vector")
        s_o_st = sem("overflow_stored")
        s_yg = [sem(f"outputs_gathered{i}") for i in range(NYG)]
        s_yu = sem("outputs_added")
        s_eo = sem("result_tile")
        s_out = [sem(f"result_stored{i}") for i in range(4)]

        small = [bank[4], bank[7]]

        block = ctx.enter_context(nc.Block())


        def load_unit(sp, u, src):
            if u.c >= RING:
                sp.wait_ge(s_lo, u.count(RING))
            sp.dma_start(raw[:, u.slot], src).then_inc(s_raw[u.slot], 16)

        def load_columns(sp, u, w, j):
            nk = w.shape[0] // P
            src = w.rearrange("(k p) (j c) -> p k j c", p=P, c=P)[:, :, bass.ds(j, 1)].rearrange("p k o c -> p k (o c)")
            sp.wait_ge(s_lo, u.count(RING))
            sp.dma_start(columns(raw, u)[:, 0:nk], src).then_inc(s_raw[u.slot], 16)

        def columns(ring, u):
            return ring[:, u.slot].rearrange("p a (k c) -> p (a k) c", c=P)

        def part(ring, u, short):
            return ring[:, u.slot, 0] if short else ring[:, u.slot]

        def split_hi(act, u, short=False):
            act.wait_ge(s_raw[u.slot], u.turn16())
            if u.c >= RING:
                act.wait_ge(s_mm, u.mm(RING))
            nc.scalar.activation(part(whi, u, short), part(raw, u, short), ACT.Copy).then_inc(s_hi, 1)

        def split_lo(dve, u, short=False):
            dve.wait_ge(s_hi, u.count())
            nc.vector.tensor_tensor(out=part(wlo, u, short), in0=part(raw, u, short),
                                    in1=part(whi, u, short).bitcast(F32), op=ALU.subtract).then_inc(s_lo, 1)

        def gate_unit(c):
            return Unit(U_C + 2 * c) if isinstance(c, int) else Unit(U_C + 2 * c[1], 4, c[0])

        def number(c):
            return c if isinstance(c, int) else 2 * c[0] + c[1]

        def later(c, n):
            return c + n if isinstance(c, int) else (c[0], c[1] + n)

        def is_zero(n):
            return isinstance(n, int) and n == 0

        def half_rows(h):
            return slice(h * HALF, (h + 1) * HALF)

        def three(pe, out, a_hi, a_lo, b_hi, b_lo, first, last):
            pe.matmul(out, a_hi, b_hi, start=first, stop=False, skip_group_check=True)
            pe.matmul(out, a_lo, b_hi, start=False, stop=False, skip_group_check=True)
            return pe.matmul(out, a_hi, b_lo, start=False, stop=last, skip_group_check=True)

        def ring_bank(g):
            return bank[5 + g % 3]

        def rows(w, k0, col):
            return w[k0 * P:(k0 + 2) * P, col:col + W].rearrange("(k p) c -> p k c", p=P)

        def flat(name):
            return I[name].rearrange("o k n -> (o k) n")

        @block.sync
        def _(sp):
            sp.dma_start(lnb[:, :], I["ln_mix"].to_broadcast([P, D])).then_inc(s_ln, 16)
            xp = I["x_prompt"].rearrange("o (t p) d -> p (o t) d", p=P)
            xs = I["x_sample"].rearrange("b s d -> (b s) d")
            w_in = flat("w_in")
            for t in range(NT):
                sp.dma_start(x[:, t], xp[:, t] if t < NT - 1 else xs).then_inc(s_x[t], 16)
                if t < RING:
                    load_unit(sp, Unit(t), rows(w_in, 2 * t, 0))
            sp.dma_start(st[:, :], I["state_conv"].rearrange("o b j c -> (o b j) c")).then_inc(s_state, 16)
            for c in range(1, 3):
                for i in range(4):
                    load_unit(sp, Unit(4 * c + i), rows(w_in, 2 * i, W * c))
            for c, place in enumerate((4, 5, 3)):
                for j in range(KW):
                    load_columns(sp, Unit(U_CC + KW * c + j), w_in, KW * place + j)

            def conv_block(c):
                load_columns(sp, gate_unit(c), w_in, 8 * KW + number(c))
                load_columns(sp, gate_unit(c).plus(1), flat("w_conv_branch"), number(c))

            def attn_block(c):
                load_columns(sp, gate_unit(c), w_in, 6 * KW - KD + number(c))
                load_columns(sp, gate_unit(c).plus(1), flat("w_attn_branch"), number(c) - KD)

            conv_block(0)
            conv_block(1)

            ck = I["cache_k"].rearrange("o b (kb p) h d -> p (o b) kb (h d)", p=P)
            cv = I["cache_v"].rearrange("o b (kb p) h d -> p (o b) kb (h d)", p=P)
            vnew = O[6].rearrange("o b s h d -> (o b) s (h d)")

            def cache_k(b):
                for i in range(2):
                    src = ck[:, bass.ds(b, 1), 2 * i:2 * i + 2].rearrange("p o kb c -> p (o kb) c")
                    if not is_zero(b):
                        sp.wait_ge(s_kt, 4 * b - 2 + 2 * i)
                    sp.dma_start(kc[:, 2 * i:2 * i + 2], src).then_inc(s_kc[i], 16)

            def cache_v(b):
                src = cv[:, bass.ds(b, 1)].rearrange("p o kb c -> p (o kb) c")
                new = vnew[bass.ds(b, 1)].rearrange("o s c -> s (o c)")
                if not is_zero(b):
                    sp.wait_ge(s_avs, b)
                sp.dma_start(vc[:, :, :], src).then_inc(s_vcl, 16)
                sp.dma_start(vn[:, :], new).then_inc(s_vcl, 16)

            sp.wait_ge(s_vout, 16 * NT)
            sp.wait_ge(s_hn, NT)
            sp.wait_ge(s_av, H)
            cache_k(0)
            cache_v(0)
            with sp.Fori(0, 3) as i:
                for n in range(1, 3):
                    cache_k(2 * i + n)
                    conv_block((i, n + 1))
                    cache_v(2 * i + n)
            cache_k(B - 1)
            attn_block(8)
            cache_v(B - 1)
            attn_block(9)
            sp.wait_ge(s_al, HP + 1)
            for t in range(NT):
                sp.dma_start(x[:, t], xp[:, t] if t < NT - 1 else xs).then_inc(s_xr, 16)
            sp.dma_start(lnb[:, :], I["ln_ffn"].to_broadcast([P, D])).then_inc(s_ln, 16)
            with sp.Fori(5, NB // 2) as i:
                attn_block((i, 0))
                attn_block((i, 1))
            sp.wait_ge(s_mm, gate_unit(B - 1).plus(1).mm())
            sp.dma_start(praw[:, 0:NT - 1], I["p_prompt"].rearrange("o b (t p) c -> p (o b t) c", p=P)
                         ).then_inc(s_ple, 16)
            sp.dma_start(praw[:, NT - 1], I["p_sample"].rearrange("o b s c -> (o b s) c")).then_inc(s_ple, 16)
            u = U_D
            for n in range(2):
                for i in range(4):
                    load_unit(sp, Unit(u), rows(flat("w_out"), 2 * i, n * W))
                    u += 1
            for n in range(2):
                load_unit(sp, Unit(u), rows(flat("w_ple_proj"), 0, n * W))
                u += 1
            assert u == U_M

            gup = [I[n].rearrange("o e (k p) f -> p (o e) k f", p=P) for n in ("w_exp_gate", "w_exp_up")]
            dwn = I["w_exp_down"].rearrange("o e (k p) f -> p (o e) k f", p=P)

            def gate_up_src(e, j):
                return gup[j // 4][:, bass.ds(e, 1), 2 * (j % 4):2 * (j % 4) + 2].rearrange("p o k f -> p (o k) f")

            def down_src(e, j):
                return dwn[:, bass.ds(e, 1), 2 * (j % 2):2 * (j % 2) + 2,
                           (j // 2) * W:(j // 2 + 1) * W].rearrange("p o k f -> p (o k) f")

            for j in range(4):
                load_unit(sp, Unit(U_M + j), gate_up_src(0, j))
            sp.wait_ge(s_scat, 16 * 2 * NT)
            for e in range(2):
                sp.dma_start(xe[:, e], Xd[e * C:(e + 1) * C, :]).then_inc(s_xe[e], 16)
            for j in range(4, 8):
                load_unit(sp, Unit(U_M + j), gate_up_src(0, j))

            def expert_loads(e, par, rows_next=True):
                for j in range(4):
                    load_unit(sp, Unit(U_M - 4 + j, NSTREAM, e), gate_up_src(e, j))
                if rows_next:
                    sp.wait_ge(s_xt, 2 * e)
                    sp.dma_start(xe[:, 1 - par], Xd[bass.ds((e + 1) * C, C), :]).then_inc(s_xe[1 - par], 16)
                for j in range(4, 8):
                    load_unit(sp, Unit(U_M - 4 + j, NSTREAM, e), gate_up_src(e, j))
                for j in range(4):
                    load_unit(sp, Unit(U_M + 4 + j, NSTREAM, e), down_src(e - 1, j))

            with sp.Fori(0, NE // 2 - 1) as i:
                expert_loads(2 * i + 1, 1)
                expert_loads(2 * i + 2, 0)
            expert_loads(NE - 1, 1, rows_next=False)
            for j in range(4):
                load_unit(sp, Unit(U_G - 4 + j), down_src(NE - 1, j))

            sp.wait_ge(s_flag, 1)
            over = sp.value_load(flag[0:1, 0:1], min_val=0, max_val=1)
            with sp.If(over > 0):
                with sp.Fori(0, NE) as e:
                    with sp.Fori(0, OV_TILES) as o:
                        n = e * OV_TILES + o
                        sp.wait_ge(s_o_act, 3 * n + 3)
                        sp.dma_start(xe[:, 0], Xd[bass.ds(NE * C + n * P, P), :]).then_inc(s_o_x, 16)
                        for j in range(12):
                            if j >= RING:
                                sp.wait_ge(s_o_pe, 14 * n + j - 2)
                            sp.dma_start(raw[:, j % RING], gate_up_src(e, j) if j < 8 else down_src(e, j - 8)
                                         ).then_inc(s_o_raw[j % RING], 16)
                sp.wait_ge(s_o_act, 3 * NE * OV_TILES + 3)
            sp.dma_start(lnb[:, :], I["ln_ple"].to_broadcast([P, D])).then_inc(s_ln, 16)
            for i in range(8):
                load_unit(sp, Unit(U_G + i), rows(flat("w_ple_gate"), 2 * (i % 4), (i // 4) * W))
            for i in range(2 * NT):
                n, t = i // NT, i % NT
                dst = (O[0].rearrange("o (t p) d -> p (o t) d", p=P)[:, t] if t < NT - 1
                       else O[1].rearrange("b s d -> (b s) d"))
                sp.wait_ge(s_eo, i + 1)
                sp.dma_start(dst[:, n * W:(n + 1) * W], eo[:, i % 4]).then_inc(s_out[i % 4], 16)
            for i in range(4):
                sp.wait_ge(s_out[i], 16 * len(range(i, 2 * NT, 4)))
            sp.wait_ge(s_ko[0], 16 * 2)
            sp.wait_ge(s_ko[1], 16 * 3)
            sp.wait_ge(s_vout, 16 * NT)
            sp.wait_ge(s_ncvo, 32)

        @block.gpsimd
        def _(pool):
            pl_ = nc.gpsimd
            for tile, value in ((ident, 0.0), (um, -1.0), (neg, -1.0), (before, 1.0), (onesb, 1.0), (ones1, 1.0),
                                (mhalf, -0.5), (zero, 0.0)):
                pl_.memset(tile[:], value).then_inc(s_made, 1)
            pl_.memset(qbd[:], 0.0).then_inc(s_made, 1)
            pl_.iota(desc[:], pattern=[[-1, 4]], base=4, channel_multiplier=0,
                     allow_small_or_imprecise_dtypes=True).then_inc(s_made, 1)
            pl_.iota(eidx[:], pattern=[[1, NE]], base=0, channel_multiplier=0,
                     allow_small_or_imprecise_dtypes=True).then_inc(s_made, 1)
            pool.wait_ge(s_made, 11)
            pl_.affine_select(out=ident[:], in_=ident[:], compare_op=ALU.not_equal, fill=1.0, base=0,
                              pattern=[[-1, P]], channel_multiplier=1).then_inc(s_made, 1)
            pl_.affine_select(out=um[:], in_=um[:], compare_op=ALU.is_ge, fill=0.0, base=0,
                              pattern=[[-1, P]], channel_multiplier=1).then_inc(s_made, 1)
            pl_.affine_select(out=before[:], in_=before[:], compare_op=ALU.is_gt, fill=0.0, base=0,
                              pattern=[[1, P]], channel_multiplier=-1).then_inc(s_made, 1)
            with nc.allow_non_contiguous_dma(reason="small weights"):
                pool.dma_start(qkg[:, 0], I["q_norm"].to_broadcast([P, HD])).then_inc(s_const, 16)
                pool.dma_start(qkg[:, 1], I["k_norm"].to_broadcast([P, HD])).then_inc(s_const, 16)

            step = [0]

            def link(ins):
                step[0] += 1
                ins.then_inc(s_pc, 1)
                pool.wait_ge(s_pc, step[0])

            def row_rms(i):
                pool.wait_ge(s_sq, i + 1)
                link(pl_.tensor_scalar(rms[:, i:i + 1], ss[:, i:i + 1], 1.0 / D, EPS, ALU.mult, ALU.add))
                pl_.tensor_tensor(rr[:, i:i + 1], rms[:, i:i + 1], mhalf[:, 0:1], ALU.pow).then_inc(s_r, 1)

            for t in range(NT):
                row_rms(t)
            pool.wait_ge(s_const, 32)
            link(pl_.tensor_scalar(qkg[:, 0], qkg[:, 0], HD ** -0.5, 1.0, ALU.mult, ALU.mult))
            with nc.allow_non_contiguous_dma(reason="small weights"):
                for j in range(3):
                    pool.dma_start(convw[:, j], I["conv_w"][0, j].rearrange("(c p) -> p c", p=P)).then_inc(s_const, 16)
                pool.dma_start(rbias[:, 0:NG], I["b_router_group"].to_broadcast([P, NG])).then_inc(s_const, 16)
                pool.dma_start(rbias[:, NG:], I["b_router_expert"].to_broadcast([P, NE])).then_inc(s_const, 16)
                pool.dma_start(wr[:, :, 0:NG], flat("w_router_group").rearrange("(k p) n -> p k n", p=P)
                               ).then_inc(s_const, 16)
                pool.dma_start(wr[:, :, NG:], flat("w_router_expert").rearrange("(k p) n -> p k n", p=P)
                               ).then_inc(s_const, 16)
            pl_.memset(up[:, :, 0:2], 0.0).then_inc(s_made, 1)

            kp = O[2].rearrange("o b (t p) h d -> p (o b t) (h d)", p=P)
            ks = O[5].rearrange("o b s h d -> (o b s) (h d)")
            vp = O[3].rearrange("o b (t p) h d -> p (o b t) (h d)", p=P)
            vs = O[6].rearrange("o b s h d -> (o b s) (h d)")

            def store_k(n):
                t = n - NT
                pool.wait_ge(s_qn2, n + 1)
                pool.dma_start(kp[:, t] if t < NT - 1 else ks, qn2[:, n % 2]).then_inc(s_ko[n % 2], 16)

            for n in range(2 * NT):
                pool.wait_ge(s_free, n + 1)
                if n:
                    pool.wait_ge(s_ssq, n)
                pl_.tensor_tensor(sqb[:, 0], zb[:, n % 2], zb[:, n % 2], ALU.mult).then_inc(s_qsq, 1)
                pool.wait_ge(s_ssq, n + 1)
                link(pl_.tensor_scalar(msq[:, n], ssq[:, n], 1.0 / HD, EPS, ALU.mult, ALU.add))
                pl_.tensor_tensor(rq[:, n], msq[:, n], mhalf[:, :], ALU.pow).then_inc(s_rq, 1)
                if n > NT:
                    store_k(n - 1)
            store_k(2 * NT - 1)
            for t in range(NT):
                pool.wait_ge(s_free, 2 * NT + t + 1)
                pool.dma_start(vp[:, t] if t < NT - 1 else vs, v[:, t]).then_inc(s_vout, 16)
            with pool.Fori(0, NE) as e:
                pool.dma_start(Xd[bass.ds(e * C, C), :].rearrange("r (a b) -> r a b", b=P),
                               zero[:, None, :].to_broadcast([P, D // P, P])).then_inc(s_zero, 16)
            pool.wait_ge(s_free, F_CC + 4 * KW)
            pl_.tensor_copy(cpk[:, :, 0:2], up[:, :, TP:TP + 2]).then_inc(s_cpk, 1)
            for j in range(KW):
                pl_.tensor_copy(cpk[:, j, 2:].rearrange("p (b s) -> p b s", s=2), us[:, j, :, TS:TS + 2]).then_inc(s_cpk, 1)
            pool.wait_ge(s_trf, G_CONV + 1)
            pool.dma_start(O[4].rearrange("o b j c -> (o b j) c"), ncv[0:2]).then_inc(s_ncvo, 16)
            pool.dma_start(O[7].rearrange("o b j c -> (o b j) c"), ncv[2:]).then_inc(s_ncvo, 16)

            diag = (0, 512, 1024, 896)
            for h in range(H + 1):
                if h < H:
                    pool.wait_ge(s_spr, 3 * h + 3)
                    for i in range(4):
                        blk = sp1280[h % 2][:, diag[i]:diag[i] + P]
                        pl_.affine_select(out=blk, in_=blk, compare_op=ALU.is_gt, fill=0.0, base=0,
                                          pattern=[[1, P]], channel_multiplier=-1).then_inc(s_sp, 1)
                if h > 0:
                    pool.wait_ge(s_ea, 3 * h)
                    for i in range(4):
                        blk = a1280[(h - 1) % 2][:, diag[i]:diag[i] + P]
                        pl_.affine_select(out=blk, in_=blk, compare_op=ALU.is_gt, fill=0.0, base=0,
                                          pattern=[[1, P]], channel_multiplier=-1).then_inc(s_am, 1)

            def mask_softplus(b):
                pool.wait_ge(s_sps, 2 * b + 2)
                pl_.affine_select(out=spn[:], in_=spn[:], compare_op=ALU.is_gt, fill=0.0, base=0,
                                  pattern=[[0, H], [1, TS]], channel_multiplier=-1).then_inc(s_spn, 1)

            def mask_weights(b):
                pool.wait_ge(s_eas, 2 * b + 2)
                pl_.affine_select(out=an[:, :], in_=an[:, :], compare_op=ALU.is_gt, fill=0.0, base=0,
                                  pattern=[[0, H], [1, TS]], channel_multiplier=-1).then_inc(s_ams, 1)

            mask_softplus(0)
            for b in range(1, B):
                mask_softplus(b)
                mask_weights(b - 1)
            mask_weights(B - 1)

            for t in range(NT):
                row_rms(NT + t)

            pool.wait_ge(s_flag, 1)
            over = pool.value_load(flag[0:1, 0:1], min_val=0, max_val=1)
            pool.wait_ge(s_zero, 16 * NE)
            with pool.If(over > 0):
                with pool.Fori(0, NE * OV_TILES) as o:
                    pool.dma_start(Xd[bass.ds(NE * C + o * P, P), :].rearrange("r (a b) -> r a b", b=P),
                                   zero[:, None, :].to_broadcast([P, D // P, P])).then_inc(s_zero, 16)
                pool.wait_ge(s_zero, 16 * (NE + NE * OV_TILES))
            pool.wait_ge(s_slot, 1)
            for t in range(NT):
                for k in range(2):
                    pool.indirect_dma_start(out=Xd[:, :], out_offset=bass.IndirectOffsetOnAxis(
                        ap=slot[:, k, t:t + 1], axis=0), in_=h2[:, t, :], in_offset=None).then_inc(s_scat, 16)

            def store_y(e, par):
                pool.wait_ge(s_y, 2 * e + 2)
                pool.dma_start(Yd[bass.ds(e * C, C), :], y[:, par]).then_inc(s_yo[par], 16)

            with pool.Fori(0, NE // 2) as i:
                store_y(2 * i, 0)
                store_y(2 * i + 1, 1)
            with pool.If(over > 0):
                pl_.tensor_tensor(free_[0:1], ones1[0:1], ones1[0:1], ALU.add).then_inc(s_o_free, 1)
                with pool.Fori(0, NE * OV_TILES) as o:
                    pool.wait_ge(s_o_act, 3 * o + 6)
                    pool.dma_start(Yd[bass.ds(NE * C + o * P, P), :], y[:, 0]).then_inc(s_o_st, 16)
                    pool.wait_ge(s_o_st, 16 * o + 16)
                    pl_.tensor_tensor(free_[0:1], ones1[0:1], ones1[0:1], ALU.add).then_inc(s_o_free, 1)
            pool.wait_ge(s_yo[0], 16 * NE // 2)
            pool.wait_ge(s_yo[1], 16 * NE // 2)

            def gather(i, n_rows):
                if i >= 2 * NT:
                    return
                if i >= NYG:
                    pool.wait_ge(s_yu, i - NYG + 1)
                pool.indirect_dma_start(out=yg[:, i % NYG, :], out_offset=None, in_=Yd[0:n_rows, :],
                                        in_offset=bass.IndirectOffsetOnAxis(ap=slot[:, i % 2, i // 2:i // 2 + 1], axis=0)
                                        ).then_inc(s_yg[i % NYG], 16)

            def gather_all(n_rows):
                for i in range(NYG):
                    gather(i, n_rows)
                for t in range(NT):
                    gather(NYG + 2 * t, n_rows)
                    gather(NYG + 2 * t + 1, n_rows)
                    row_rms(2 * NT + t)

            at_step = step[0]
            with pool.If(over > 0):
                gather_all(NE * C + NE * OV_TILES * P)
            step[0] = at_step
            with pool.Else():
                gather_all(NE * C)

        @block.scalar
        def _(act):
            sc = nc.scalar
            hi = lambda u: split_hi(act, Unit(u))

            def square(i, out, wait_sem, value):
                act.wait_ge(wait_sem, value)
                if i % NT:
                    act.wait_ge(s_sq, i)
                sc.activation(out[:, :], x[:, i % NT], ACT.Square, accum_out=ss[:, i:i + 1]).then_inc(s_sq, 1)

            for t in range(NT):
                square(t, junk, s_x[t], 16)
                if t < RING:
                    hi(t)

            def norm_hi(g, t, half):
                act.wait_ge(s_tr, g + 1)
                sc.activation(hh[:, 4 * half:4 * half + 4, t * P:(t + 1) * P],
                              ring_bank(g)[:, :].rearrange("p (k t) -> p k t", k=4), ACT.Copy).then_inc(s_trh, 1)

            for t in range(NT):
                for half in range(2):
                    norm_hi(G_X + 2 * t + half, t, half)

            for c in range(3):
                for i in range(4, 7):
                    hi(4 * c + i)
                for t in range(NT):
                    n = c * NT + t
                    act.wait_ge(s_mm, 5 * (4 * c + 3) + t + 1)
                    if c < 2:
                        if n >= 2:
                            act.wait_ge(s_qn1, n - 1)
                        sc.activation(zb[:, n % 2], bank[t][:, :], ACT.Copy).then_inc(s_free, 1)
                    else:
                        act.wait_ge(s_trf, G_STATE + 1)
                        sc.activation(v[:, t], bank[t][:, :], ACT.Copy).then_inc(s_free, 1)
                hi(4 * c + 7)
            act.wait_ge(s_hn, NT)
            for j in range(KW):
                for h in range(2):
                    act.wait_ge(s_mm, Unit(U_CC + j).half(h))
                    sc.activation(ccT[:, j, half_rows(h)], bank[2 * (j % 2) + h][:, 0:HALF], ACT.Copy).then_inc(s_free, 1)
                hi(U_CC + KW + j)
            for j in range(KW):
                hi(U_CC + 2 * KW + j)
            for j in range(KW):
                split_hi(act, Unit(U_C + j), j % 2 == 1)
                act.wait_ge(s_free, F_CC + 4 * KW + 2 * j + 2)
                sc.activation(ch[:, j], ccT[:, j], ACT.Copy).then_inc(s_ch, 1)

            act.wait_ge(s_cl, KW)
            act.wait_ge(s_cpk, 1 + KW)
            act.wait_ge(s_ncvo, 32)
            for h in range(H + 1):
                if h < H:
                    tmp, zb3 = tmp1280[h % 2], bank[3 * (h % 2):3 * (h % 2) + 3]
                    act.wait_ge(s_z, h + 1)
                    if h >= 2:
                        act.wait_ge(s_spr, 3 * (h - 1))
                    for i, width in enumerate((512, 512, 256)):
                        sc.activation(tmp[:, 512 * i:512 * i + width], zb3[i][:, 0:width], ACT.Abs).then_inc(s_ln1, 1)
                    act.wait_ge(s_ln1, 5 * h + 3)
                    sc.activation(tmp[:, :], tmp[:, :], ACT.Exp, scale=-1.0).then_inc(s_ln1, 1)
                    act.wait_ge(s_ln1, 5 * h + 4)
                    sc.activation(tmp[:, :], tmp[:, :], ACT.Ln, bias=1.0).then_inc(s_ln1, 1)
                if h > 0:
                    a, zb3 = a1280[(h - 1) % 2], bank[3 * ((h - 1) % 2):3 * ((h - 1) % 2) + 3]
                    act.wait_ge(s_acc, h)
                    if h >= 3:
                        act.wait_ge(s_av, h - 2)
                    for i, width in enumerate((512, 512, 256)):
                        sc.activation(a[:, 512 * i:512 * i + width], zb3[i][:, 0:width], ACT.Exp).then_inc(s_ea, 1)
                if h in (3, 5, 7):
                    pair = (h - 3) // 2
                    act.wait_ge(s_av, 2 * pair + 2)
                    sc.activation(ah[:, pair, 0:TP], bank[6 + pair % 2][:, :], ACT.Copy).then_inc(s_ah, 1)
            act.wait_ge(s_av, H)
            sc.activation(ah[:, HP - 1, 0:TP], bank[6 + (HP - 1) % 2][:, :], ACT.Copy).then_inc(s_ah, 1)

            def keys_out(b, i):
                act.wait_ge(s_kt, 4 * b + 2 * i + 1)
                if not (is_zero(b) and i == 0):
                    act.wait_ge(s_zs, 2 * b + i)
                sc.activation(ktc[:, 0], bank[0][:, :].rearrange("p (h t) -> p h t", h=HP), ACT.Copy).then_inc(s_kta, 1)

            def logs(b, par):
                zs, zn = bank[2 + par][:, :], small[par][0:TS, 0:P]
                act.wait_ge(s_zs, 2 * b + 2)
                if not is_zero(b):
                    act.wait_ge(s_sps, 2 * b)
                sc.activation(tms[:], zs, ACT.Abs).then_inc(s_lns, 1)
                sc.activation(tmpn[:], zn, ACT.Abs).then_inc(s_lns, 1)
                act.wait_ge(s_lns, 6 * b + 2)
                sc.activation(tms[:], tms[:], ACT.Exp, scale=-1.0).then_inc(s_lns, 1)
                sc.activation(tmpn[:], tmpn[:], ACT.Exp, scale=-1.0).then_inc(s_lns, 1)
                act.wait_ge(s_lns, 6 * b + 4)
                sc.activation(tms[:], tms[:], ACT.Ln, bias=1.0).then_inc(s_lns, 1)
                sc.activation(tmpn[:], tmpn[:], ACT.Ln, bias=1.0).then_inc(s_lns, 1)

            def weights(b, par):
                act.wait_ge(s_accs, b + 1)
                if not is_zero(b):
                    act.wait_ge(s_avs, b)
                sc.activation(a_s[:], bank[2 + par][:, :], ACT.Exp).then_inc(s_eas, 1)
                sc.activation(an[:, :], small[par][0:TS, 0:P], ACT.Exp).then_inc(s_eas, 1)

            def gate(c, h):
                act.wait_ge(s_mm, gate_unit(c).half(h))
                if not is_zero(c):
                    act.wait_ge(s_br, 2 * number(c))
                sc.activation(sg[:, half_rows(h)], bank[5 + h][:, 0:HALF], ACT.Sigmoid).then_inc(s_gate, 1)

            def sequence(b, c, par):
                keys_out(b, 0)
                gate(c, 0)
                keys_out(b, 1)
                gate(c, 1)
                logs(b, par)
                if not is_zero(b):
                    weights(b - 1, 1 - par)
                split_hi(act, gate_unit(later(c, 2)))
                split_hi(act, gate_unit(later(c, 2)).plus(1), True)

            sequence(0, 0, 0)
            sequence(1, 1, 1)
            with act.Fori(1, 4) as i:
                sequence(2 * i, (i, 0), 0)
                sequence(2 * i + 1, (i, 1), 1)
            weights(B - 1, 1)
            gate(8, 0)
            act.wait_ge(s_af, 2 * B)
            sc.activation(ah[:, :, TP:T], af[:, :, :], ACT.Copy).then_inc(s_ah, 1)
            gate(8, 1)
            split_hi(act, gate_unit(10))
            split_hi(act, gate_unit(10).plus(1), True)

            def block_gates(c):
                gate(c, 0)
                gate(c, 1)
                split_hi(act, gate_unit(later(c, 2)))
                split_hi(act, gate_unit(later(c, 2)).plus(1), True)

            block_gates(9)
            with act.Fori(5, NB // 2 - 1) as i:
                block_gates((i, 0))
                block_gates((i, 1))

            def merged_hi(k):
                act.wait_ge(s_m, 2 * k + 2)
                sc.activation(hh[:, k], m[:, k], ACT.Copy).then_inc(s_mh, 1)

            for c in (NB - 2, NB - 1):
                gate(c, 0)
                gate(c, 1)
                hi(U_C + 2 * c + 4)
                if c == NB - 2:
                    hi(U_C + 2 * c + 5)
            for k in range(KD - 2):
                merged_hi(k)
            hi(U_D + 3)
            merged_hi(KD - 2)
            merged_hi(KD - 1)
            for n in range(2):
                u0 = U_D + 4 * n
                for i in range(4, 8):
                    hi(u0 + i)
                if n == 0:
                    for t in range(NT):
                        act.wait_ge(s_tr, G_PLE + t + 1)
                        sc.activation(ph[:, :, t * P:(t + 1) * P], ring_bank(G_PLE + t)[:, 0:2 * P].rearrange(
                            "p (k t) -> p k t", k=2), ACT.Copy).then_inc(s_trh, 1)
            for t in range(NT):
                square(NT + t, junk2, s_free, F_D + NT + t + 1)
            for n in range(2):
                for t in range(NT):
                    act.wait_ge(s_mm, 5 * (U_P + n) + t + 1)
                    sc.activation(pp[:, t, n * W:(n + 1) * W], bank[t][:, :], ACT.Copy).then_inc(s_free, 1)
                hi(U_P + n + 4)
                if n == 0:
                    act.wait_ge(s_d, 1)
                    sc.activation(gexp[:], gdiff[:], ACT.Exp).then_inc(s_rx, 1)
                    act.wait_ge(s_d, 2)
                    sc.activation(vexp[:], vdiff[:], ACT.Exp).then_inc(s_rx, 1)

            def rows_hi(e):
                for half in range(2):
                    act.wait_ge(s_xt, 2 * e + half + 1)
                    sc.activation(xh[:, 4 * half:4 * half + 4], bank[4 + half][:, :].rearrange("p (k t) -> p k t", k=4),
                                  ACT.Copy).then_inc(s_xh, 1)

            def silu(e, last_gate_unit):
                act.wait_ge(s_mm, last_gate_unit.mm())
                act.wait_ge(s_hm, e)
                sc.activation(si[:, :], bank[0][:, :], ACT.Silu).then_inc(s_si, 1)

            def hidden_hi(e):
                act.wait_ge(s_ht, e + 1)
                sc.activation(mh[:, :, :], bank[6][:, :].rearrange("p (k t) -> p k t", k=4), ACT.Copy).then_inc(s_hth, 1)

            def out_rows(n, e, par, turn, unit):
                act.wait_ge(s_mm, unit.mm())
                act.wait_ge(s_yo[par], 16 * turn)
                sc.activation(y[:, par, n * W:(n + 1) * W], bank[2 + n][:, :], ACT.Copy).then_inc(s_y, 1)

            rows_hi(0)
            for j in range(4, 8):
                hi(U_M + j)
            silu(0, Unit(U_M + 3))
            for j in range(8, 12):
                hi(U_M + j)
            rows_hi(1)

            def expert_scalar(e, par, turn, rows_next=True):
                u = lambda j: Unit(U_M - 4 + j, NSTREAM, e)
                for j in range(4, 8):
                    split_hi(act, u(j))
                hidden_hi(e - 1)
                silu(e, u(3))
                for j in range(8, 12):
                    split_hi(act, u(j))
                if rows_next:
                    rows_hi(e + 1)
                split_hi(act, u(12))
                split_hi(act, u(13))
                out_rows(0, e - 1, 1 - par, turn, u(9))
                split_hi(act, u(14))
                split_hi(act, u(15))
                out_rows(1, e - 1, 1 - par, turn, u(11))

            expert_scalar(1, 1, 0)
            expert_scalar(2, 0, 0)
            with act.Fori(1, NE // 2 - 1) as i:
                expert_scalar(2 * i + 1, 1, i)
                expert_scalar(2 * i + 2, 0, i)
            expert_scalar(NE - 1, 1, NE // 2 - 1, rows_next=False)
            hidden_hi(NE - 1)
            out_rows(0, NE - 1, 1, NE // 2 - 1, Unit(U_G - 3))
            out_rows(1, NE - 1, 1, NE // 2 - 1, Unit(U_G - 1))

            act.wait_ge(s_flag, 1)
            over = act.value_load(flag[0:1, 0:1], min_val=0, max_val=1)
            with act.If(over > 0):
                act.wait_ge(s_yo[0], 16 * NE // 2)
                act.wait_ge(s_hm, NE)
                sc.activation(si[:, 0:1], ss[:, 0:1], ACT.Copy).then_inc(s_o_act, 3)
                act.wait_ge(s_o_act, 3)
                with act.Fori(0, NE * OV_TILES) as o:
                    act.wait_ge(s_o_pe, 14 * o + 5)
                    sc.activation(si[:, :], bank[0][:, :], ACT.Silu).then_inc(s_o_act, 1)
                    act.wait_ge(s_o_free, o + 1)
                    for n in range(2):
                        act.wait_ge(s_o_pe, 14 * o + 12 + 2 * n)
                        sc.activation(y[:, 0, n * W:(n + 1) * W], bank[2 + n][:, :], ACT.Copy).then_inc(s_o_act, 1)

            for i in range(4):
                hi(U_G + i)
            for t in range(NT):
                square(2 * NT + t, junk2, s_yu, 2 * t + 2)
                for half in range(2):
                    norm_hi(G_F + 2 * t + half, t, half)
            for n in range(2):
                if n == 0:
                    for i in range(4, 7):
                        hi(U_G + i)
                for t in range(NT):
                    i = n * NT + t
                    act.wait_ge(s_mm, 5 * (U_G + 4 * n + 3) + t + 1)
                    if i >= 4:
                        act.wait_ge(s_out[i % 4], 16 * (i // 4))
                    sc.activation(eo[:, i % 4], bank[t][:, :], ACT.Sigmoid).then_inc(s_free, 1)
                if n == 0:
                    hi(U_G + 7)

        @block.vector
        def _(dve):
            ve = nc.vector
            lo = lambda u: split_lo(dve, Unit(u))
            step = [0]

            def link(ins):
                step[0] += 1
                ins.then_inc(s_vc, 1)
                dve.wait_ge(s_vc, step[0])

            def tt(out, a, b, op):
                return ve.tensor_tensor(out=out, in0=a, in1=b, op=op)

            def norm_rows(i, out):
                dve.wait_ge(s_r, i + 1)
                return ve.scalar_tensor_tensor(out=out, in0=x[:, i % NT], scalar=rr[:, i:i + 1], in1=lnb[:, :],
                                               op0=ALU.mult, op1=ALU.mult)

            def norm_lo(g, t, half):
                dve.wait_ge(s_trh, trh(g))
                dst = (slice(4 * half, 4 * half + 4), slice(t * P, (t + 1) * P))
                tt(hl[:, dst[0], dst[1]], ring_bank(g)[:, :].rearrange("p (k t) -> p k t", k=4),
                   hh[:, dst[0], dst[1]].bitcast(F32), ALU.subtract).then_inc(s_trf, 1)

            def trh(g):
                return g + 1 if g < 10 else 10 + g - G_PLE + 1 if g < G_R else 15 + g - G_F + 1

            dve.wait_ge(s_ln, 16)
            for t in range(NT):
                if t >= 2:
                    dve.wait_ge(s_tr, 2 * (t - 2) + 2)
                norm_rows(t, hn[:, t % 2]).then_inc(s_hn, 1)
                if t < RING:
                    lo(t)
                if t >= 1:
                    norm_lo(2 * t - 2, t - 1, 0)
                    norm_lo(2 * t - 1, t - 1, 1)
            norm_lo(8, 4, 0)
            norm_lo(9, 4, 1)
            dve.wait_ge(s_sq, NT)
            dve.wait_ge(s_tr, G_STATE + 1)
            ve.tensor_copy(us[:, :, :, 0:2], ring_bank(G_STATE)[:, 0:KW * 2 * B].rearrange(
                "p (j b s) -> p j b s", j=KW, s=2)).then_inc(s_trf, 1)

            def head_sums(n):
                dve.wait_ge(s_qsq, n + 1)
                ve.tensor_reduce(out=ssq[:, n], in_=sqb[:, 0].rearrange("p (h d) -> p h d", h=H), axis=AX.X,
                                 op=ALU.add).then_inc(s_ssq, 1)
                dve.wait_ge(s_rq, n + 1)
                if n:
                    dve.wait_ge(s_qn2, n)
                tt(qn1[:, 0].rearrange("p (h d) -> p h d", h=H), zb[:, n % 2].rearrange("p (h d) -> p h d", h=H),
                   rq[:, n, :, None].to_broadcast([P, H, HD]), ALU.mult).then_inc(s_qn1, 1)

            def head_normed(n):
                if n >= 2:
                    dve.wait_ge(s_tr, G_QK + n - 1)
                if n >= NT + 2:
                    dve.wait_ge(s_ko[n % 2], 16 * ((n - NT) // 2))
                dve.wait_ge(s_qn1, n + 1)
                tt(qn2[:, n % 2].rearrange("p (h d) -> p h d", h=H), qn1[:, 0].rearrange("p (h d) -> p h d", h=H),
                   qkg[:, n // NT, None, :].to_broadcast([P, H, HD]), ALU.mult).then_inc(s_qn2, 1)

            def qk_out(n):
                g = G_QK + n
                dve.wait_ge(s_tr, g + 1)
                dst = (qT if n < NT else kT)[:, :, (n % NT) * P:(n % NT + 1) * P]
                ve.tensor_copy(dst, ring_bank(g)[:, :].rearrange("p (j t) -> p j t", j=KW)).then_inc(s_trf, 1)

            for c in range(3):
                for i in range(4, 7):
                    lo(4 * c + i)
                if c < 2:
                    n = c * NT
                    if c == 1:
                        qk_out(n - 2)
                        qk_out(n - 1)
                    head_sums(n)
                    head_normed(n)
                    head_sums(n + 1)
                    head_normed(n + 1)
                    head_sums(n + 2)
                    lo(4 * c + 7)
                    qk_out(n)
                    head_normed(n + 2)
                    head_sums(n + 3)
                    qk_out(n + 1)
                    head_normed(n + 3)
                    head_sums(n + 4)
                    qk_out(n + 2)
                    head_normed(n + 4)
                else:
                    qk_out(8)
                    qk_out(9)
                    lo(4 * c + 7)

            def conv(j):
                outs = (yc[:, j, 0:TP], yc[:, j, TP:T].rearrange("p (b s) -> p b s", b=B))
                ins_ = (lambda s: up[:, j, s:s + TP], lambda s: us[:, j, :, s:s + TS])
                for s in range(3):
                    for n in range(2):
                        if s == 0:
                            ins = ve.tensor_scalar(outs[n], ins_[n](0), convw[:, 0, j:j + 1], None, ALU.mult)
                        else:
                            ins = ve.scalar_tensor_tensor(out=outs[n], in0=ins_[n](s), scalar=convw[:, s, j:j + 1],
                                                          in1=outs[n], op0=ALU.mult, op1=ALU.add)
                    link(ins)

            for j in range(KW):
                lo(U_CC + KW + j)
            dve.wait_ge(s_free, F_CC + 2 * KW)
            dve.wait_ge(s_made, 15)
            dve.wait_ge(s_const, 16 * 9)
            for j in range(KW):
                u = Unit(U_CC + KW + j)
                b0, b1 = bank[2 * (j % 2)], bank[2 * (j % 2) + 1]
                dve.wait_ge(s_mm, u.half(0))
                tt(up[:, j, 2:2 + HALF], b0[:, 0:HALF], ccT[:, j, 0:HALF], ALU.mult).then_inc(s_free, 1)
                dve.wait_ge(s_mm, u.half(1))
                tt(up[:, j, 2 + HALF:2 + TP], b1[:, 0:TP - HALF], ccT[:, j, HALF:TP], ALU.mult)
                tt(us[:, j, :, 2:2 + TS], b1[:, TP - HALF:HALF].rearrange("p (b s) -> p b s", b=B),
                   ccT[:, j, TP:T].rearrange("p (b s) -> p b s", b=B), ALU.mult).then_inc(s_free, 1)
                dve.wait_ge(s_free, F_CC + 2 * KW + 2 * j + 2)
                conv(j)
                lo(U_CC + 2 * KW + j)

            def conv_lo(j):
                dve.wait_ge(s_ch, j + 1)
                tt(cl[:, j], ccT[:, j], ch[:, j].bitcast(F32), ALU.subtract).then_inc(s_cl, 1)

            for j in range(KW):
                for h in range(2):
                    dve.wait_ge(s_mm, Unit(U_CC + 2 * KW + j).half(h))
                    tt(ccT[:, j, half_rows(h)], bank[2 * (j % 2) + h][:, 0:HALF], yc[:, j, half_rows(h)], ALU.mult
                       ).then_inc(s_free, 1)
                split_lo(dve, Unit(U_C + j), j % 2 == 1)
                conv_lo(j)
            dve.wait_ge(s_tr, G_CONV + 1)
            ve.tensor_copy(ncv[:, :], ring_bank(G_CONV)[0:2 + 2 * B, :]).then_inc(s_trf, 1)

            dve.wait_ge(s_cl, KW)
            for h in range(H):
                tmp, out, zb3 = tmp1280[h % 2], sp1280[h % 2], bank[3 * (h % 2):3 * (h % 2) + 3]
                dve.wait_ge(s_ln1, 5 * h + 5)
                if h >= 2:
                    dve.wait_ge(s_acc, h - 1)
                for i, width in enumerate((512, 512, 256)):
                    ve.scalar_tensor_tensor(out=out[:, 512 * i:512 * i + width], in0=zb3[i][:, 0:width], scalar=0.0,
                                            in1=tmp[:, 512 * i:512 * i + width], op0=ALU.max, op1=ALU.add
                                            ).then_inc(s_spr, 1)
                if h in (3, 5, 7):
                    pair = (h - 3) // 2
                    dve.wait_ge(s_ah, pair + 1)
                    tt(al[:, pair, 0:TP], bank[6 + pair % 2][:, :], ah[:, pair, 0:TP].bitcast(F32), ALU.subtract
                       ).then_inc(s_al, 1)
            dve.wait_ge(s_ah, HP)
            tt(al[:, HP - 1, 0:TP], bank[6 + (HP - 1) % 2][:, :], ah[:, HP - 1, 0:TP].bitcast(F32), ALU.subtract
               ).then_inc(s_al, 1)

            def keys_out(b, i):
                dve.wait_ge(s_kt, 4 * b + 2 * i + 2)
                if not (is_zero(b) and i == 0):
                    dve.wait_ge(s_zs, 2 * b + i)
                ve.tensor_copy(ktc[:, 1], bank[1][:, :].rearrange("p (h t) -> p h t", h=HP)).then_inc(s_ktv, 1)

            def softplus(b, par):
                dve.wait_ge(s_lns, 6 * b + 6)
                if not is_zero(b):
                    dve.wait_ge(s_accs, b)
                for out, z, tmp in ((sps, bank[2 + par][:, :], tms), (spn, small[par][0:TS, 0:P], tmpn)):
                    ve.scalar_tensor_tensor(out=out[:], in0=z, scalar=0.0, in1=tmp[:], op0=ALU.max, op1=ALU.add
                                            ).then_inc(s_sps, 1)

            def keep(b, par):
                dve.wait_ge(s_avs, b + 1)
                o = small[par][:, P:2 * P].rearrange("p (h q) -> p h q", h=HP)
                ve.tensor_copy(af[0:HD, :, bass.ds(b * TS, TS)], o[0:HD, :, 0:TS]).then_inc(s_af, 1)
                ve.tensor_copy(af[HD:P, :, bass.ds(b * TS, TS)], o[HD:P, :, TS:]).then_inc(s_af, 1)

            def gated(c, h, out):
                dve.wait_ge(s_gate, 2 * number(c) + 2)
                dve.wait_ge(s_mm, gate_unit(c).plus(1).half(h))
                tt(out, bank[5 + h][:, 0:HALF], sg[:, half_rows(h)], ALU.mult).then_inc(s_br, 1)

            dve.wait_ge(s_av, H)
            ve.tensor_copy(qs[:], qT[:, :, TP:T]).then_inc(s_qs, 1)
            ve.tensor_copy(ks[:], kT[:, :, TP:T]).then_inc(s_qs, 1)
            dve.wait_ge(s_qs, 2)

            def place(b, par):
                if not isinstance(b, int):
                    dve.wait_ge(s_accs, b - 1)
                q_b = qs[:, :, bass.ds(b * TS, TS)]
                ve.tensor_copy(qbd[0:HD, par, :, 0:TS], q_b[0:HD]).then_inc(s_qb, 1)
                ve.tensor_copy(qbd[HD:P, par, :, TS:], q_b[HD:P]).then_inc(s_qb, 1)
                ve.tensor_copy(ktb[:, par], ks[:, :, bass.ds(b * TS, TS)]).then_inc(s_qb, 1)

            def sequence(b, c, par):
                place(b, par)
                keys_out(b, 0)
                keys_out(b, 1)
                softplus(b, par)
                split_lo(dve, gate_unit(later(c, 2)))
                for h in range(2):
                    gated(c, h, m[:, bass.ds(number(c), 1), half_rows(h)].rearrange("p o t -> p (o t)"))
                split_lo(dve, gate_unit(later(c, 2)).plus(1), True)
                if not is_zero(b):
                    keep(b - 1, 1 - par)

            sequence(0, 0, 0)
            sequence(1, 1, 1)
            with dve.Fori(1, 4) as i:
                sequence(2 * i, (i, 0), 0)
                sequence(2 * i + 1, (i, 1), 1)
            keep(B - 1, 1)
            dve.wait_ge(s_ah, HP + 1)
            tt(al[:, :, TP:T], af[:, :, :], ah[:, :, TP:T].bitcast(F32), ALU.subtract).then_inc(s_al, 1)

            def merged(c):
                if not (isinstance(c, int) and c == KD):
                    dve.wait_ge(s_m, 2 * number(c) - 2 * KD)
                for h in range(2):
                    gated(c, h, mt[:, half_rows(h)])
                for h in range(2):
                    dve.wait_ge(s_br, 2 * number(c) + h + 1)
                    out = m[:, bass.ds(number(c) - KD, 1), half_rows(h)].rearrange("p o t -> p (o t)")
                    tt(out, out, mt[:, half_rows(h)], ALU.add).then_inc(s_m, 1)

            def merged_block(c):
                split_lo(dve, gate_unit(later(c, 2)))
                merged(c)
                split_lo(dve, gate_unit(later(c, 2)).plus(1), True)

            def merged_lo(k):
                dve.wait_ge(s_mh, k + 1)
                tt(hl[:, k], m[:, k], hh[:, k].bitcast(F32), ALU.subtract).then_inc(s_ml, 1)

            merged_block(8)
            merged_block(9)
            with dve.Fori(5, NB // 2 - 1) as i:
                merged_block((i, 0))
                merged_block((i, 1))
            lo(U_D)
            merged(NB - 2)
            lo(U_D + 1)
            lo(U_D + 2)
            for k in range(2):
                merged_lo(k)
            merged(NB - 1)
            for k in range(2, KD - 2):
                merged_lo(k)
            lo(U_D + 3)
            merged_lo(KD - 2)
            merged_lo(KD - 1)

            for n in range(2):
                u0 = U_D + 4 * n
                for i in range(4, 7):
                    lo(u0 + i)
                dve.wait_ge(s_xr, 16 * NT)
                for t in range(NT):
                    dve.wait_ge(s_mm, 5 * (u0 + 3) + t + 1)
                    tt(x[:, t, n * W:(n + 1) * W], x[:, t, n * W:(n + 1) * W], bank[t][:, :], ALU.add).then_inc(s_free, 1)
                lo(u0 + 7)
                if n == 0:
                    for t in range(NT):
                        g = G_PLE + t
                        dve.wait_ge(s_trh, trh(g))
                        tt(pl[:, :, t * P:(t + 1) * P], ring_bank(g)[:, 0:2 * P].rearrange("p (k t) -> p k t", k=2),
                           ph[:, :, t * P:(t + 1) * P].bitcast(F32), ALU.subtract).then_inc(s_trf, 1)

            def h2_out(t):
                for half in range(2):
                    g = G_R + 2 * t + half
                    dve.wait_ge(s_tr, g + 1)
                    ve.tensor_copy(h2T[:, 4 * half:4 * half + 4, t * P:(t + 1) * P],
                                   ring_bank(g)[:, :].rearrange("p (k t) -> p k t", k=4)).then_inc(s_trf, 1)

            dve.wait_ge(s_ln, 32)
            for t in range(NT):
                norm_rows(NT + t, h2[:, t]).then_inc(s_hn, 1)
                if t:
                    h2_out(t - 1)
            h2_out(NT - 1)

            def bc(a, n):
                return a[:, :, None].to_broadcast([P, NT, n])

            def top(logits, vmax, choice):
                link(ve.tensor_reduce(out=vmax[:], in_=logits, axis=AX.X, op=ALU.max))
                link(tt(cand[:], logits, bc(vmax, 4), ALU.is_ge))
                link(tt(cand[:], cand[:], desc[:, None, :].to_broadcast([P, NT, 4]), ALU.mult))
                link(ve.tensor_reduce(out=cm1[:], in_=cand[:], axis=AX.X, op=ALU.max))
                link(tt(choice, cand[:], bc(cm1, 4), ALU.is_equal))

            dve.wait_ge(s_rt, 1)
            link(tt(lg[:], bank[6][:, 0:NT * (NG + NE)].rearrange("p (t n) -> p t n", t=NT),
                    rbias[:, None, :].to_broadcast([P, NT, NG + NE]), ALU.add))
            top(lg[:, :, 0:NG], gmax, og[:])
            tt(gdiff[:], lg[:, :, 0:NG], bc(gmax, NG), ALU.subtract).then_inc(s_d, 1)
            link(tt(prod[:], lg[:, :, NG:].rearrange("p t (g j) -> p t j g", g=NG),
                    og[:, :, None, :].to_broadcast([P, NT, EG, NG]), ALU.mult))
            link(ve.tensor_reduce(out=lsel[:], in_=prod[:], axis=AX.X, op=ALU.add))
            top(lsel[:], v1, ok[:, 0])
            link(ve.scalar_tensor_tensor(out=lsel2[:], in0=ok[:, 0], scalar=-3.0e38, in1=lsel[:], op0=ALU.mult,
                                         op1=ALU.add))
            top(lsel2[:], v2, ok[:, 1])
            tt(vdiff[:], v2[:], v1[:], ALU.subtract).then_inc(s_d, 1)
            for k in range(2):
                ins = tt(Mk[:, k].rearrange("p t (g j) -> p t g j", g=NG), og[:, :, :, None].to_broadcast([P, NT, NG, EG]),
                         ok[:, k, :, None, :].to_broadcast([P, NT, NG, EG]), ALU.mult)
            link(ins)
            tt(Mb[:], Mk[:, 0], Mk[:, 1], ALU.add).then_inc(s_M, 1)
            dve.wait_ge(s_rx, 2)
            ve.tensor_reduce(out=gsum[:], in_=gexp[:], axis=AX.X, op=ALU.add)
            link(ve.tensor_scalar(vsum[:], vexp[:], 1.0, None, ALU.add))
            link(tt(gsum[:], gsum[:], vsum[:], ALU.mult))
            link(ve.reciprocal(gate[:, 0], gsum[:]))
            link(tt(gate[:, 1], gate[:, 0], vexp[:], ALU.mult))
            dve.wait_ge(s_rk, 1)
            link(ve.tensor_copy(rk[:], bank[6][:, P:P + NT * NE].rearrange("p (t e) -> p t e", t=NT)))
            for k in range(2):
                ins = tt(mr[:, k], Mk[:, k], rk[:], ALU.mult)
            link(ins)
            link(ve.tensor_reduce(out=slotf[:, 0], in_=mr[:], axis=AX.X, op=ALU.add))
            link(tt(mr[:].rearrange("p k t e -> p (k t) e"), Mk[:].rearrange("p k t e -> p (k t) e"),
                    eidx[:, None, :].to_broadcast([P, 2 * NT, NE]), ALU.mult))
            link(ve.tensor_reduce(out=slotf[:, 1], in_=mr[:], axis=AX.X, op=ALU.add))
            link(ve.tensor_scalar(slotf[:, 2], slotf[:, 0], float(C), None, ALU.is_ge))
            ve.tensor_reduce(out=ovm[:], in_=slotf[:, 2], axis=AX.XY, op=ALU.max).then_inc(s_ovm, 1)
            link(ve.tensor_scalar(slotf[:, 3], slotf[:, 1], float(T - 2 * C), float((NE - 1) * C), ALU.mult, ALU.add))
            link(tt(slotf[:, 3], slotf[:, 3], slotf[:, 2], ALU.mult))
            link(ve.scalar_tensor_tensor(out=slotf[:, 0], in0=slotf[:, 1], scalar=float(C), in1=slotf[:, 0],
                                         op0=ALU.mult, op1=ALU.add))
            tt(slot[:], slotf[:, 0], slotf[:, 3], ALU.add).then_inc(s_slot, 1)
            dve.wait_ge(s_ov, 1)
            ve.tensor_scalar(flag[0:1, 0:1], bank[7][0:1, 0:1], 1.0, None, ALU.min).then_inc(s_flag, 1)
            lo(U_M + 2)
            lo(U_M + 3)

            def rows_lo(e):
                for half in range(2):
                    dve.wait_ge(s_xh, 2 * e + half + 1)
                    tt(xl[:, 4 * half:4 * half + 4], bank[4 + half][:, :].rearrange("p (k t) -> p k t", k=4),
                       xh[:, 4 * half:4 * half + 4].bitcast(F32), ALU.subtract).then_inc(s_xl, 1)

            def hidden(e, last_up_unit):
                dve.wait_ge(s_mm, last_up_unit.mm())
                dve.wait_ge(s_si, e + 1)
                dve.wait_ge(s_ht, e)
                tt(hm[:, :], bank[1][:, :], si[:, :], ALU.mult).then_inc(s_hm, 1)

            def hidden_lo(e):
                dve.wait_ge(s_hth, e + 1)
                tt(ml[:, :, :], bank[6][:, :].rearrange("p (k t) -> p k t", k=4), mh[:, :, :].bitcast(F32),
                   ALU.subtract).then_inc(s_htl, 1)

            rows_lo(0)
            for j in range(4, 11):
                lo(U_M + j)
            hidden(0, Unit(U_M + 7))
            lo(U_M + 11)
            rows_lo(1)

            def expert_vector(e, rows_next=True):
                u = lambda j: Unit(U_M - 4 + j, NSTREAM, e)
                for j in range(4, 8):
                    split_lo(dve, u(j))
                hidden_lo(e - 1)
                for j in range(8, 11):
                    split_lo(dve, u(j))
                hidden(e, u(7))
                split_lo(dve, u(11))
                if rows_next:
                    rows_lo(e + 1)
                for j in range(12, 16):
                    split_lo(dve, u(j))

            with dve.Fori(1, NE - 1) as e:
                expert_vector(e)
            expert_vector(NE - 1, rows_next=False)
            hidden_lo(NE - 1)

            dve.wait_ge(s_flag, 1)
            over = dve.value_load(flag[0:1, 0:1], min_val=0, max_val=1)
            with dve.If(over > 0):
                ve.memset(cm1[:], 0.0).then_inc(s_o_dve, 3)
                with dve.Fori(0, NE * OV_TILES) as o:
                    dve.wait_ge(s_o_pe, 14 * o + 1)
                    for half in range(2):
                        ins = ve.tensor_copy(oxT[:, 4 * half:4 * half + 4],
                                             bank[4 + half][:, :].rearrange("p (k t) -> p k t", k=4))
                    ins.then_inc(s_o_dve, 1)
                    dve.wait_ge(s_o_pe, 14 * o + 9)
                    dve.wait_ge(s_o_act, 3 * o + 4)
                    tt(hm[:, :], bank[1][:, :], si[:, :], ALU.mult).then_inc(s_o_dve, 1)
                    dve.wait_ge(s_o_pe, 14 * o + 10)
                    ve.tensor_copy(omT[:, :, :], bank[6][:, :].rearrange("p (k t) -> p k t", k=4)).then_inc(s_o_dve, 1)

            for i in range(4):
                lo(U_G + i)
            dve.wait_ge(s_ln, 48)
            for t in range(NT):
                for k in range(2):
                    i = 2 * t + k
                    dve.wait_ge(s_yg[i % NYG], 16 * (i // NYG + 1))
                    dve.wait_ge(s_yu, i)
                    ve.scalar_tensor_tensor(out=x[:, t], in0=yg[:, i % NYG], scalar=gate[:, k, t:t + 1], in1=x[:, t],
                                            op0=ALU.mult, op1=ALU.add).then_inc(s_yu, 1)
                if t >= 2:
                    dve.wait_ge(s_tr, G_F + 2 * (t - 2) + 2)
                norm_rows(2 * NT + t, hn3[:, t % 2]).then_inc(s_hn, 1)
                if t:
                    for half in range(2):
                        norm_lo(G_F + 2 * (t - 1) + half, t - 1, half)
            for half in range(2):
                norm_lo(G_F + 2 * (NT - 1) + half, NT - 1, half)
            for n in range(2):
                if n == 0:
                    for i in range(4, 7):
                        lo(U_G + i)
                for t in range(NT):
                    i = n * NT + t
                    cols = slice(n * W, (n + 1) * W)
                    dve.wait_ge(s_free, F_G + i + 1)
                    link(tt(eo[:, i % 4], eo[:, i % 4], pp[:, t, cols], ALU.mult))
                    tt(eo[:, i % 4], eo[:, i % 4], x[:, t, cols], ALU.add).then_inc(s_eo, 1)
                if n == 0:
                    lo(U_G + 7)

        @block.tensor
        def _(pe):
            def tr(g, pairs):
                if g >= 3:
                    pe.wait_ge(s_trf, g - 2)
                for out, src, idn in pairs:
                    ins = pe.transpose(out, src, idn)
                ins.then_inc(s_tr, 1)

            def tr_rows(g, src, n=4):
                tr(g, [(ring_bank(g)[:, q * P:(q + 1) * P], src[:, q * P:(q + 1) * P], ident[:, :]) for q in range(n)])

            def natural(u0, nu, free, a_hi, a_lo, before_unit=None, before_tile=None):
                for i in range(nu):
                    u = Unit(u0 + i)
                    pe.wait_ge(s_lo, u.count())
                    if before_unit:
                        before_unit(i)
                    for t in range(NT):
                        if i == 0 and free > 0:
                            pe.wait_ge(s_free, free - NT + t + 1)
                        if before_tile:
                            before_tile(i, t)
                        for kk in range(2):
                            k = 2 * i + kk
                            a = (slice(0, P), k, slice(t * P, (t + 1) * P))
                            ins = three(pe, bank[t][:, :], a_hi[a], a_lo[a], whi[:, u.slot, kk], wlo[:, u.slot, kk],
                                        i == 0 and kk == 0, i == nu - 1 and kk == 1)
                        ins.then_inc(s_mm, 1)

            def by_column(u, nk, b_hi, b_lo, h, out):
                pe.wait_ge(s_lo, u.count())
                for k in range(nk):
                    ins = three(pe, out[:, 0:HALF], columns(whi, u)[:, k], columns(wlo, u)[:, k],
                                b_hi[:, k, half_rows(h)], b_lo[:, k, half_rows(h)], k == 0, k == nk - 1)
                ins.then_inc(s_mm, 2 + h)

            def gate_half(c, h):
                if not is_zero(c):
                    pe.wait_ge(s_br, 2 * number(c) + h - 1)
                by_column(gate_unit(c), KD, hh, hl, h, bank[5 + h])

            def branch(c, b_hi, b_lo):
                for h in range(2):
                    pe.wait_ge(s_gate, 2 * number(c) + h + 1)
                    by_column(gate_unit(c).plus(1), KW, b_hi, b_lo, h, bank[5 + h])

            def x_rows(t):
                pe.wait_ge(s_hn, t + 1)
                for half in range(2):
                    tr_rows(G_X + 2 * t + half, hn[:, t % 2, half * W:(half + 1) * W])

            pe.wait_ge(s_made, 14)
            x_rows(0)

            def q_tile(i, t):
                if i == 0:
                    if t + 1 < NT:
                        x_rows(t + 1)
                    pe.wait_ge(s_trf, 2 * t + 2)

            natural(0, 4, 0, hh, hl, before_tile=q_tile)
            pe.wait_ge(s_state, 16)
            tr(G_STATE, [(ring_bank(G_STATE)[:, j * 2 * B:(j + 1) * 2 * B], st[:, j * P:(j + 1) * P],
                          ident[0:2 * B, 0:2 * B]) for j in range(KW)])

            def qk_rows(first):
                def before(i, t):
                    if t == 0 and i >= 2:
                        for n in ((0, 1), (2, 3))[i - 2]:
                            pe.wait_ge(s_qn2, first + n + 1)
                            tr_rows(G_QK + first + n, qn2[:, (first + n) % 2])
                return before

            def qk_last(first):
                pe.wait_ge(s_qn2, first + NT)
                tr_rows(G_QK + first + NT - 1, qn2[:, (first + NT - 1) % 2])

            natural(4, 4, NT, hh, hl, before_tile=qk_rows(0))
            qk_last(0)
            natural(8, 4, 2 * NT, hh, hl, before_tile=qk_rows(NT))
            qk_last(NT)
            with pe.Fori(0, 3) as c:
                for j in range(KW):
                    for h in range(2):
                        pe.wait_ge(s_free, 2 * KW * c + F_CC + 2 * j + h - 3)
                        by_column(Unit(U_CC + j, KW, c), KD, hh, hl, h, bank[2 * (j % 2) + h])
            pe.wait_ge(s_cpk, 1 + KW)
            tr(G_CONV, [(ring_bank(G_CONV)[0:2 + 2 * B, j * P:(j + 1) * P], cpk[:, j], ident[:, :]) for j in range(KW)])

            region = {0: (0, 0), 1: (1, 0), 2: (2, 0), 3: (1, 384)}
            off = {0: 0, 1: 512, 2: 1024, 3: 896}
            width = [TP - i * P for i in range(4)]

            def zreg(h, i, skip=0):
                bk, o = region[i]
                return bank[3 * (h % 2) + bk][:, o + skip:o + width[i]]

            def scores(h):
                r = HD * (h % 2)
                if h >= 2:
                    pe.wait_ge(s_ea, 3 * (h - 1))
                for i in (0, 1, 3, 2):
                    ins = pe.matmul(zreg(h, i), kT[r:r + HD, h // 2, i * P:(i + 1) * P],
                                    qT[r:r + HD, h // 2, i * P:TP], start=i != 3, stop=False, skip_group_check=True)
                ins.then_inc(s_z, 1)

            def log_sums(h):
                t = sp1280[h % 2]
                pe.wait_ge(s_sp, 4 * h + 4)
                for i in range(4):
                    ins = pe.matmul(zreg(h, i), um[:, :], t[:, off[i]:off[i] + width[i]], start=False, stop=False,
                                    skip_group_check=True)
                    for later in range(i + 1, 4):
                        ins = pe.matmul(zreg(h, i, (later - i) * P), neg[:, :], t[:, off[later]:off[later] + width[later]],
                                        start=False, stop=later == 3, skip_group_check=True)
                ins.then_inc(s_acc, 1)

            def values(h):
                r, pair = HD * (h % 2), h // 2
                pe.wait_ge(s_am, 4 * h + 4)
                if pair >= 2:
                    pe.wait_ge(s_al, pair - 1)
                for i in range(4):
                    ins = pe.matmul(bank[6 + pair % 2][r:r + HD, i * P:TP], v[:, i, h * HD:(h + 1) * HD],
                                    a1280[h % 2][:, off[i]:off[i] + width[i]], start=i == 0, stop=i == 3,
                                    skip_group_check=True)
                ins.then_inc(s_av, 1)

            pe.wait_ge(s_trf, G_CONV + 1)
            pe.wait_ge(s_free, F_D)
            scores(0)
            for h in range(H):
                if h + 1 < H:
                    scores(h + 1)
                log_sums(h)
                if h:
                    values(h - 1)
            values(H - 1)

            def keys(b, i):
                pe.wait_ge(s_kc[i], 16 * b + 16)
                if not (is_zero(b) and i == 0):
                    pe.wait_ge(s_kta, 2 * b + i)
                    pe.wait_ge(s_ktv, 2 * b + i)
                for kb in range(2):
                    for hp in range(HP):
                        ins = pe.transpose(bank[kb][:, hp * P:(hp + 1) * P], kc[:, 2 * i + kb, hp * P:(hp + 1) * P],
                                           ident[:, :])
                    ins.then_inc(s_kt, 1)

            def scores_of(b, i, par):
                pe.wait_ge(s_kta, 2 * b + i + 1)
                pe.wait_ge(s_ktv, 2 * b + i + 1)
                if i == 0:
                    pe.wait_ge(s_qb, 3 * b + 3)
                    if not isinstance(b, int):
                        pe.wait_ge(s_eas, 2 * b - 2)
                for kb in range(2):
                    for hp in range(HP):
                        o = (2 * i + kb) * P + hp * 2 * TS
                        ins = pe.matmul(bank[2 + par][:, o:o + 2 * TS], ktc[:, kb, hp],
                                        qbd[:, par, hp],
                                        start=i == 0 and kb == 0 and hp == 0, stop=False, skip_group_check=True)
                if i == 1:
                    if not isinstance(b, int):
                        pe.wait_ge(s_af, 2 * b - 2)
                    for hp in range(HP):
                        ins = pe.matmul(small[par][0:TS, hp * 2 * TS:(hp + 1) * 2 * TS], ktb[:, par, hp],
                                        qbd[:, par, hp], start=hp == 0, stop=False, skip_group_check=True)
                ins.then_inc(s_zs, 1)

            def log_terms(b, par):
                pe.wait_ge(s_spn, b + 1)
                z = bank[2 + par]
                pe.matmul(z[:, :], um[:, :], sps[:, :], start=False, stop=False, skip_group_check=True)
                for kb in range(1, KB):
                    pe.matmul(z[:, 0:kb * P], neg[:, :], sps[:, None, kb * P:(kb + 1) * P].to_broadcast([P, kb, P]),
                              start=False, stop=False, skip_group_check=True)
                pe.matmul(z[:, :], neg[0:TS, :], spn[:, None, :].to_broadcast([TS, KB, P]), start=False, stop=True,
                          skip_group_check=True)
                pe.matmul(small[par][0:TS, 0:P], um[0:TS, 0:TS], spn[:, :], start=False, stop=True,
                          skip_group_check=True).then_inc(s_accs, 1)

            def sample_values(b, par):
                pe.wait_ge(s_eas, 2 * b + 2)
                pe.wait_ge(s_ams, b + 1)
                pe.wait_ge(s_vcl, 32 * b + 32)
                for hp in range(HP):
                    out = small[par][:, P + hp * 2 * TS:P + (hp + 1) * 2 * TS]
                    for kb in range(KB):
                        pe.matmul(out, vc[:, kb, hp * P:(hp + 1) * P],
                                  a_s[:, kb * P + hp * 2 * TS:kb * P + (hp + 1) * 2 * TS],
                                  start=kb == 0, stop=False, skip_group_check=True)
                    ins = pe.matmul(out, vn[:, hp * P:(hp + 1) * P], an[:, hp * 2 * TS:(hp + 1) * 2 * TS],
                                    start=False, stop=True, skip_group_check=True)
                ins.then_inc(s_avs, 1)

            def sequence(b, c, par):
                keys(b, 0)
                gate_half(c, 0)
                scores_of(b, 0, par)
                keys(b, 1)
                gate_half(c, 1)
                scores_of(b, 1, par)
                if not is_zero(b):
                    log_terms(b - 1, 1 - par)
                branch(c, ch, cl)
                if not is_zero(b):
                    sample_values(b - 1, 1 - par)

            pe.wait_ge(s_al, HP)
            pe.wait_ge(s_cl, KW)
            sequence(0, 0, 0)
            sequence(1, 1, 1)
            with pe.Fori(1, 4) as i:
                sequence(2 * i, (i, 0), 0)
                sequence(2 * i + 1, (i, 1), 1)
            log_terms(B - 1, 1)

            gate_half(8, 0)
            sample_values(B - 1, 1)
            gate_half(8, 1)
            pe.wait_ge(s_al, HP + 1)
            branch(8, ah, al)
            gate_half(9, 0)
            gate_half(9, 1)
            branch(9, ah, al)
            with pe.Fori(5, NB // 2) as i:
                for n in range(2):
                    gate_half((i, n), 0)
                    gate_half((i, n), 1)
                    branch((i, n), ah, al)

            natural(U_D, 4, F_D, hh, hl, before_unit=lambda i: pe.wait_ge(s_ml, 2 * i + 2))
            pe.wait_ge(s_ple, 32)
            pe.wait_ge(s_m, 2 * KD)
            for t in range(NT):
                tr_rows(G_PLE + t, praw[:, t], n=2)
            natural(U_D + 4, 4, F_D + NT, hh, hl)
            for t in range(NT):
                pe.wait_ge(s_hn, NT + t + 1)
                for half in range(2):
                    tr_rows(G_R + 2 * t + half, h2[:, t, half * W:(half + 1) * W])
            pe.wait_ge(s_trf, G_F)
            for t in range(NT):
                for k in range(KD):
                    ins = pe.matmul(bank[6][:, t * (NG + NE):(t + 1) * (NG + NE)], h2T[:, k, t * P:(t + 1) * P],
                                    wr[:, k], start=k == 0, stop=k == KD - 1, skip_group_check=True)
            ins.then_inc(s_rt, 1)
            natural(U_P, 1, F_P, ph, pl)
            pe.wait_ge(s_M, 1)
            for t in range(NT):
                out = bank[6][:, P + t * NE:P + (t + 1) * NE]
                ins = pe.matmul(out, before[:, :], Mb[:, t], start=True, stop=t == 0, skip_group_check=True)
                for s in range(t):
                    ins = pe.matmul(out, onesb[:, :], Mb[:, s], start=False, stop=s == t - 1, skip_group_check=True)
            ins.then_inc(s_rk, 1)
            natural(U_P + 1, 1, F_P + NT, ph, pl)
            pe.wait_ge(s_ovm, 1)
            pe.matmul(bank[7][0:1, 0:1], ovm[:, 0:1], ones1[:, 0:1], start=True, stop=True).then_inc(s_ov, 1)

            def expert_rows(e, par, turn):
                pe.wait_ge(s_xe[par], 16 * turn + 16)
                for half in range(2):
                    if not (isinstance(e, int) and e == 0):
                        pe.wait_ge(s_xl, 2 * e - 1 + half)
                    for q in range(4):
                        ins = pe.transpose(bank[4 + half][:, q * P:(q + 1) * P],
                                           xe[:, par, (4 * half + q) * P:(4 * half + q + 1) * P], ident[:, :])
                    ins.then_inc(s_xt, 1)

            def product(u, out, a_hi, a_lo, k0, first, last):
                pe.wait_ge(s_lo, u.count())
                for kk in range(2):
                    ins = three(pe, out, a_hi[:, k0 + kk], a_lo[:, k0 + kk], whi[:, u.slot, kk], wlo[:, u.slot, kk],
                                first and kk == 0, last and kk == 1)
                ins.then_inc(s_mm, 5)

            def gate_or_up(u, e, which):
                if which == 0:
                    pe.wait_ge(s_xl, 2 * e + 2)
                    pe.wait_ge(s_si, e)
                else:
                    pe.wait_ge(s_hm, e)
                for i in range(4):
                    product(u.plus(i), bank[which][:, :], xh, xl, 2 * i, i == 0, i == 3)

            def hidden_rows(e):
                pe.wait_ge(s_hm, e + 1)
                pe.wait_ge(s_htl, e)
                for q in range(4):
                    ins = pe.transpose(bank[6][:, q * P:(q + 1) * P], hm[:, q * P:(q + 1) * P], ident[:, :])
                ins.then_inc(s_ht, 1)

            def down(u, e):
                pe.wait_ge(s_htl, e + 1)
                for n in range(2):
                    pe.wait_ge(s_y, 2 * e)
                    for i in range(2):
                        product(u.plus(2 * n + i), bank[2 + n][:, :], mh, ml, 2 * i, i == 0, i == 1)

            pe.wait_ge(s_free, F_G)
            expert_rows(0, 0, 0)
            gate_or_up(Unit(U_M), 0, 0)
            gate_or_up(Unit(U_M + 4), 0, 1)
            expert_rows(1, 1, 0)

            def expert(e, par, turn, rows_next=True):
                u = Unit(U_M - 4, NSTREAM, e)
                gate_or_up(u, e, 0)
                hidden_rows(e - 1)
                gate_or_up(u.plus(4), e, 1)
                if rows_next:
                    expert_rows(e + 1, 1 - par, turn)
                down(u.plus(8), e - 1)

            with pe.Fori(0, NE // 2 - 1) as i:
                expert(2 * i + 1, 1, i + 1)
                expert(2 * i + 2, 0, i + 1)
            expert(NE - 1, 1, 0, rows_next=False)
            hidden_rows(NE - 1)
            down(Unit(U_G - 4), NE - 1)

            pe.wait_ge(s_flag, 1)
            over = pe.value_load(flag[0:1, 0:1], min_val=0, max_val=1)
            with pe.If(over > 0):
                with pe.Fori(0, NE * OV_TILES) as o:
                    pe.wait_ge(s_o_dve, 3 * o + 3)
                    pe.wait_ge(s_o_act, 3 * o + 3)
                    pe.wait_ge(s_o_x, 16 * o + 16)
                    for k in range(KD):
                        ins = pe.transpose(bank[4 + k // 4][:, (k % 4) * P:(k % 4 + 1) * P], xe[:, 0, k * P:(k + 1) * P],
                                           ident[:, :])
                    ins.then_inc(s_o_pe, 1)
                    pe.wait_ge(s_o_dve, 3 * o + 4)
                    for j in range(12):
                        if j == 8:
                            pe.wait_ge(s_o_dve, 3 * o + 5)
                            for q in range(4):
                                ins = pe.transpose(bank[6][:, q * P:(q + 1) * P], hm[:, q * P:(q + 1) * P], ident[:, :])
                            ins.then_inc(s_o_pe, 1)
                            pe.wait_ge(s_o_dve, 3 * o + 6)
                        pe.wait_ge(s_o_raw[j % RING], 48 * o + 16 * (j // RING) + 16)
                        a, k0, nk = (oxT, 2 * (j % 4), KD) if j < 8 else (omT, 2 * (j % 2), FE // P)
                        out = bank[j // 4] if j < 8 else bank[2 + (j - 8) // 2]
                        for kk in range(2):
                            ins = pe.matmul(out[:, :], a[:, k0 + kk], raw[:, j % RING, kk], start=k0 + kk == 0,
                                            stop=k0 + kk == nk - 1)
                        ins.then_inc(s_o_pe, 1)

            def rows3(t):
                pe.wait_ge(s_hn, 2 * NT + t + 1)
                for half in range(2):
                    tr_rows(G_F + 2 * t + half, hn3[:, t % 2, half * W:(half + 1) * W])

            def g_tile(i, t):
                if i == 0:
                    if t == 0:
                        rows3(0)
                    if t + 1 < NT:
                        rows3(t + 1)
                    pe.wait_ge(s_trf, G_F + 2 * t + 2)

            natural(U_G, 4, F_G, hh, hl, before_tile=g_tile)
            natural(U_G + 4, 4, F_G + NT, hh, hl)


def kernel(**inputs):
    import concourse.bacc as bacc
    from concourse.bass_utils import run_bass_kernel_spmd

    nc = bacc.Bacc("TRN2", target_bir_lowering=False, num_devices=1)
    arrays, I = {}, {}
    for name, a in inputs.items():
        a = np.ascontiguousarray(a)
        arrays["in_" + name] = a
        I[name] = nc.dram_tensor("in_" + name, a.shape, mybir.dt.from_np(a.dtype), kind="ExternalInput").ap()
    shapes = [(1, TP, D), (B, TS, D), (1, 1, TP, H, HD), (1, 1, TP, H, HD), (1, 1, 2, W),
              (1, B, TS, H, HD), (1, B, TS, H, HD), (1, B, 2, W)]
    O = [nc.dram_tensor(f"out_{i}", s, F32, kind="ExternalOutput").ap() for i, s in enumerate(shapes)]
    program(nc, I, O)
    r = run_bass_kernel_spmd(nc, [arrays], core_ids=[0])
    return tuple(r.results[0][f"out_{i}"] for i in range(len(shapes)))
```

```python
from contextlib import ExitStack

import numpy as np
import concourse.bass as bass
from concourse import mybir

F32, F32R, BF16, I32 = mybir.dt.float32, mybir.dt.float32r, mybir.dt.bfloat16, mybir.dt.int32
ACT, ALU, AX = mybir.ActivationFunctionType, mybir.AluOpType, mybir.AxisListType

P = 128
D = 1024
KD = D // P
TP, B, TS = 512, 8, 16
T = TP + B * TS
NT = T // P
W = 512
KW = W // P
H, HD = 8, 64
HP = H // 2
PAST = 512
KB = PAST // P
NG, EG = 4, 4
NE = NG * EG
FE = 512
PLE = 256
EPS = 1e-6
C = 128
OV_TILES = (T - C) // P
RING = 4

HALF = T // 2
NB = 2 * KD
U_CC = 3 * KD // 2
U_C = U_CC + 3 * KW
U_D = U_C + 2 * NB
U_P, U_M = U_D + KD, U_D + KD + 2
F_CC = 3 * NT
F_D = F_CC + 3 * 2 * KW
F_P, F_G = F_D + 2 * NT, F_D + 4 * NT
NSTREAM = 12
U_G = U_M + NE * NSTREAM
G_X, G_STATE, G_QK, G_CONV, G_PLE, G_R, G_F = 0, 10, 11, 21, 22, 27, 37


class Unit:

    def __init__(self, c, stride=0, k=0):
        self.c, self.stride, self.k, self.slot = c, stride, k, c % RING
        v = c - U_M
        self.deep = v >= RING or stride == NSTREAM
        if not self.deep:
            self.raw, self.turn = c % RING, c // RING + 1
            return
        self.raw, self.turn = v % NSTREAM, v // NSTREAM + 1
        if self.raw < RING:
            self.raw = (U_M + self.raw) % RING
            self.turn += len(range(self.raw, U_M, RING))
        elif v >= NE * NSTREAM:
            self.raw += 4

    def plus(self, n):
        return Unit(self.c + n, self.stride, self.k)

    def count(self, less=0):
        return (self.c + 1 - less) + self.stride * self.k

    def loaded(self):
        return 16 * self.turn + 16 * (self.stride // (NSTREAM if self.deep else RING)) * self.k

    def split_before(self):
        if not self.deep:
            return self.count(RING)
        return self.count(NSTREAM - 4 if self.c >= U_G + 4 else NSTREAM)

    def mm(self, less=0):
        return 5 * (self.c + 1 - less) + 5 * self.stride * self.k

    def half(self, h):
        return 5 * self.c + (2, 5)[h] + 5 * self.stride * self.k


def program(nc, I, O):
    ctx = ExitStack()
    with ctx:
        base = 16512
        cursor = [base]

        def at(name, shape, dt, off):
            return nc.alloc_sbuf_tensor_at(name, shape, dt, offset=off)

        def size(shape, dt=F32):
            n = 2 if dt == BF16 else 4
            for s in shape[1:]:
                n *= s
            return (n + 31) // 32 * 32

        def sb(name, shape, dt=F32):
            t = at(name, shape, dt, cursor[0])
            cursor[0] += size(shape, dt)
            return t

        class Region:
            def __init__(self, nbytes):
                self.start = cursor[0]
                self.end = self.start + nbytes
                cursor[0] += nbytes

            def lay(self, *specs):
                off, out = self.start, []
                for name, shape, dt in specs:
                    out.append(at(name, shape, dt, off))
                    off += size(shape, dt)
                assert off <= self.end, (specs, off, self.end)
                return out if len(out) > 1 else out[0]

        ident = sb("ident", [P, P])
        um = sb("um", [P, P])
        neg = sb("neg", [P, P])
        before = sb("before", [P, P], BF16)
        onesb = sb("onesb", [P, P], BF16)
        ones1 = sb("ones1", [P, 1])
        zero = sb("zero", [P, P])
        mhalf = sb("mhalf", [P, 8])
        lnb_off = cursor[0]
        lnb = sb("lnb", [P, D])
        qkg = sb("qkg", [P, 2, HD])
        convw = sb("convw", [P, 3, KW])
        rbias = sb("rbias", [P, NG + NE])
        wr = sb("wr", [P, KD, NG + NE])
        ss = sb("ss", [P, 3 * NT])
        rms = sb("rms", [P, 3 * NT])
        rr = sb("rr", [P, 3 * NT])
        ssq = sb("ssq", [P, 10, H])
        msq = sb("msq", [P, 10, H])
        rq = sb("rq", [P, 10, H])
        cpk = sb("cpk", [P, KW, 2 + 2 * B])
        lg = sb("lg", [P, NT, NG + NE])
        desc = sb("desc", [P, 4])
        eidx = sb("eidx", [P, NE])
        gmax, cm1, v1, v2, vdiff, vexp, vsum, gsum = [
            sb(name, [P, NT]) for name in ("gmax", "cm1", "v1", "v2", "vdiff", "vexp", "vsum", "gsum")]
        gdiff, gexp, lsel2 = [sb(name, [P, NT, 4]) for name in ("gdiff", "gexp", "lsel2")]
        ovm = sb("ovm", [P, 1])
        free_ = sb("free_", [P, 1])
        og = sb("og", [P, NT, 4])
        ok = sb("ok", [P, 2, NT, 4])
        cand = sb("cand", [P, NT, 4])
        lsel = sb("lsel", [P, NT, 4])
        prod = sb("prod", [P, NT, 4, 4])
        Mk = sb("Mk", [P, 2, NT, NE])
        Mb = sb("Mb", [P, NT, NE], BF16)
        rk = sb("rk", [P, NT, NE])
        mr = sb("mr", [P, 2, NT, NE])
        slotf = sb("slotf", [P, 4, 2, NT])
        gate = sb("gate", [P, 2, NT])
        slot = sb("slot", [P, 2, NT], I32)
        flag = sb("flag", [1, 1], I32)
        tmpn = sb("tmpn", [TS, P])
        an = sb("an", [TS, P])
        qbd = sb("qbd", [P, 2, HP, 2 * TS])
        spn_rows = sb("spn_rows", [P, P])
        ktb = sb("ktb", [P, 2, HP, TS])
        af = sb("af", [P, HP, P])
        raw = sb("raw", [P, RING, 2, W])
        whi = sb("whi", [P, RING, 2, W], F32R)
        wlo = sb("wlo", [P, RING, 2, W], F32R)

        XR = Region(NT * D * 4)
        HT = Region(2 * KD * T * 4)
        CT = Region(2 * KW * T * 4)
        AT = Region(2 * KW * T * 4)
        QK = Region(2 * KW * T * 4)
        VV = Region(NT * W * 4)
        TAIL = Region(229344 - cursor[0])

        x = XR.lay(("x", [P, NT, D], F32))
        hh, hl = HT.lay(("hh", [P, KD, T], F32R), ("hl", [P, KD, T], F32R))
        ch, cl = CT.lay(("ch", [P, KW, T], F32R), ("cl", [P, KW, T], F32R))
        ah, al = AT.lay(("ah", [P, KW, T], F32R), ("al", [P, KW, T], F32R))
        qT, kT = QK.lay(("qT", [P, KW, T], F32), ("kT", [P, KW, T], F32))
        v = VV.lay(("v", [P, NT, W], F32))
        hn, zb, sqb, qn1, qn2 = AT.lay(("hn", [P, 2, D], F32), ("zb", [P, 2, W], F32), ("sqb", [P, 1, W], F32),
                                       ("qn1", [P, 1, W], F32), ("qn2", [P, 2, W], F32))
        junk = TAIL.lay(("junk", [P, D], F32))
        ccT, yc = XR.lay(("ccT", [P, KW, T], F32), ("yc", [P, KW, T], F32))
        up, us = TAIL.lay(("up", [P, KW, 2 + TP], F32), ("us", [P, KW, B, 2 + TS], F32))
        ncv = at("ncv", [2 + 2 * B, W], F32, AT.start)
        st = at("st", [2 * B, W], F32, VV.start)
        tm0, tm1, sp0, sp1 = XR.lay(("tm0", [P, 1280], F32), ("tm1", [P, 1280], F32),
                                    ("sp0", [P, 1280], F32), ("sp1", [P, 1280], F32))
        a0, a1 = TAIL.lay(("a0", [P, 1280], F32), ("a1", [P, 1280], F32))
        tmp1280, sp1280, a1280 = [a0] + [tm1, tm0] * 4, [a1] + [sp1, sp0] * 4, [a0, a1] * 4
        later0, later1 = at("later0", [P, 384], F32, lnb_off), at("later1", [P, 256], F32, lnb_off + 384 * 4)
        vc, tms, sps, spl = XR.lay(("vc", [P, KB, W], F32), ("tms", [P, W], F32), ("sps", [P, W], F32),
                                   ("spl", [P, KB - 1, P], F32))
        kc, sg = TAIL.lay(("kc", [P, KB, W], F32), ("sg", [P, T], F32))
        ktc, qs, ks, a_s = VV.lay(("ktc", [P, 2, HP, P], F32), ("qs", [P, HP, P], F32), ("ks", [P, HP, P], F32),
                                  ("a_s", [P, W], F32))
        vn = at("vn", [TS, W], F32, lnb_off)
        m = QK.lay(("m", [P, KD, T], F32))
        mt = TAIL.lay(("mt", [P, T], F32))
        h2 = QK.lay(("h2", [P, NT, D], F32))
        h2T = at("h2T", [P, KD, T], F32, VV.start)
        praw, junk2 = CT.lay(("praw", [P, NT, PLE], F32), ("junk2", [P, D], F32))
        ph, pl = [at(n, [P, 2, T], F32R, CT.start + KW * T * 4 + i * 2 * T * 4) for i, n in enumerate(("ph", "pl"))]
        pp = AT.lay(("pp", [P, NT, D], F32))
        xe, xh, xl, si, hm, mh, ml, y = HT.lay(
            ("xe", [P, 2, D], F32), ("xh", [P, KD, P], F32R), ("xl", [P, KD, P], F32R), ("si", [P, FE], F32),
            ("hm", [P, FE], F32), ("mh", [P, FE // P, P], F32R), ("ml", [P, FE // P, P], F32R), ("y", [P, 2, D], F32))
        oxT, omT = CT.lay(("oxT", [P, KD, P], F32), ("omT", [P, FE // P, P], F32))
        raws = [raw[:, i] for i in range(RING)]
        for region, n in ((TAIL, 2), (VV, 2), (CT, 4)):
            more = region.lay(*[(f"raw{len(raws) + i}", [P, 2, W], F32) for i in range(n)])
            raws += [t[:, :, :] for t in more]
        NYG = 4
        yg = at("yg", [P, NYG, D], F32, VV.start)
        hn3, eo, junk3 = QK.lay(("hn3", [P, 2, D], F32), ("eo", [P, 4, W], F32), ("junk3", [P, D], F32))

        bank = [ctx.enter_context(nc.psum_tensor(f"bank{i}", [P, 512], F32)) for i in range(8)]
        Xd = nc.dram_tensor("moe_rows", ((NE * C) + NE * OV_TILES * P, D), F32, kind="Internal").ap()
        Yd = nc.dram_tensor("moe_out", ((NE * C) + NE * OV_TILES * P, D), F32, kind="Internal").ap()

        def sem(name):
            return ctx.enter_context(nc.semaphore(name))

        s_const = sem("constants_loaded")
        s_ln = sem("norm_weights_loaded")
        s_x = [sem(f"x_loaded{t}") for t in range(NT)]
        s_made = sem("constants_made")
        s_pc = sem("pool_step")
        s_vc = sem("vector_step")
        s_raw = [sem(f"raw_loaded{i}") for i in range(NSTREAM)]
        s_hi = sem("weights_hi")
        s_lo = sem("weights_lo")
        s_mm = sem("products_done")
        s_free = sem("banks_read")
        s_sq = sem("squares_summed")
        s_r = sem("rms_ready")
        s_hn = sem("rows_normed")
        s_tr = sem("transposed")
        s_trh = sem("transposed_hi")
        s_trf = sem("transposed_read")
        s_qsq = sem("head_squares")
        s_ssq = sem("head_sums")
        s_rq = sem("head_rms")
        s_qn1 = sem("head_scaled")
        s_qn2 = sem("head_normed")
        s_ko = [sem(f"k_stored{i}") for i in range(2)]
        s_vout = sem("v_stored")
        s_state = sem("conv_state_loaded")
        s_ch = sem("gated_conv_hi")
        s_cl = sem("gated_conv_lo")
        s_cpk = sem("last_inputs_packed")
        s_ncvo = sem("conv_state_stored")
        s_zero = sem("rows_zeroed")
        s_z = sem("scores")
        s_ln1 = sem("log_terms")
        s_spr = sem("softplus")
        s_sp = sem("softplus_masked")
        s_acc = sem("log_sums")
        s_ea = sem("weights_exp")
        s_am = sem("weights_masked")
        s_av = sem("head_pairs_summed")
        s_ah = sem("attn_hi")
        s_al = sem("attn_lo")
        s_kc = [sem(f"cache_k_loaded{i}") for i in range(2)]
        s_vcl = sem("cache_v_loaded")
        s_qb = sem("queries_placed")
        s_qs = sem("sample_rows_moved")
        s_kt = sem("cache_k_transposed")
        s_kta = sem("cache_kT_scalar")
        s_ktv = sem("cache_kT_vector")
        s_zs = sem("sample_scores")
        s_lns = sem("sample_log_terms")
        s_sps = sem("sample_softplus")
        s_spn = sem("sample_softplus_masked")
        s_later = sem("prompt_later_blocks_summed")
        s_spl = sem("later_blocks_summed")
        s_accs = sem("sample_log_sums")
        s_eas = sem("sample_weights_exp")
        s_ams = sem("sample_weights_masked")
        s_avs = sem("sample_values")
        s_af = sem("sample_attn_kept")
        s_gate = sem("gate_sigmoids")
        s_br = sem("branches_gated")
        s_m = sem("merged")
        s_mh = sem("merged_hi")
        s_ml = sem("merged_lo")
        s_xr = sem("x_reloaded")
        s_ple = sem("ple_rows_loaded")
        s_rt = sem("router_logits")
        s_rx = sem("router_exps")
        s_d = sem("router_differences")
        s_M = sem("choices")
        s_rk = sem("ranks")
        s_slot = sem("slots")
        s_ovm = sem("overflow_rows_marked")
        s_ov = sem("overflow_sum")
        s_flag = sem("overflow_flag")
        s_scat = sem("rows_scattered")
        s_xe = [sem(f"expert_rows_loaded{i}") for i in range(2)]
        s_xt = sem("expert_rows_transposed")
        s_xh = sem("expert_rows_hi")
        s_xl = sem("expert_rows_lo")
        s_si = sem("silu")
        s_hm = sem("hidden")
        s_ht = sem("hidden_transposed")
        s_hth = sem("hidden_hi")
        s_htl = sem("hidden_lo")
        s_y = sem("expert_outputs")
        s_yo = [sem(f"expert_outputs_stored{i}") for i in range(2)]
        s_o_x = sem("overflow_rows_loaded")
        s_o_raw = [sem(f"overflow_raw_loaded{i}") for i in range(RING)]
        s_o_free = sem("overflow_output_free")
        s_o_pe = sem("overflow_products")
        s_o_act = sem("overflow_scalar")
        s_o_dve = sem("overflow_vector")
        s_o_st = sem("overflow_stored")
        s_yg = [sem(f"outputs_gathered{i}") for i in range(NYG)]
        s_yu = sem("outputs_added")
        s_eo = sem("result_tile")
        s_out = [sem(f"result_stored{i}") for i in range(4)]

        small = [bank[4], bank[7]]

        block = ctx.enter_context(nc.Block())


        def load_unit(sp, u, src):
            if u.c >= RING:
                sp.wait_ge(s_lo, u.split_before())
            sp.dma_start(raws[u.raw], src).then_inc(s_raw[u.raw], 16)

        def load_columns(sp, u, w, j):
            nk = w.shape[0] // P
            src = w.rearrange("(k p) (j c) -> p k j c", p=P, c=P)[:, :, bass.ds(j, 1)].rearrange("p k o c -> p k (o c)")
            sp.wait_ge(s_lo, u.split_before())
            sp.dma_start(columns(raws[u.raw])[:, 0:nk], src).then_inc(s_raw[u.raw], 16)

        def columns(slot):
            return slot.rearrange("p a (k c) -> p (a k) c", c=P)

        def part(slot, short):
            return slot[:, 0] if short else slot

        def split_hi(act, u, short=False):
            act.wait_ge(s_raw[u.raw], u.loaded())
            if u.c >= RING:
                act.wait_ge(s_mm, u.mm(RING))
            nc.scalar.activation(part(whi[:, u.slot], short), part(raws[u.raw], short), ACT.Copy).then_inc(s_hi, 1)

        def split_lo(dve, u, short=False):
            dve.wait_ge(s_hi, u.count())
            nc.vector.tensor_tensor(out=part(wlo[:, u.slot], short), in0=part(raws[u.raw], short),
                                    in1=part(whi[:, u.slot], short).bitcast(F32), op=ALU.subtract).then_inc(s_lo, 1)

        def gate_unit(c):
            return Unit(U_C + 2 * c) if isinstance(c, int) else Unit(U_C + 2 * c[1], 4, c[0])

        def number(c):
            return c if isinstance(c, int) else 2 * c[0] + c[1]

        def later(c, n):
            return c + n if isinstance(c, int) else (c[0], c[1] + n)

        def is_zero(n):
            return isinstance(n, int) and n == 0

        widths = (512, 512, 256)

        def z_banks(h):
            return (bank[4:7], bank[0:3])[h % 2]

        def pair_bank(pair):
            return bank[(3, 7)[pair % 2]]

        def half_rows(h):
            return slice(h * HALF, (h + 1) * HALF)

        def three(pe, out, a_hi, a_lo, b_hi, b_lo, first, last):
            pe.matmul(out, a_hi, b_hi, start=first, stop=False, skip_group_check=True)
            pe.matmul(out, a_lo, b_hi, start=False, stop=False, skip_group_check=True)
            return pe.matmul(out, a_hi, b_lo, start=False, stop=last, skip_group_check=True)

        def ring_bank(g):
            return bank[7 - 2 * (g % 2)] if G_R <= g < G_F else bank[5 + g % 3]

        def tile_done(u0, t, by_tile):
            if by_tile:
                return 5 * u0 + t + 1 if t < NT - 1 else 5 * (u0 + 4)
            return 5 * (u0 + 3) + t + 1

        def rows(w, k0, col):
            return w[k0 * P:(k0 + 2) * P, col:col + W].rearrange("(k p) c -> p k c", p=P)

        def flat(name):
            return I[name].rearrange("o k n -> (o k) n")

        @block.sync
        def _(sp):
            xp = I["x_prompt"].rearrange("o (t p) d -> p (o t) d", p=P)
            xs = I["x_sample"].rearrange("b s d -> (b s) d")
            w_in = flat("w_in")
            for t in range(NT):
                sp.dma_start(x[:, t], xp[:, t] if t < NT - 1 else xs).then_inc(s_x[t], 16)
                if t == 0:
                    sp.dma_start(lnb[:, :], I["ln_mix"].to_broadcast([P, D])).then_inc(s_ln, 16)
                for i in ((0, 1), (2, 3), (), (), ())[t]:
                    load_unit(sp, Unit(i), rows(w_in, 2 * i, 0))
            sp.dma_start(st[:, :], I["state_conv"].rearrange("o b j c -> (o b j) c")).then_inc(s_state, 16)
            for c in range(1, 3):
                for i in range(4):
                    load_unit(sp, Unit(4 * c + i), rows(w_in, 2 * i, W * c))
            for c, place in enumerate((4, 5, 3)):
                for j in range(KW):
                    load_columns(sp, Unit(U_CC + KW * c + j), w_in, KW * place + j)

            def conv_block(c):
                load_columns(sp, gate_unit(c), w_in, 8 * KW + number(c))
                load_columns(sp, gate_unit(c).plus(1), flat("w_conv_branch"), number(c))

            def attn_block(c):
                load_columns(sp, gate_unit(c), w_in, 6 * KW - KD + number(c))
                load_columns(sp, gate_unit(c).plus(1), flat("w_attn_branch"), number(c) - KD)

            conv_block(0)
            conv_block(1)

            ck = I["cache_k"].rearrange("o b (kb p) h d -> p (o b) kb (h d)", p=P)
            cv = I["cache_v"].rearrange("o b (kb p) h d -> p (o b) kb (h d)", p=P)
            vnew = O[6].rearrange("o b s h d -> (o b) s (h d)")

            def cache_k(b):
                for i in range(2):
                    src = ck[:, bass.ds(b, 1), 2 * i:2 * i + 2].rearrange("p o kb c -> p (o kb) c")
                    if not is_zero(b):
                        sp.wait_ge(s_kt, 4 * b - 2 + 2 * i)
                    sp.dma_start(kc[:, 2 * i:2 * i + 2], src).then_inc(s_kc[i], 16)

            def cache_v(b):
                src = cv[:, bass.ds(b, 1)].rearrange("p o kb c -> p (o kb) c")
                new = vnew[bass.ds(b, 1)].rearrange("o s c -> s (o c)")
                if not is_zero(b):
                    sp.wait_ge(s_avs, b)
                sp.dma_start(vc[:, :, :], src).then_inc(s_vcl, 16)
                sp.dma_start(vn[:, :], new).then_inc(s_vcl, 16)

            sp.wait_ge(s_vout, 16 * NT)
            sp.wait_ge(s_hn, NT)
            sp.wait_ge(s_av, H)
            cache_k(0)
            conv_block(2)
            cache_k(1)
            cache_v(0)
            conv_block(3)
            cache_k(2)
            cache_v(1)
            with sp.Fori(1, 3) as i:
                for n in range(2):
                    conv_block((i, n + 2))
                    cache_k(2 * i + n + 1)
                    cache_v(2 * i + n)
            attn_block(8)
            cache_k(B - 1)
            cache_v(B - 2)
            attn_block(9)
            cache_v(B - 1)
            attn_block(10)
            attn_block(11)
            sp.wait_ge(s_al, HP + 1)
            for t in range(NT):
                sp.dma_start(x[:, t], xp[:, t] if t < NT - 1 else xs).then_inc(s_xr, 16)
            sp.dma_start(lnb[:, :], I["ln_ffn"].to_broadcast([P, D])).then_inc(s_ln, 16)
            with sp.Fori(6, NB // 2) as i:
                attn_block((i, 0))
                attn_block((i, 1))
            sp.wait_ge(s_mm, gate_unit(B - 1).plus(1).mm())
            sp.dma_start(praw[:, 0:NT - 1], I["p_prompt"].rearrange("o b (t p) c -> p (o b t) c", p=P)
                         ).then_inc(s_ple, 16)
            sp.dma_start(praw[:, NT - 1], I["p_sample"].rearrange("o b s c -> (o b s) c")).then_inc(s_ple, 16)
            u = U_D
            for n in range(2):
                for i in range(4):
                    load_unit(sp, Unit(u), rows(flat("w_out"), 2 * i, n * W))
                    u += 1
            for n in range(2):
                load_unit(sp, Unit(u), rows(flat("w_ple_proj"), 0, n * W))
                u += 1
            assert u == U_M

            gup = [I[n].rearrange("o e (k p) f -> p (o e) k f", p=P) for n in ("w_exp_gate", "w_exp_up")]
            dwn = I["w_exp_down"].rearrange("o e (k p) f -> p (o e) k f", p=P)

            def gate_up_src(e, j):
                return gup[j // 4][:, bass.ds(e, 1), 2 * (j % 4):2 * (j % 4) + 2].rearrange("p o k f -> p (o k) f")

            def down_src(e, j):
                return dwn[:, bass.ds(e, 1), 2 * (j % 2):2 * (j % 2) + 2,
                           (j // 2) * W:(j // 2 + 1) * W].rearrange("p o k f -> p (o k) f")

            sp.wait_ge(s_hn, 2 * NT)
            sp.dma_start(lnb[:, :], I["ln_ple"].to_broadcast([P, D])).then_inc(s_ln, 16)
            for j in range(4):
                load_unit(sp, Unit(U_M + j), gate_up_src(0, j))
            sp.wait_ge(s_rt, 1)
            for j in range(4, 8):
                load_unit(sp, Unit(U_M + j), gate_up_src(0, j))
            sp.wait_ge(s_scat, 16 * 2 * NT)
            for e in range(2):
                sp.dma_start(xe[:, e], Xd[e * C:(e + 1) * C, :]).then_inc(s_xe[e], 16)
            sp.wait_ge(s_free, F_G)
            sp.wait_ge(s_sq, 2 * NT)
            for j in range(4):
                load_unit(sp, Unit(U_M + 8 + j), gate_up_src(1, j))

            def expert_loads(e, par, rows_next=True):
                if rows_next:
                    sp.wait_ge(s_xt, 2 * e)
                    sp.dma_start(xe[:, 1 - par], Xd[bass.ds((e + 1) * C, C), :]).then_inc(s_xe[1 - par], 16)
                for j in range(4, 8):
                    load_unit(sp, Unit(U_M - 4 + j, NSTREAM, e), gate_up_src(e, j))
                for j in range(4):
                    load_unit(sp, Unit(U_M + 4 + j, NSTREAM, e), down_src(e - 1, j))
                if rows_next:
                    for j in range(4):
                        load_unit(sp, Unit(U_M + 8 + j, NSTREAM, e), gate_up_src(e + 1, j))

            with sp.Fori(0, NE // 2 - 1) as i:
                expert_loads(2 * i + 1, 1)
                expert_loads(2 * i + 2, 0)
            expert_loads(NE - 1, 1, rows_next=False)
            for j in range(4):
                load_unit(sp, Unit(U_G - 4 + j), down_src(NE - 1, j))

            sp.wait_ge(s_flag, 1)
            over = sp.value_load(flag[0:1, 0:1], min_val=0, max_val=1)
            with sp.If(over > 0):
                with sp.Fori(0, NE) as e:
                    with sp.Fori(0, OV_TILES) as o:
                        n = e * OV_TILES + o
                        sp.wait_ge(s_o_act, 3 * n + 3)
                        sp.dma_start(xe[:, 0], Xd[bass.ds(NE * C + n * P, P), :]).then_inc(s_o_x, 16)
                        for j in range(12):
                            if j >= RING:
                                sp.wait_ge(s_o_pe, 14 * n + j - 2)
                            sp.dma_start(raw[:, j % RING], gate_up_src(e, j) if j < 8 else down_src(e, j - 8)
                                         ).then_inc(s_o_raw[j % RING], 16)
                sp.wait_ge(s_o_act, 3 * NE * OV_TILES + 3)
            for i in range(8):
                load_unit(sp, Unit(U_G + i), rows(flat("w_ple_gate"), 2 * (i % 4), (i // 4) * W))
            for i in range(2 * NT):
                n, t = i // NT, i % NT
                dst = (O[0].rearrange("o (t p) d -> p (o t) d", p=P)[:, t] if t < NT - 1
                       else O[1].rearrange("b s d -> (b s) d"))
                sp.wait_ge(s_eo, i + 1)
                sp.dma_start(dst[:, n * W:(n + 1) * W], eo[:, i % 4]).then_inc(s_out[i % 4], 16)
            for i in range(4):
                sp.wait_ge(s_out[i], 16 * len(range(i, 2 * NT, 4)))
            sp.wait_ge(s_ko[0], 16 * 2)
            sp.wait_ge(s_ko[1], 16 * 3)
            sp.wait_ge(s_vout, 16 * NT)
            sp.wait_ge(s_ncvo, 32)

        @block.gpsimd
        def _(pool):
            pl_ = nc.gpsimd
            for tile, value in ((ident, 0.0), (um, -1.0), (neg, -1.0), (before, 1.0), (onesb, 1.0), (ones1, 1.0),
                                (mhalf, -0.5), (zero, 0.0)):
                pl_.memset(tile[:], value).then_inc(s_made, 1)
            pl_.memset(qbd[:], 0.0).then_inc(s_made, 1)
            pl_.memset(spn_rows[:], 0.0).then_inc(s_made, 1)
            pl_.iota(desc[:], pattern=[[-1, 4]], base=4, channel_multiplier=0,
                     allow_small_or_imprecise_dtypes=True).then_inc(s_made, 1)
            pl_.iota(eidx[:], pattern=[[1, NE]], base=0, channel_multiplier=0,
                     allow_small_or_imprecise_dtypes=True).then_inc(s_made, 1)
            pool.wait_ge(s_made, 12)
            pl_.affine_select(out=ident[:], in_=ident[:], compare_op=ALU.not_equal, fill=1.0, base=0,
                              pattern=[[-1, P]], channel_multiplier=1).then_inc(s_made, 1)
            pl_.affine_select(out=um[:], in_=um[:], compare_op=ALU.is_ge, fill=0.0, base=0,
                              pattern=[[-1, P]], channel_multiplier=1).then_inc(s_made, 1)
            pl_.affine_select(out=before[:], in_=before[:], compare_op=ALU.is_gt, fill=0.0, base=0,
                              pattern=[[1, P]], channel_multiplier=-1).then_inc(s_made, 1)
            with nc.allow_non_contiguous_dma(reason="small weights"):
                pool.dma_start(qkg[:, 0], I["q_norm"].to_broadcast([P, HD])).then_inc(s_const, 16)
                pool.dma_start(qkg[:, 1], I["k_norm"].to_broadcast([P, HD])).then_inc(s_const, 16)

            step = [0]

            def link(ins):
                step[0] += 1
                ins.then_inc(s_pc, 1)
                pool.wait_ge(s_pc, step[0])

            def row_rms(i):
                pool.wait_ge(s_sq, i + 1)
                link(pl_.tensor_scalar(rms[:, i:i + 1], ss[:, i:i + 1], 1.0 / D, EPS, ALU.mult, ALU.add))
                pl_.tensor_tensor(rr[:, i:i + 1], rms[:, i:i + 1], mhalf[:, 0:1], ALU.pow).then_inc(s_r, 1)

            for t in range(NT):
                row_rms(t)
            pool.wait_ge(s_const, 32)
            link(pl_.tensor_scalar(qkg[:, 0], qkg[:, 0], HD ** -0.5, 1.0, ALU.mult, ALU.mult))
            kp = O[2].rearrange("o b (t p) h d -> p (o b t) (h d)", p=P)
            ks = O[5].rearrange("o b s h d -> (o b s) (h d)")
            vp = O[3].rearrange("o b (t p) h d -> p (o b t) (h d)", p=P)
            vs = O[6].rearrange("o b s h d -> (o b s) (h d)")

            def store_k(n):
                t = n - NT
                pool.wait_ge(s_qn2, n + 1)
                pool.dma_start(kp[:, t] if t < NT - 1 else ks, qn2[:, n % 2]).then_inc(s_ko[n % 2], 16)

            for n in range(2 * NT):
                pool.wait_ge(s_free, n + 1)
                if n:
                    pool.wait_ge(s_ssq, n)
                pl_.tensor_tensor(sqb[:, 0], zb[:, n % 2], zb[:, n % 2], ALU.mult).then_inc(s_qsq, 1)
                pool.wait_ge(s_ssq, n + 1)
                link(pl_.tensor_scalar(msq[:, n], ssq[:, n], 1.0 / HD, EPS, ALU.mult, ALU.add))
                pl_.tensor_tensor(rq[:, n], msq[:, n], mhalf[:, :], ALU.pow).then_inc(s_rq, 1)
                if n > NT:
                    store_k(n - 1)
            store_k(2 * NT - 1)
            with nc.allow_non_contiguous_dma(reason="small weights"):
                for j in range(3):
                    pool.dma_start(convw[:, j], I["conv_w"][0, j].rearrange("(c p) -> p c", p=P)).then_inc(s_const, 16)
                pool.dma_start(rbias[:, 0:NG], I["b_router_group"].to_broadcast([P, NG])).then_inc(s_const, 16)
                pool.dma_start(rbias[:, NG:], I["b_router_expert"].to_broadcast([P, NE])).then_inc(s_const, 16)
                pool.dma_start(wr[:, :, 0:NG], flat("w_router_group").rearrange("(k p) n -> p k n", p=P)
                               ).then_inc(s_const, 16)
                pool.dma_start(wr[:, :, NG:], flat("w_router_expert").rearrange("(k p) n -> p k n", p=P)
                               ).then_inc(s_const, 16)
            pl_.memset(up[:, :, 0:2], 0.0).then_inc(s_made, 1)
            for t in range(NT):
                pool.wait_ge(s_free, 2 * NT + t + 1)
                pool.dma_start(vp[:, t] if t < NT - 1 else vs, v[:, t]).then_inc(s_vout, 16)
            with pool.Fori(0, NE) as e:
                pool.dma_start(Xd[bass.ds(e * C, C), :].rearrange("r (a b) -> r a b", b=P),
                               zero[:, None, :].to_broadcast([P, D // P, P])).then_inc(s_zero, 16)
            pool.wait_ge(s_free, F_CC + 4 * KW)
            pl_.tensor_copy(cpk[:, :, 0:2], up[:, :, TP:TP + 2]).then_inc(s_cpk, 1)
            for j in range(KW):
                pl_.tensor_copy(cpk[:, j, 2:].rearrange("p (b s) -> p b s", s=2), us[:, j, :, TS:TS + 2]).then_inc(s_cpk, 1)
            pool.wait_ge(s_trf, G_CONV + 1)
            pool.dma_start(O[4].rearrange("o b j c -> (o b j) c"), ncv[0:2]).then_inc(s_ncvo, 16)
            pool.dma_start(O[7].rearrange("o b j c -> (o b j) c"), ncv[2:]).then_inc(s_ncvo, 16)

            diag = (0, 512, 896, 1024)
            for h in range(H + 1):
                if h < H:
                    for i in range(4):
                        pool.wait_ge(s_spr, 3 * h + (1, 2, 2, 3)[i])
                        blk = sp1280[h][:, diag[i]:diag[i] + P]
                        pl_.affine_select(out=blk, in_=blk, compare_op=ALU.is_gt, fill=0.0, base=0,
                                          pattern=[[1, P]], channel_multiplier=-1).then_inc(s_sp, 1)
                if h > 0:
                    for i in range(4):
                        pool.wait_ge(s_ea, 3 * h - 3 + (1, 2, 2, 3)[i])
                        blk = a1280[h - 1][:, diag[i]:diag[i] + P]
                        pl_.affine_select(out=blk, in_=blk, compare_op=ALU.is_gt, fill=0.0, base=0,
                                          pattern=[[1, P]], channel_multiplier=-1).then_inc(s_am, 1)

            def mask_softplus(b):
                pool.wait_ge(s_sps, 2 * b + 2)
                pl_.affine_select(out=spn_rows[0:TS], in_=spn_rows[0:TS], compare_op=ALU.is_gt, fill=0.0, base=0,
                                  pattern=[[0, H], [1, TS]], channel_multiplier=-1).then_inc(s_spn, 1)

            def mask_weights(b):
                pool.wait_ge(s_eas, 2 * b + 2)
                pl_.affine_select(out=an[:, :], in_=an[:, :], compare_op=ALU.is_gt, fill=0.0, base=0,
                                  pattern=[[0, H], [1, TS]], channel_multiplier=-1).then_inc(s_ams, 1)

            mask_softplus(0)
            for b in range(1, B):
                mask_weights(b - 1)
                mask_softplus(b)
            mask_weights(B - 1)

            for t in range(NT):
                row_rms(NT + t)

            pool.wait_ge(s_flag, 1)
            over = pool.value_load(flag[0:1, 0:1], min_val=0, max_val=1)
            pool.wait_ge(s_zero, 16 * NE)
            with pool.If(over > 0):
                with pool.Fori(0, NE * OV_TILES) as o:
                    pool.dma_start(Xd[bass.ds(NE * C + o * P, P), :].rearrange("r (a b) -> r a b", b=P),
                                   zero[:, None, :].to_broadcast([P, D // P, P])).then_inc(s_zero, 16)
                pool.wait_ge(s_zero, 16 * (NE + NE * OV_TILES))
            pool.wait_ge(s_slot, 1)
            for t in range(NT):
                for k in range(2):
                    pool.indirect_dma_start(out=Xd[:, :], out_offset=bass.IndirectOffsetOnAxis(
                        ap=slot[:, k, t:t + 1], axis=0), in_=h2[:, t, :], in_offset=None).then_inc(s_scat, 16)

            def store_y(e, par):
                pool.wait_ge(s_y, 2 * e + 2)
                pool.dma_start(Yd[bass.ds(e * C, C), :], y[:, par]).then_inc(s_yo[par], 16)

            with pool.Fori(0, NE // 2) as i:
                store_y(2 * i, 0)
                store_y(2 * i + 1, 1)
            with pool.If(over > 0):
                pl_.tensor_tensor(free_[0:1], ones1[0:1], ones1[0:1], ALU.add).then_inc(s_o_free, 1)
                with pool.Fori(0, NE * OV_TILES) as o:
                    pool.wait_ge(s_o_act, 3 * o + 6)
                    pool.dma_start(Yd[bass.ds(NE * C + o * P, P), :], y[:, 0]).then_inc(s_o_st, 16)
                    pool.wait_ge(s_o_st, 16 * o + 16)
                    pl_.tensor_tensor(free_[0:1], ones1[0:1], ones1[0:1], ALU.add).then_inc(s_o_free, 1)
            pool.wait_ge(s_yo[0], 16 * NE // 2)
            pool.wait_ge(s_yo[1], 16 * NE // 2)

            def gather(i, n_rows):
                if i >= 2 * NT:
                    return
                if i >= NYG:
                    pool.wait_ge(s_yu, i - NYG + 1)
                pool.indirect_dma_start(out=yg[:, i % NYG, :], out_offset=None, in_=Yd[0:n_rows, :],
                                        in_offset=bass.IndirectOffsetOnAxis(ap=slot[:, i % 2, i // 2:i // 2 + 1], axis=0)
                                        ).then_inc(s_yg[i % NYG], 16)

            def gather_all(n_rows):
                for i in range(NYG):
                    gather(i, n_rows)
                for t in range(NT):
                    gather(NYG + 2 * t, n_rows)
                    gather(NYG + 2 * t + 1, n_rows)
                    row_rms(2 * NT + t)

            at_step = step[0]
            with pool.If(over > 0):
                gather_all(NE * C + NE * OV_TILES * P)
            step[0] = at_step
            with pool.Else():
                gather_all(NE * C)

        @block.scalar
        def _(act):
            sc = nc.scalar
            hi = lambda u: split_hi(act, Unit(u))

            def square(i, out, wait_sem, value):
                act.wait_ge(wait_sem, value)
                if i % NT:
                    act.wait_ge(s_sq, i)
                sc.activation(out[:, :], x[:, i % NT], ACT.Square, accum_out=ss[:, i:i + 1]).then_inc(s_sq, 1)

            def norm_hi(g, t, half):
                act.wait_ge(s_tr, g + 1)
                sc.activation(hh[:, 4 * half:4 * half + 4, t * P:(t + 1) * P],
                              ring_bank(g)[:, :].rearrange("p (k t) -> p k t", k=4), ACT.Copy).then_inc(s_trh, 1)

            def x_hi(t):
                for half in range(2):
                    norm_hi(G_X + 2 * t + half, t, half)

            def rows_out(c, t):
                n = c * NT + t
                act.wait_ge(s_mm, tile_done(4 * c, t, c < 2))
                if c < 2:
                    if n >= 2:
                        act.wait_ge(s_qn1, n - 1)
                    sc.activation(zb[:, n % 2], bank[t][:, :], ACT.Copy).then_inc(s_free, 1)
                else:
                    act.wait_ge(s_trf, G_STATE + 1)
                    sc.activation(v[:, t], bank[t][:, :], ACT.Copy).then_inc(s_free, 1)

            def x_square(t):
                square(t, junk, s_x[t], 16)

            x_square(0)
            hi(0)
            x_hi(0)
            hi(1)
            x_square(1)
            hi(2)
            hi(3)
            x_hi(1)
            x_square(2)
            x_square(3)
            x_hi(2)
            rows_out(0, 0)
            x_square(4)
            x_hi(3)
            rows_out(0, 1)
            x_hi(4)
            rows_out(0, 2)
            rows_out(0, 3)
            for i in range(4, 7):
                hi(i)
            rows_out(0, 4)
            hi(7)
            for t in range(4):
                rows_out(1, t)
            for i in range(4, 7):
                hi(4 + i)
            rows_out(1, 4)
            hi(4 + 7)
            for i in range(4, 7):
                hi(8 + i)
            for t in range(NT):
                rows_out(2, t)
            hi(8 + 7)
            act.wait_ge(s_hn, NT)
            for j in range(KW):
                for h in range(2):
                    act.wait_ge(s_mm, Unit(U_CC + j).half(h))
                    sc.activation(ccT[:, j, half_rows(h)], bank[2 * (j % 2) + h][:, 0:HALF], ACT.Copy).then_inc(s_free, 1)
                hi(U_CC + KW + j)
            for j in range(KW):
                hi(U_CC + 2 * KW + j)
            def log_terms(h):
                tmp, zb3 = tmp1280[h], z_banks(h)
                if h >= 2:
                    act.wait_ge(s_spr, 3 * (h - 1))
                for i, width in enumerate(widths):
                    act.wait_ge(s_z, 3 * h + i + 1)
                    sc.activation(tmp[:, 512 * i:512 * i + width], zb3[i][:, 0:width], ACT.Abs).then_inc(s_ln1, 1)
                for i, width in enumerate(widths):
                    part_ = tmp[:, 512 * i:512 * i + width]
                    act.wait_ge(s_ln1, 9 * h + i + 1)
                    sc.activation(part_, part_, ACT.Exp, scale=-1.0).then_inc(s_ln1, 1)
                for i, width in enumerate(widths):
                    part_ = tmp[:, 512 * i:512 * i + width]
                    act.wait_ge(s_ln1, 9 * h + i + 4)
                    sc.activation(part_, part_, ACT.Ln, bias=1.0).then_inc(s_ln1, 1)

            for j in range(KW):
                if j == KW - 1:
                    log_terms(0)
                split_hi(act, Unit(U_C + j), j % 2 == 1)
                act.wait_ge(s_free, F_CC + 4 * KW + 2 * j + 2)
                sc.activation(ch[:, j], ccT[:, j], ACT.Copy).then_inc(s_ch, 1)

            act.wait_ge(s_cl, KW)
            act.wait_ge(s_cpk, 1 + KW)
            act.wait_ge(s_ncvo, 32)
            for h in range(H + 1):
                if 0 < h < H:
                    log_terms(h)
                if h > 0:
                    a, zb3 = a1280[h - 1], z_banks(h - 1)
                    if h >= 3:
                        act.wait_ge(s_av, h - 2)
                    for i, width in enumerate(widths):
                        act.wait_ge(s_acc, 3 * h - 2 + i)
                        sc.activation(a[:, 512 * i:512 * i + width], zb3[i][:, 0:width], ACT.Exp).then_inc(s_ea, 1)
                if h in (3, 5, 7):
                    pair = (h - 3) // 2
                    act.wait_ge(s_av, 2 * pair + 2)
                    sc.activation(ah[:, pair, 0:TP], pair_bank(pair)[:, :], ACT.Copy).then_inc(s_ah, 1)
            act.wait_ge(s_av, H)
            sc.activation(ah[:, HP - 1, 0:TP], pair_bank(HP - 1)[:, :], ACT.Copy).then_inc(s_ah, 1)

            def keys_out(b, i):
                act.wait_ge(s_kt, 4 * b + 2 * i + 1)
                if not (is_zero(b) and i == 0):
                    act.wait_ge(s_zs, 2 * b + i)
                sc.activation(ktc[:, 0], bank[0][:, :].rearrange("p (h t) -> p h t", h=HP), ACT.Copy).then_inc(s_kta, 1)

            def logs(b, par):
                zs, zn = bank[2 + par][:, :], small[par][0:TS, 0:P]
                act.wait_ge(s_zs, 2 * b + 2)
                if not is_zero(b):
                    act.wait_ge(s_sps, 2 * b)
                sc.activation(tms[:], zs, ACT.Abs).then_inc(s_lns, 1)
                sc.activation(tmpn[:], zn, ACT.Abs).then_inc(s_lns, 1)
                act.wait_ge(s_lns, 6 * b + 2)
                sc.activation(tms[:], tms[:], ACT.Exp, scale=-1.0).then_inc(s_lns, 1)
                sc.activation(tmpn[:], tmpn[:], ACT.Exp, scale=-1.0).then_inc(s_lns, 1)
                act.wait_ge(s_lns, 6 * b + 4)
                sc.activation(tms[:], tms[:], ACT.Ln, bias=1.0).then_inc(s_lns, 1)
                sc.activation(tmpn[:], tmpn[:], ACT.Ln, bias=1.0).then_inc(s_lns, 1)

            def weights(b, par):
                act.wait_ge(s_accs, b + 1)
                if not is_zero(b):
                    act.wait_ge(s_avs, b)
                sc.activation(a_s[:], bank[2 + par][:, :], ACT.Exp).then_inc(s_eas, 1)
                sc.activation(an[:, :], small[par][0:TS, 0:P], ACT.Exp).then_inc(s_eas, 1)

            def gate(c, h):
                act.wait_ge(s_mm, gate_unit(c).half(h))
                if not is_zero(c):
                    act.wait_ge(s_br, 2 * number(c))
                sc.activation(sg[:, half_rows(h)], bank[5 + h][:, 0:HALF], ACT.Sigmoid).then_inc(s_gate, 1)

            def sequence(b, c, par):
                keys_out(b, 0)
                if not is_zero(b):
                    weights(b - 1, 1 - par)
                gate(c, 0)
                keys_out(b, 1)
                gate(c, 1)
                logs(b, par)
                split_hi(act, gate_unit(later(c, 2)))
                split_hi(act, gate_unit(later(c, 2)).plus(1), True)

            sequence(0, 0, 0)
            sequence(1, 1, 1)
            with act.Fori(1, 4) as i:
                sequence(2 * i, (i, 0), 0)
                sequence(2 * i + 1, (i, 1), 1)
            weights(B - 1, 1)
            gate(8, 0)
            gate(8, 1)
            act.wait_ge(s_af, 2 * B)
            sc.activation(ah[:, :, TP:T], af[:, :, :], ACT.Copy).then_inc(s_ah, 1)
            split_hi(act, gate_unit(10))
            split_hi(act, gate_unit(10).plus(1), True)

            def block_gates(c):
                gate(c, 0)
                gate(c, 1)
                split_hi(act, gate_unit(later(c, 2)))
                split_hi(act, gate_unit(later(c, 2)).plus(1), True)

            block_gates(9)
            with act.Fori(5, NB // 2 - 1) as i:
                block_gates((i, 0))
                block_gates((i, 1))

            def merged_hi(k):
                act.wait_ge(s_m, 2 * k + 2)
                sc.activation(hh[:, k], m[:, k], ACT.Copy).then_inc(s_mh, 1)

            for c in (NB - 2, NB - 1):
                gate(c, 0)
                gate(c, 1)
                hi(U_C + 2 * c + 4)
                if c == NB - 2:
                    hi(U_C + 2 * c + 5)
            for k in range(KD - 2):
                merged_hi(k)
            hi(U_D + 3)
            merged_hi(KD - 2)
            merged_hi(KD - 1)
            for i in range(4, 8):
                hi(U_D + i)
            for t in range(NT):
                act.wait_ge(s_tr, G_PLE + t + 1)
                sc.activation(ph[:, :, t * P:(t + 1) * P], ring_bank(G_PLE + t)[:, 0:2 * P].rearrange(
                    "p (k t) -> p k t", k=2), ACT.Copy).then_inc(s_trh, 1)
            for t in range(NT):
                if t == NT - 1:
                    hi(U_P)
                square(NT + t, junk2, s_free, F_D + NT + t + 1)
            for i in range(1, 4):
                hi(U_P + i)
            for n in range(2):
                for t in range(NT):
                    act.wait_ge(s_mm, 5 * (U_P + n) + t + 1)
                    sc.activation(pp[:, t, n * W:(n + 1) * W], bank[t][:, :], ACT.Copy).then_inc(s_free, 1)
                hi(U_P + n + 4)
                if n == 0:
                    act.wait_ge(s_d, 1)
                    sc.activation(gexp[:], gdiff[:], ACT.Exp).then_inc(s_rx, 1)
                    act.wait_ge(s_d, 2)
                    sc.activation(vexp[:], vdiff[:], ACT.Exp).then_inc(s_rx, 1)

            def rows_hi(e):
                for half in range(2):
                    act.wait_ge(s_xt, 2 * e + half + 1)
                    sc.activation(xh[:, 4 * half:4 * half + 4], bank[4 + half][:, :].rearrange("p (k t) -> p k t", k=4),
                                  ACT.Copy).then_inc(s_xh, 1)

            def silu(e, last_gate_unit):
                act.wait_ge(s_mm, last_gate_unit.mm())
                act.wait_ge(s_hm, e)
                sc.activation(si[:, :], bank[0][:, :], ACT.Silu).then_inc(s_si, 1)

            def hidden_hi(e):
                act.wait_ge(s_ht, e + 1)
                sc.activation(mh[:, :, :], bank[6][:, :].rearrange("p (k t) -> p k t", k=4), ACT.Copy).then_inc(s_hth, 1)

            def out_rows(n, e, par, turn, unit):
                act.wait_ge(s_mm, unit.mm())
                act.wait_ge(s_yo[par], 16 * turn)
                sc.activation(y[:, par, n * W:(n + 1) * W], bank[2 + n][:, :], ACT.Copy).then_inc(s_y, 1)

            rows_hi(0)
            for j in range(4, 8):
                hi(U_M + j)
            silu(0, Unit(U_M + 3))
            for j in range(8, 12):
                hi(U_M + j)
            rows_hi(1)

            def expert_scalar(e, par, turn, rows_next=True):
                u = lambda j: Unit(U_M - 4 + j, NSTREAM, e)
                for j in range(4, 8):
                    split_hi(act, u(j))
                hidden_hi(e - 1)
                silu(e, u(3))
                for j in range(8, 12):
                    split_hi(act, u(j))
                if rows_next:
                    rows_hi(e + 1)
                split_hi(act, u(12))
                split_hi(act, u(13))
                out_rows(0, e - 1, 1 - par, turn, u(9))
                split_hi(act, u(14))
                split_hi(act, u(15))
                out_rows(1, e - 1, 1 - par, turn, u(11))

            expert_scalar(1, 1, 0)
            expert_scalar(2, 0, 0)
            with act.Fori(1, NE // 2 - 1) as i:
                expert_scalar(2 * i + 1, 1, i)
                expert_scalar(2 * i + 2, 0, i)
            expert_scalar(NE - 1, 1, NE // 2 - 1, rows_next=False)
            hidden_hi(NE - 1)
            out_rows(0, NE - 1, 1, NE // 2 - 1, Unit(U_G - 3))
            out_rows(1, NE - 1, 1, NE // 2 - 1, Unit(U_G - 1))

            act.wait_ge(s_flag, 1)
            over = act.value_load(flag[0:1, 0:1], min_val=0, max_val=1)
            with act.If(over > 0):
                act.wait_ge(s_yo[0], 16 * NE // 2)
                act.wait_ge(s_hm, NE)
                sc.activation(si[:, 0:1], ss[:, 0:1], ACT.Copy).then_inc(s_o_act, 3)
                act.wait_ge(s_o_act, 3)
                with act.Fori(0, NE * OV_TILES) as o:
                    act.wait_ge(s_o_pe, 14 * o + 5)
                    sc.activation(si[:, :], bank[0][:, :], ACT.Silu).then_inc(s_o_act, 1)
                    act.wait_ge(s_o_free, o + 1)
                    for n in range(2):
                        act.wait_ge(s_o_pe, 14 * o + 12 + 2 * n)
                        sc.activation(y[:, 0, n * W:(n + 1) * W], bank[2 + n][:, :], ACT.Copy).then_inc(s_o_act, 1)

            for i in range(4):
                hi(U_G + i)
            def gates(n, t):
                i = n * NT + t
                act.wait_ge(s_mm, tile_done(U_G + 4 * n, t, n == 0))
                if i >= 4:
                    act.wait_ge(s_out[i % 4], 16 * (i // 4))
                sc.activation(eo[:, i % 4], bank[t][:, :], ACT.Sigmoid).then_inc(s_free, 1)

            square(2 * NT, junk3, s_yu, 2)
            for t in range(NT):
                if t + 1 < NT:
                    square(2 * NT + t + 1, junk3, s_yu, 2 * t + 4)
                if t >= 2:
                    gates(0, t - 2)
                for half in range(2):
                    norm_hi(G_F + 2 * t + half, t, half)
            gates(0, NT - 2)
            for i in range(4, 7):
                hi(U_G + i)
            gates(0, NT - 1)
            hi(U_G + 7)
            for t in range(NT):
                gates(1, t)

        @block.vector
        def _(dve):
            ve = nc.vector
            lo = lambda u: split_lo(dve, Unit(u))
            step = [0]

            def link(ins):
                step[0] += 1
                ins.then_inc(s_vc, 1)
                dve.wait_ge(s_vc, step[0])

            def tt(out, a, b, op):
                return ve.tensor_tensor(out=out, in0=a, in1=b, op=op)

            def norm_rows(i, out):
                dve.wait_ge(s_r, i + 1)
                return ve.scalar_tensor_tensor(out=out, in0=x[:, i % NT], scalar=rr[:, i:i + 1], in1=lnb[:, :],
                                               op0=ALU.mult, op1=ALU.mult)

            def norm_lo(g, t, half):
                dve.wait_ge(s_trh, trh(g))
                dst = (slice(4 * half, 4 * half + 4), slice(t * P, (t + 1) * P))
                tt(hl[:, dst[0], dst[1]], ring_bank(g)[:, :].rearrange("p (k t) -> p k t", k=4),
                   hh[:, dst[0], dst[1]].bitcast(F32), ALU.subtract).then_inc(s_trf, 1)

            def trh(g):
                return g + 1 if g < 10 else 10 + g - G_PLE + 1 if g < G_R else 15 + g - G_F + 1

            dve.wait_ge(s_ln, 16)
            def x_rows(t):
                if t >= 2:
                    dve.wait_ge(s_tr, 2 * (t - 2) + 2)
                norm_rows(t, hn[:, t % 2]).then_inc(s_hn, 1)

            def x_lo(t):
                norm_lo(2 * t, t, 0)
                norm_lo(2 * t + 1, t, 1)

            def head_sums(n):
                dve.wait_ge(s_qsq, n + 1)
                ve.tensor_reduce(out=ssq[:, n], in_=sqb[:, 0].rearrange("p (h d) -> p h d", h=H), axis=AX.X,
                                 op=ALU.add).then_inc(s_ssq, 1)

            def head_scaled(n):
                dve.wait_ge(s_rq, n + 1)
                if n:
                    dve.wait_ge(s_qn2, n)
                tt(qn1[:, 0].rearrange("p (h d) -> p h d", h=H), zb[:, n % 2].rearrange("p (h d) -> p h d", h=H),
                   rq[:, n, :, None].to_broadcast([P, H, HD]), ALU.mult).then_inc(s_qn1, 1)

            def head_normed(n):
                if n >= 2:
                    dve.wait_ge(s_tr, G_QK + n - 1)
                if n >= NT + 2:
                    dve.wait_ge(s_ko[n % 2], 16 * ((n - NT) // 2))
                dve.wait_ge(s_qn1, n + 1)
                tt(qn2[:, n % 2].rearrange("p (h d) -> p h d", h=H), qn1[:, 0].rearrange("p (h d) -> p h d", h=H),
                   qkg[:, n // NT, None, :].to_broadcast([P, H, HD]), ALU.mult).then_inc(s_qn2, 1)

            def qk_out(n):
                g = G_QK + n
                dve.wait_ge(s_tr, g + 1)
                dst = (qT if n < NT else kT)[:, :, (n % NT) * P:(n % NT + 1) * P]
                ve.tensor_copy(dst, ring_bank(g)[:, :].rearrange("p (j t) -> p j t", j=KW)).then_inc(s_trf, 1)

            x_rows(0)
            lo(0)
            x_lo(0)
            lo(1)
            x_rows(1)
            lo(2)
            lo(3)
            x_rows(2)
            x_lo(1)
            x_rows(3)
            x_lo(2)
            x_rows(4)
            head_sums(0)
            x_lo(3)
            head_scaled(0)
            head_normed(0)
            head_sums(1)
            x_lo(4)
            head_scaled(1)
            head_normed(1)
            head_sums(2)
            dve.wait_ge(s_sq, NT)
            dve.wait_ge(s_tr, G_STATE + 1)
            ve.tensor_copy(us[:, :, :, 0:2], ring_bank(G_STATE)[:, 0:KW * 2 * B].rearrange(
                "p (j b s) -> p j b s", j=KW, s=2)).then_inc(s_trf, 1)

            lo(4)
            head_scaled(2)
            for i in range(5, 8):
                lo(i)
            for n in range(2 * NT - 5):
                qk_out(n)
                head_normed(n + 2)
                head_sums(n + 3)
                head_scaled(n + 3)
            for i in range(4, 8):
                lo(4 + i)
            for n in range(2 * NT - 5, 2 * NT - 3):
                qk_out(n)
                head_normed(n + 2)
                head_sums(n + 3)
                head_scaled(n + 3)
            qk_out(2 * NT - 3)
            head_normed(2 * NT - 1)
            for i in range(4, 7):
                lo(8 + i)
            qk_out(2 * NT - 2)
            qk_out(2 * NT - 1)
            lo(8 + 7)

            def conv(j):
                outs = (yc[:, j, 0:TP], yc[:, j, TP:T].rearrange("p (b s) -> p b s", b=B))
                ins_ = (lambda s: up[:, j, s:s + TP], lambda s: us[:, j, :, s:s + TS])
                for s in range(3):
                    for n in range(2):
                        if s == 0:
                            ins = ve.tensor_scalar(outs[n], ins_[n](0), convw[:, 0, j:j + 1], None, ALU.mult)
                        else:
                            ins = ve.scalar_tensor_tensor(out=outs[n], in0=ins_[n](s), scalar=convw[:, s, j:j + 1],
                                                          in1=outs[n], op0=ALU.mult, op1=ALU.add)
                    link(ins)

            for j in range(KW):
                lo(U_CC + KW + j)
            dve.wait_ge(s_free, F_CC + 2 * KW)
            dve.wait_ge(s_made, 16)
            dve.wait_ge(s_const, 16 * 9)
            for j in range(KW):
                u = Unit(U_CC + KW + j)
                b0, b1 = bank[2 * (j % 2)], bank[2 * (j % 2) + 1]
                dve.wait_ge(s_mm, u.half(0))
                tt(up[:, j, 2:2 + HALF], b0[:, 0:HALF], ccT[:, j, 0:HALF], ALU.mult).then_inc(s_free, 1)
                dve.wait_ge(s_mm, u.half(1))
                tt(up[:, j, 2 + HALF:2 + TP], b1[:, 0:TP - HALF], ccT[:, j, HALF:TP], ALU.mult)
                tt(us[:, j, :, 2:2 + TS], b1[:, TP - HALF:HALF].rearrange("p (b s) -> p b s", b=B),
                   ccT[:, j, TP:T].rearrange("p (b s) -> p b s", b=B), ALU.mult).then_inc(s_free, 1)
                dve.wait_ge(s_free, F_CC + 2 * KW + 2 * j + 2)
                conv(j)
                lo(U_CC + 2 * KW + j)

            def conv_lo(j):
                dve.wait_ge(s_ch, j + 1)
                tt(cl[:, j], ccT[:, j], ch[:, j].bitcast(F32), ALU.subtract).then_inc(s_cl, 1)

            def softplus_of(h):
                tmp, out, zb3 = tmp1280[h], sp1280[h], z_banks(h)
                if h >= 2:
                    dve.wait_ge(s_acc, 3 * h - 3)
                for i, width in enumerate(widths):
                    dve.wait_ge(s_ln1, 9 * h + i + 7)
                    ve.scalar_tensor_tensor(out=out[:, 512 * i:512 * i + width], in0=zb3[i][:, 0:width], scalar=0.0,
                                            in1=tmp[:, 512 * i:512 * i + width], op0=ALU.max, op1=ALU.add
                                            ).then_inc(s_spr, 1)

            for j in range(KW):
                for h in range(2):
                    dve.wait_ge(s_mm, Unit(U_CC + 2 * KW + j).half(h))
                    tt(ccT[:, j, half_rows(h)], bank[2 * (j % 2) + h][:, 0:HALF], yc[:, j, half_rows(h)], ALU.mult
                       ).then_inc(s_free, 1)
                if j == KW - 1:
                    softplus_of(0)
                split_lo(dve, Unit(U_C + j), j % 2 == 1)
                conv_lo(j)
                if j == 1:
                    dve.wait_ge(s_tr, G_CONV + 1)
                    ve.tensor_copy(ncv[:, :], ring_bank(G_CONV)[0:2 + 2 * B, :]).then_inc(s_trf, 1)

            dve.wait_ge(s_cl, KW)
            for h in range(H):
                out = sp1280[h]
                if h:
                    softplus_of(h)
                dve.wait_ge(s_sp, 4 * h + 4)
                if h:
                    dve.wait_ge(s_acc, 3 * h)
                ve.tensor_copy(later1[:, 0:P], out[:, 1024:1152]).then_inc(s_later, 1)
                tt(later1[:, P:], out[:, 1152:1280], out[:, 896:1024], ALU.add).then_inc(s_later, 1)
                ve.tensor_copy(later0[:, 0:P], out[:, 512:640]).then_inc(s_later, 1)
                dve.wait_ge(s_later, 4 * h + 2)
                tt(later0[:, P:], out[:, 640:896], later1[:, :], ALU.add).then_inc(s_later, 1)
                if h in (3, 5, 7):
                    pair = (h - 3) // 2
                    dve.wait_ge(s_ah, pair + 1)
                    tt(al[:, pair, 0:TP], pair_bank(pair)[:, :], ah[:, pair, 0:TP].bitcast(F32), ALU.subtract
                       ).then_inc(s_al, 1)
            dve.wait_ge(s_ah, HP)
            tt(al[:, HP - 1, 0:TP], pair_bank(HP - 1)[:, :], ah[:, HP - 1, 0:TP].bitcast(F32), ALU.subtract
               ).then_inc(s_al, 1)

            def keys_out(b, i):
                dve.wait_ge(s_kt, 4 * b + 2 * i + 2)
                if not (is_zero(b) and i == 0):
                    dve.wait_ge(s_zs, 2 * b + i)
                ve.tensor_copy(ktc[:, 1], bank[1][:, :].rearrange("p (h t) -> p h t", h=HP)).then_inc(s_ktv, 1)

            def softplus(b, par):
                dve.wait_ge(s_lns, 6 * b + 6)
                if not is_zero(b):
                    dve.wait_ge(s_accs, b)
                for out, z, tmp in ((sps[:], bank[2 + par][:, :], tms[:]),
                                    (spn_rows[0:TS], small[par][0:TS, 0:P], tmpn[:])):
                    ve.scalar_tensor_tensor(out=out, in0=z, scalar=0.0, in1=tmp, op0=ALU.max, op1=ALU.add
                                            ).then_inc(s_sps, 1)
                dve.wait_ge(s_spn, b + 1)
                for kb in range(KB - 2, -1, -1):
                    last = spn_rows[:, :] if kb == KB - 2 else spl[:, kb + 1]
                    if kb < KB - 2:
                        dve.wait_ge(s_spl, 3 * b + KB - 2 - kb)
                    tt(spl[:, kb], last, sps[:, (kb + 1) * P:(kb + 2) * P], ALU.add).then_inc(s_spl, 1)

            def keep(b, par):
                dve.wait_ge(s_avs, b + 1)
                o = small[par][:, P:2 * P].rearrange("p (h q) -> p h q", h=HP)
                ve.tensor_copy(af[0:HD, :, bass.ds(b * TS, TS)], o[0:HD, :, 0:TS]).then_inc(s_af, 1)
                ve.tensor_copy(af[HD:P, :, bass.ds(b * TS, TS)], o[HD:P, :, TS:]).then_inc(s_af, 1)

            def gated(c, h, out):
                dve.wait_ge(s_gate, 2 * number(c) + 2)
                dve.wait_ge(s_mm, gate_unit(c).plus(1).half(h))
                tt(out, bank[5 + h][:, 0:HALF], sg[:, half_rows(h)], ALU.mult).then_inc(s_br, 1)

            dve.wait_ge(s_av, H)
            ve.tensor_copy(qs[:], qT[:, :, TP:T]).then_inc(s_qs, 1)
            ve.tensor_copy(ks[:], kT[:, :, TP:T]).then_inc(s_qs, 1)
            dve.wait_ge(s_qs, 2)

            def place(b, par):
                if not isinstance(b, int):
                    dve.wait_ge(s_accs, b - 1)
                q_b = qs[:, :, bass.ds(b * TS, TS)]
                ve.tensor_copy(qbd[0:HD, par, :, 0:TS], q_b[0:HD]).then_inc(s_qb, 1)
                ve.tensor_copy(qbd[HD:P, par, :, TS:], q_b[HD:P]).then_inc(s_qb, 1)
                ve.tensor_copy(ktb[:, par], ks[:, :, bass.ds(b * TS, TS)]).then_inc(s_qb, 1)

            def sequence(b, c, par):
                place(b, par)
                keys_out(b, 0)
                keys_out(b, 1)
                for h in range(2):
                    gated(c, h, m[:, bass.ds(number(c), 1), half_rows(h)].rearrange("p o t -> p (o t)"))
                softplus(b, par)
                if not is_zero(b):
                    keep(b - 1, 1 - par)
                split_lo(dve, gate_unit(later(c, 2)))
                split_lo(dve, gate_unit(later(c, 2)).plus(1), True)

            sequence(0, 0, 0)
            sequence(1, 1, 1)
            with dve.Fori(1, 4) as i:
                sequence(2 * i, (i, 0), 0)
                sequence(2 * i + 1, (i, 1), 1)
            keep(B - 1, 1)
            dve.wait_ge(s_ah, HP + 1)
            tt(al[:, :, TP:T], af[:, :, :], ah[:, :, TP:T].bitcast(F32), ALU.subtract).then_inc(s_al, 1)

            def merged(c):
                if not (isinstance(c, int) and c == KD):
                    dve.wait_ge(s_m, 2 * number(c) - 2 * KD)
                for h in range(2):
                    gated(c, h, mt[:, half_rows(h)])
                for h in range(2):
                    dve.wait_ge(s_br, 2 * number(c) + h + 1)
                    out = m[:, bass.ds(number(c) - KD, 1), half_rows(h)].rearrange("p o t -> p (o t)")
                    tt(out, out, mt[:, half_rows(h)], ALU.add).then_inc(s_m, 1)

            def merged_block(c):
                split_lo(dve, gate_unit(later(c, 2)))
                merged(c)
                split_lo(dve, gate_unit(later(c, 2)).plus(1), True)

            def merged_lo(k):
                dve.wait_ge(s_mh, k + 1)
                tt(hl[:, k], m[:, k], hh[:, k].bitcast(F32), ALU.subtract).then_inc(s_ml, 1)

            merged_block(8)
            merged_block(9)
            with dve.Fori(5, NB // 2 - 1) as i:
                merged_block((i, 0))
                merged_block((i, 1))
            lo(U_D)
            merged(NB - 2)
            lo(U_D + 1)
            lo(U_D + 2)
            for k in range(2):
                merged_lo(k)
            merged(NB - 1)
            for k in range(2, KD - 2):
                merged_lo(k)
            lo(U_D + 3)
            merged_lo(KD - 2)
            merged_lo(KD - 1)

            def x_add(n, t):
                dve.wait_ge(s_mm, tile_done(U_D + 4 * n, t, n == 1))
                tt(x[:, t, n * W:(n + 1) * W], x[:, t, n * W:(n + 1) * W], bank[t][:, :], ALU.add).then_inc(s_free, 1)

            def h2_out(t):
                for half in range(2):
                    g = G_R + 2 * t + half
                    dve.wait_ge(s_tr, g + 1)
                    ve.tensor_copy(h2T[:, 4 * half:4 * half + 4, t * P:(t + 1) * P],
                                   ring_bank(g)[:, :].rearrange("p (k t) -> p k t", k=4)).then_inc(s_trf, 1)

            for i in range(4, 7):
                lo(U_D + i)
            dve.wait_ge(s_xr, 16 * NT)
            for t in range(NT):
                x_add(0, t)
            lo(U_D + 7)
            for t in range(NT):
                g = G_PLE + t
                dve.wait_ge(s_trh, trh(g))
                tt(pl[:, :, t * P:(t + 1) * P], ring_bank(g)[:, 0:2 * P].rearrange("p (k t) -> p k t", k=2),
                   ph[:, :, t * P:(t + 1) * P].bitcast(F32), ALU.subtract).then_inc(s_trf, 1)
            dve.wait_ge(s_ln, 32)
            for t in range(NT):
                if t >= 2:
                    h2_out(t - 2)
                if t == NT - 1:
                    lo(U_P)
                x_add(1, t)
                norm_rows(NT + t, h2[:, t]).then_inc(s_hn, 1)
            h2_out(NT - 2)
            lo(U_P + 1)
            h2_out(NT - 1)
            lo(U_M)
            lo(U_M + 1)

            def bc(a, n):
                return a[:, :, None].to_broadcast([P, NT, n])

            def top(logits, vmax, choice):
                link(ve.tensor_reduce(out=vmax[:], in_=logits, axis=AX.X, op=ALU.max))
                link(tt(cand[:], logits, bc(vmax, 4), ALU.is_ge))
                link(tt(cand[:], cand[:], desc[:, None, :].to_broadcast([P, NT, 4]), ALU.mult))
                link(ve.tensor_reduce(out=cm1[:], in_=cand[:], axis=AX.X, op=ALU.max))
                link(tt(choice, cand[:], bc(cm1, 4), ALU.is_equal))

            dve.wait_ge(s_rt, 1)
            link(tt(lg[:], bank[6][:, 0:NT * (NG + NE)].rearrange("p (t n) -> p t n", t=NT),
                    rbias[:, None, :].to_broadcast([P, NT, NG + NE]), ALU.add))
            top(lg[:, :, 0:NG], gmax, og[:])
            tt(gdiff[:], lg[:, :, 0:NG], bc(gmax, NG), ALU.subtract).then_inc(s_d, 1)
            link(tt(prod[:], lg[:, :, NG:].rearrange("p t (g j) -> p t j g", g=NG),
                    og[:, :, None, :].to_broadcast([P, NT, EG, NG]), ALU.mult))
            link(ve.tensor_reduce(out=lsel[:], in_=prod[:], axis=AX.X, op=ALU.add))
            top(lsel[:], v1, ok[:, 0])
            link(ve.scalar_tensor_tensor(out=lsel2[:], in0=ok[:, 0], scalar=-3.0e38, in1=lsel[:], op0=ALU.mult,
                                         op1=ALU.add))
            top(lsel2[:], v2, ok[:, 1])
            tt(vdiff[:], v2[:], v1[:], ALU.subtract).then_inc(s_d, 1)
            for k in range(2):
                ins = tt(Mk[:, k].rearrange("p t (g j) -> p t g j", g=NG), og[:, :, :, None].to_broadcast([P, NT, NG, EG]),
                         ok[:, k, :, None, :].to_broadcast([P, NT, NG, EG]), ALU.mult)
            link(ins)
            tt(Mb[:], Mk[:, 0], Mk[:, 1], ALU.add).then_inc(s_M, 1)
            dve.wait_ge(s_rx, 2)
            ve.tensor_reduce(out=gsum[:], in_=gexp[:], axis=AX.X, op=ALU.add)
            link(ve.tensor_scalar(vsum[:], vexp[:], 1.0, None, ALU.add))
            link(tt(gsum[:], gsum[:], vsum[:], ALU.mult))
            link(ve.reciprocal(gate[:, 0], gsum[:]))
            link(tt(gate[:, 1], gate[:, 0], vexp[:], ALU.mult))
            dve.wait_ge(s_rk, 1)
            link(ve.tensor_copy(rk[:], bank[6][:, P:P + NT * NE].rearrange("p (t e) -> p t e", t=NT)))
            for k in range(2):
                ins = tt(mr[:, k], Mk[:, k], rk[:], ALU.mult)
            link(ins)
            link(ve.tensor_reduce(out=slotf[:, 0], in_=mr[:], axis=AX.X, op=ALU.add))
            link(tt(mr[:].rearrange("p k t e -> p (k t) e"), Mk[:].rearrange("p k t e -> p (k t) e"),
                    eidx[:, None, :].to_broadcast([P, 2 * NT, NE]), ALU.mult))
            link(ve.tensor_reduce(out=slotf[:, 1], in_=mr[:], axis=AX.X, op=ALU.add))
            link(ve.tensor_scalar(slotf[:, 2], slotf[:, 0], float(C), None, ALU.is_ge))
            ve.tensor_reduce(out=ovm[:], in_=slotf[:, 2], axis=AX.XY, op=ALU.max).then_inc(s_ovm, 1)
            link(ve.tensor_scalar(slotf[:, 3], slotf[:, 1], float(T - 2 * C), float((NE - 1) * C), ALU.mult, ALU.add))
            link(tt(slotf[:, 3], slotf[:, 3], slotf[:, 2], ALU.mult))
            link(ve.scalar_tensor_tensor(out=slotf[:, 0], in0=slotf[:, 1], scalar=float(C), in1=slotf[:, 0],
                                         op0=ALU.mult, op1=ALU.add))
            tt(slot[:], slotf[:, 0], slotf[:, 3], ALU.add).then_inc(s_slot, 1)
            dve.wait_ge(s_ov, 1)
            ve.tensor_scalar(flag[0:1, 0:1], bank[7][0:1, 0:1], 1.0, None, ALU.min).then_inc(s_flag, 1)
            lo(U_M + 2)
            lo(U_M + 3)

            def rows_lo(e):
                for half in range(2):
                    dve.wait_ge(s_xh, 2 * e + half + 1)
                    tt(xl[:, 4 * half:4 * half + 4], bank[4 + half][:, :].rearrange("p (k t) -> p k t", k=4),
                       xh[:, 4 * half:4 * half + 4].bitcast(F32), ALU.subtract).then_inc(s_xl, 1)

            def hidden(e, last_up_unit):
                dve.wait_ge(s_mm, last_up_unit.mm())
                dve.wait_ge(s_si, e + 1)
                dve.wait_ge(s_ht, e)
                tt(hm[:, :], bank[1][:, :], si[:, :], ALU.mult).then_inc(s_hm, 1)

            def hidden_lo(e):
                dve.wait_ge(s_hth, e + 1)
                tt(ml[:, :, :], bank[6][:, :].rearrange("p (k t) -> p k t", k=4), mh[:, :, :].bitcast(F32),
                   ALU.subtract).then_inc(s_htl, 1)

            rows_lo(0)
            for j in range(4, 11):
                lo(U_M + j)
            hidden(0, Unit(U_M + 7))
            lo(U_M + 11)
            rows_lo(1)

            def expert_vector(e, rows_next=True):
                u = lambda j: Unit(U_M - 4 + j, NSTREAM, e)
                for j in range(4, 8):
                    split_lo(dve, u(j))
                hidden_lo(e - 1)
                for j in range(8, 11):
                    split_lo(dve, u(j))
                hidden(e, u(7))
                split_lo(dve, u(11))
                if rows_next:
                    rows_lo(e + 1)
                for j in range(12, 16):
                    split_lo(dve, u(j))

            with dve.Fori(1, NE - 1) as e:
                expert_vector(e)
            expert_vector(NE - 1, rows_next=False)
            hidden_lo(NE - 1)

            dve.wait_ge(s_flag, 1)
            over = dve.value_load(flag[0:1, 0:1], min_val=0, max_val=1)
            with dve.If(over > 0):
                ve.memset(cm1[:], 0.0).then_inc(s_o_dve, 3)
                with dve.Fori(0, NE * OV_TILES) as o:
                    dve.wait_ge(s_o_pe, 14 * o + 1)
                    for half in range(2):
                        ins = ve.tensor_copy(oxT[:, 4 * half:4 * half + 4],
                                             bank[4 + half][:, :].rearrange("p (k t) -> p k t", k=4))
                    ins.then_inc(s_o_dve, 1)
                    dve.wait_ge(s_o_pe, 14 * o + 9)
                    dve.wait_ge(s_o_act, 3 * o + 4)
                    tt(hm[:, :], bank[1][:, :], si[:, :], ALU.mult).then_inc(s_o_dve, 1)
                    dve.wait_ge(s_o_pe, 14 * o + 10)
                    ve.tensor_copy(omT[:, :, :], bank[6][:, :].rearrange("p (k t) -> p k t", k=4)).then_inc(s_o_dve, 1)

            for i in range(4):
                lo(U_G + i)
            dve.wait_ge(s_ln, 48)
            def rows_added(t):
                for k in range(2):
                    i = 2 * t + k
                    dve.wait_ge(s_yg[i % NYG], 16 * (i // NYG + 1))
                    dve.wait_ge(s_yu, i)
                    ve.scalar_tensor_tensor(out=x[:, t], in0=yg[:, i % NYG], scalar=gate[:, k, t:t + 1], in1=x[:, t],
                                            op0=ALU.mult, op1=ALU.add).then_inc(s_yu, 1)

            def rows3_lo(t):
                for half in range(2):
                    norm_lo(G_F + 2 * t + half, t, half)

            def result(n, t):
                i = n * NT + t
                cols = slice(n * W, (n + 1) * W)
                dve.wait_ge(s_free, F_G + i + 1)
                link(tt(eo[:, i % 4], eo[:, i % 4], pp[:, t, cols], ALU.mult))
                tt(eo[:, i % 4], eo[:, i % 4], x[:, t, cols], ALU.add).then_inc(s_eo, 1)

            rows_added(0)
            for t in range(NT):
                if t + 1 < NT:
                    rows_added(t + 1)
                if t >= 2:
                    dve.wait_ge(s_tr, G_F + 2 * (t - 2) + 2)
                norm_rows(2 * NT + t, hn3[:, t % 2]).then_inc(s_hn, 1)
                if t >= 1:
                    rows3_lo(t - 1)
                if t >= 3:
                    result(0, t - 3)
            rows3_lo(NT - 1)
            result(0, NT - 3)
            result(0, NT - 2)
            for i in range(4, 7):
                lo(U_G + i)
            result(0, NT - 1)
            lo(U_G + 7)
            for t in range(NT):
                result(1, t)

        @block.tensor
        def _(pe):
            def tr(g, pairs):
                if g >= 3:
                    pe.wait_ge(s_trf, g if g == G_R else g - 1 if G_R < g < G_F else g - 2)
                for out, src, idn in pairs:
                    ins = pe.transpose(out, src, idn)
                ins.then_inc(s_tr, 1)

            def tr_rows(g, src, n=4):
                tr(g, [(ring_bank(g)[:, q * P:(q + 1) * P], src[:, q * P:(q + 1) * P], ident[:, :]) for q in range(n)])

            def natural(u0, nu, free, a_hi, a_lo, before_unit=None, before_tile=None):
                for i in range(nu):
                    u = Unit(u0 + i)
                    pe.wait_ge(s_lo, u.count())
                    if before_unit:
                        before_unit(i)
                    for t in range(NT):
                        if i == 0 and free > 0:
                            pe.wait_ge(s_free, free - NT + t + 1)
                        if before_tile:
                            before_tile(i, t)
                        for kk in range(2):
                            k = 2 * i + kk
                            a = (slice(0, P), k, slice(t * P, (t + 1) * P))
                            ins = three(pe, bank[t][:, :], a_hi[a], a_lo[a], whi[:, u.slot, kk], wlo[:, u.slot, kk],
                                        i == 0 and kk == 0, i == nu - 1 and kk == 1)
                        ins.then_inc(s_mm, 1)

            def tile_by_tile(u0, free, a_hi, a_lo, between):
                for t in range(NT):
                    for i in range(4):
                        between(t, i)
                        if t == 0:
                            pe.wait_ge(s_lo, u0 + i + 1)
                        if i == 0 and free > 0:
                            pe.wait_ge(s_free, free - NT + t + 1)
                        for kk in range(2):
                            k, u = 2 * i + kk, Unit(u0 + i)
                            a = (slice(0, P), k, slice(t * P, (t + 1) * P))
                            ins = three(pe, bank[t][:, :], a_hi[a], a_lo[a], whi[:, u.slot, kk], wlo[:, u.slot, kk],
                                        k == 0, k == KD - 1)
                        if i == 3 and t < NT - 1:
                            ins.then_inc(s_mm, 1)
                        elif t == NT - 1:
                            ins.then_inc(s_mm, 1 if i == 0 else 5)

            def by_column(u, nk, b_hi, b_lo, h, out):
                pe.wait_ge(s_lo, u.count())
                for k in range(nk):
                    ins = three(pe, out[:, 0:HALF], columns(whi[:, u.slot])[:, k], columns(wlo[:, u.slot])[:, k],
                                b_hi[:, k, half_rows(h)], b_lo[:, k, half_rows(h)], k == 0, k == nk - 1)
                ins.then_inc(s_mm, 2 + h)

            def gate_half(c, h):
                if not is_zero(c):
                    pe.wait_ge(s_br, 2 * number(c) + h - 1)
                by_column(gate_unit(c), KD, hh, hl, h, bank[5 + h])

            def branch_half(c, h, b_hi, b_lo):
                pe.wait_ge(s_gate, 2 * number(c) + h + 1)
                by_column(gate_unit(c).plus(1), KW, b_hi, b_lo, h, bank[5 + h])

            def branch(c, b_hi, b_lo):
                for h in range(2):
                    branch_half(c, h, b_hi, b_lo)

            def x_rows(t):
                pe.wait_ge(s_hn, t + 1)
                for half in range(2):
                    tr_rows(G_X + 2 * t + half, hn[:, t % 2, half * W:(half + 1) * W])

            pe.wait_ge(s_made, 15)
            x_rows(0)

            def x_between(t, i):
                if i == 1 and t + 1 < NT:
                    x_rows(t + 1)
                if i == 0:
                    pe.wait_ge(s_trf, 2 * t + 2)

            tile_by_tile(0, 0, hh, hl, x_between)
            pe.wait_ge(s_state, 16)
            tr(G_STATE, [(ring_bank(G_STATE)[:, j * 2 * B:(j + 1) * 2 * B], st[:, j * P:(j + 1) * P],
                          ident[0:2 * B, 0:2 * B]) for j in range(KW)])

            def qk_rows(first, places):
                def before(a, b):
                    if (a, b) in places:
                        n = first + places.index((a, b))
                        pe.wait_ge(s_qn2, n + 1)
                        tr_rows(G_QK + n, qn2[:, n % 2])
                return before

            tile_by_tile(4, NT, hh, hl, qk_rows(0, ((0, 1), (0, 3), (1, 1), (1, 3), (2, 2), (3, 1), (4, 0))))
            natural(8, 4, 2 * NT, hh, hl, before_tile=qk_rows(7, ((0, 4), (1, 3), (2, 3))))
            region = {0: (0, 0), 1: (1, 0), 2: (2, 0), 3: (1, 384)}
            off = {0: 0, 1: 512, 2: 1024, 3: 896}
            width = [TP - i * P for i in range(4)]

            def zreg(h, i, skip=0):
                bk, o = region[i]
                return z_banks(h)[bk][:, o + skip:o + width[i]]

            def scores(h):
                r = HD * (h % 2)
                for n, i in enumerate((0, 1, 3, 2)):
                    if h >= 2:
                        pe.wait_ge(s_ea, 3 * h - 6 + (1, 2, 2, 3)[n])
                    ins = pe.matmul(zreg(h, i), kT[r:r + HD, h // 2, i * P:(i + 1) * P],
                                    qT[r:r + HD, h // 2, i * P:TP], start=i != 3, stop=False, skip_group_check=True)
                    if i != 1:
                        ins.then_inc(s_z, 1)

            def conv_block(c, j):
                for h in range(2):
                    pe.wait_ge(s_free, 2 * KW * c + F_CC + 2 * j + h - 3)
                    by_column(Unit(U_CC + j, KW, c), KD, hh, hl, h, bank[2 * (j % 2) + h])

            with pe.Fori(0, 2) as c:
                for j in range(KW):
                    conv_block(c, j)
            for j in range(KW):
                conv_block(2, j)
                if j == 1:
                    pe.wait_ge(s_cpk, 1 + KW)
                    tr(G_CONV, [(ring_bank(G_CONV)[0:2 + 2 * B, jj * P:(jj + 1) * P], cpk[:, jj], ident[:, :])
                                for jj in range(KW)])
                if j == KW - 2:
                    pe.wait_ge(s_trf, G_CONV + 1)
                    scores(0)

            def log_sums(h):
                t = sp1280[h]
                pe.wait_ge(s_sp, 4 * h + 4)
                for i in (0, 1, 3, 2):
                    pe.matmul(zreg(h, i), um[:, :], t[:, off[i]:off[i] + width[i]], start=False, stop=i == 3,
                              skip_group_check=True)
                pe.wait_ge(s_later, 4 * h + 4)
                for i, sums in enumerate((later0[:, :], later1[:, :], t[:, off[3]:off[3] + P])):
                    pe.matmul(zreg(h, i, P), neg[:, :], sums, start=False, stop=True, skip_group_check=True
                              ).then_inc(s_acc, 1)

            def values(h):
                r, pair = HD * (h % 2), h // 2
                pe.wait_ge(s_am, 4 * h + 4)
                if pair >= 2:
                    pe.wait_ge(s_al, pair - 1)
                for i in range(4):
                    ins = pe.matmul(pair_bank(pair)[r:r + HD, i * P:TP], v[:, i, h * HD:(h + 1) * HD],
                                    a1280[h][:, off[i]:off[i] + width[i]], start=i == 0, stop=i == 3,
                                    skip_group_check=True)
                ins.then_inc(s_av, 1)

            pe.wait_ge(s_free, F_D)
            for h in range(H):
                if h + 1 < H:
                    scores(h + 1)
                log_sums(h)
                if h:
                    values(h - 1)
            values(H - 1)

            def keys(b, i):
                pe.wait_ge(s_kc[i], 16 * b + 16)
                if not (is_zero(b) and i == 0):
                    pe.wait_ge(s_kta, 2 * b + i)
                    pe.wait_ge(s_ktv, 2 * b + i)
                for kb in range(2):
                    for hp in range(HP):
                        ins = pe.transpose(bank[kb][:, hp * P:(hp + 1) * P], kc[:, 2 * i + kb, hp * P:(hp + 1) * P],
                                           ident[:, :])
                    ins.then_inc(s_kt, 1)

            def scores_of(b, i, par):
                pe.wait_ge(s_kta, 2 * b + i + 1)
                pe.wait_ge(s_ktv, 2 * b + i + 1)
                if i == 0:
                    pe.wait_ge(s_qb, 3 * b + 3)
                    if not isinstance(b, int):
                        pe.wait_ge(s_eas, 2 * b - 2)
                for kb in range(2):
                    for hp in range(HP):
                        o = (2 * i + kb) * P + hp * 2 * TS
                        ins = pe.matmul(bank[2 + par][:, o:o + 2 * TS], ktc[:, kb, hp],
                                        qbd[:, par, hp],
                                        start=i == 0 and kb == 0 and hp == 0, stop=False, skip_group_check=True)
                if i == 1:
                    if not isinstance(b, int):
                        pe.wait_ge(s_af, 2 * b - 2)
                    for hp in range(HP):
                        ins = pe.matmul(small[par][0:TS, hp * 2 * TS:(hp + 1) * 2 * TS], ktb[:, par, hp],
                                        qbd[:, par, hp], start=hp == 0, stop=False, skip_group_check=True)
                ins.then_inc(s_zs, 1)

            def log_terms(b, par):
                z = bank[2 + par]
                pe.wait_ge(s_sps, 2 * b + 2)
                pe.matmul(z[:, :], um[:, :], sps[:, :], start=False, stop=False, skip_group_check=True)
                pe.wait_ge(s_spn, b + 1)
                pe.matmul(z[:, (KB - 1) * P:], neg[0:TS, :], spn_rows[0:TS, :], start=False, stop=True,
                          skip_group_check=True)
                pe.wait_ge(s_spl, 3 * b + 3)
                pe.matmul(z[:, 0:(KB - 1) * P], neg[:, :], spl[:].rearrange("p k c -> p (k c)"), start=False, stop=True,
                          skip_group_check=True)
                pe.matmul(small[par][0:TS, 0:P], um[0:TS, 0:TS], spn_rows[0:TS, :], start=False, stop=True,
                          skip_group_check=True).then_inc(s_accs, 1)

            def sample_values(b, par, i):
                pe.wait_ge(s_eas, 2 * b + 2)
                pe.wait_ge(s_ams, b + 1)
                pe.wait_ge(s_vcl, 32 * b + 32)
                for hp in range(2 * i, 2 * i + 2):
                    out = small[par][:, P + hp * 2 * TS:P + (hp + 1) * 2 * TS]
                    for kb in range(KB):
                        pe.matmul(out, vc[:, kb, hp * P:(hp + 1) * P],
                                  a_s[:, kb * P + hp * 2 * TS:kb * P + (hp + 1) * 2 * TS],
                                  start=kb == 0, stop=False, skip_group_check=True)
                    ins = pe.matmul(out, vn[:, hp * P:(hp + 1) * P], an[:, hp * 2 * TS:(hp + 1) * 2 * TS],
                                    start=False, stop=True, skip_group_check=True)
                if i == 1:
                    ins.then_inc(s_avs, 1)

            def sequence(b, c, par):
                if is_zero(b):
                    gate_half(c, 0)
                    keys(b, 0)
                else:
                    keys(b, 0)
                    gate_half(c, 0)
                    log_terms(b - 1, 1 - par)
                scores_of(b, 0, par)
                keys(b, 1)
                gate_half(c, 1)
                scores_of(b, 1, par)
                for i in range(2):
                    branch_half(c, i, ch, cl)
                    if not is_zero(b):
                        sample_values(b - 1, 1 - par, i)

            pe.wait_ge(s_al, HP)
            pe.wait_ge(s_cl, KW)
            sequence(0, 0, 0)
            sequence(1, 1, 1)
            with pe.Fori(1, 4) as i:
                sequence(2 * i, (i, 0), 0)
                sequence(2 * i + 1, (i, 1), 1)

            gate_half(8, 0)
            log_terms(B - 1, 1)
            gate_half(8, 1)
            for i in range(2):
                sample_values(B - 1, 1, i)
            pe.wait_ge(s_al, HP + 1)
            branch(8, ah, al)
            gate_half(9, 0)
            gate_half(9, 1)
            branch(9, ah, al)
            with pe.Fori(5, NB // 2) as i:
                for n in range(2):
                    gate_half((i, n), 0)
                    gate_half((i, n), 1)
                    branch((i, n), ah, al)

            natural(U_D, 4, F_D, hh, hl, before_unit=lambda i: pe.wait_ge(s_ml, 2 * i + 2))
            pe.wait_ge(s_ple, 32)
            pe.wait_ge(s_m, 2 * KD)
            for t in range(NT):
                tr_rows(G_PLE + t, praw[:, t], n=2)
            def h2_rows(t):
                pe.wait_ge(s_hn, NT + t + 1)
                for half in range(2):
                    tr_rows(G_R + 2 * t + half, h2[:, t, half * W:(half + 1) * W])

            def router(t):
                pe.wait_ge(s_trf, G_R + 2 * t + 2)
                for k in range(KD):
                    ins = pe.matmul(bank[6][:, t * (NG + NE):(t + 1) * (NG + NE)], h2T[:, k, t * P:(t + 1) * P],
                                    wr[:, k], start=k == 0, stop=k == KD - 1, skip_group_check=True)
                return ins

            def h2_between(t, i):
                if i == 0 and t >= 2:
                    h2_rows(t - 2)
                if i == 1 and t >= 3:
                    router(t - 3)

            tile_by_tile(U_D + 4, F_D + NT, hh, hl, h2_between)
            h2_rows(NT - 2)

            def p_tile(i, t):
                if t == 1:
                    router(NT - 3)
                if t == 2:
                    h2_rows(NT - 1)
                if t == 3:
                    router(NT - 2)
                if t == 4:
                    router(NT - 1).then_inc(s_rt, 1)

            natural(U_P, 1, F_P, ph, pl, before_tile=p_tile)
            pe.wait_ge(s_M, 1)
            for t in range(NT):
                out = bank[6][:, P + t * NE:P + (t + 1) * NE]
                ins = pe.matmul(out, before[:, :], Mb[:, t], start=True, stop=t == 0, skip_group_check=True)
                for s in range(t):
                    ins = pe.matmul(out, onesb[:, :], Mb[:, s], start=False, stop=s == t - 1, skip_group_check=True)
            ins.then_inc(s_rk, 1)

            def over_sum(i, t):
                if t == 1:
                    pe.wait_ge(s_ovm, 1)
                    pe.matmul(bank[7][0:1, 0:1], ovm[:, 0:1], ones1[:, 0:1], start=True, stop=True).then_inc(s_ov, 1)

            natural(U_P + 1, 1, F_P + NT, ph, pl, before_tile=over_sum)

            def expert_rows(e, par, turn):
                pe.wait_ge(s_xe[par], 16 * turn + 16)
                for half in range(2):
                    if not (isinstance(e, int) and e == 0):
                        pe.wait_ge(s_xl, 2 * e - 1 + half)
                    for q in range(4):
                        ins = pe.transpose(bank[4 + half][:, q * P:(q + 1) * P],
                                           xe[:, par, (4 * half + q) * P:(4 * half + q + 1) * P], ident[:, :])
                    ins.then_inc(s_xt, 1)

            def product(u, out, a_hi, a_lo, k0, first, last):
                pe.wait_ge(s_lo, u.count())
                for kk in range(2):
                    ins = three(pe, out, a_hi[:, k0 + kk], a_lo[:, k0 + kk], whi[:, u.slot, kk], wlo[:, u.slot, kk],
                                first and kk == 0, last and kk == 1)
                ins.then_inc(s_mm, 5)

            def gate_or_up(u, e, which):
                if which == 0:
                    pe.wait_ge(s_xl, 2 * e + 2)
                    pe.wait_ge(s_si, e)
                else:
                    pe.wait_ge(s_hm, e)
                for i in range(4):
                    product(u.plus(i), bank[which][:, :], xh, xl, 2 * i, i == 0, i == 3)

            def hidden_rows(e):
                pe.wait_ge(s_hm, e + 1)
                pe.wait_ge(s_htl, e)
                for q in range(4):
                    ins = pe.transpose(bank[6][:, q * P:(q + 1) * P], hm[:, q * P:(q + 1) * P], ident[:, :])
                ins.then_inc(s_ht, 1)

            def down(u, e):
                pe.wait_ge(s_htl, e + 1)
                for n in range(2):
                    pe.wait_ge(s_y, 2 * e)
                    for i in range(2):
                        product(u.plus(2 * n + i), bank[2 + n][:, :], mh, ml, 2 * i, i == 0, i == 1)

            pe.wait_ge(s_free, F_G)
            expert_rows(0, 0, 0)
            gate_or_up(Unit(U_M), 0, 0)
            gate_or_up(Unit(U_M + 4), 0, 1)
            expert_rows(1, 1, 0)

            def expert(e, par, turn, rows_next=True):
                u = Unit(U_M - 4, NSTREAM, e)
                gate_or_up(u, e, 0)
                hidden_rows(e - 1)
                gate_or_up(u.plus(4), e, 1)
                if rows_next:
                    expert_rows(e + 1, 1 - par, turn)
                down(u.plus(8), e - 1)

            expert(1, 1, 1)
            expert(2, 0, 1)
            with pe.Fori(1, NE // 2 - 1) as i:
                expert(2 * i + 1, 1, i + 1)
                expert(2 * i + 2, 0, i + 1)
            expert(NE - 1, 1, 0, rows_next=False)
            hidden_rows(NE - 1)
            down(Unit(U_G - 4), NE - 1)

            pe.wait_ge(s_flag, 1)
            over = pe.value_load(flag[0:1, 0:1], min_val=0, max_val=1)
            with pe.If(over > 0):
                with pe.Fori(0, NE * OV_TILES) as o:
                    pe.wait_ge(s_o_dve, 3 * o + 3)
                    pe.wait_ge(s_o_act, 3 * o + 3)
                    pe.wait_ge(s_o_x, 16 * o + 16)
                    for k in range(KD):
                        ins = pe.transpose(bank[4 + k // 4][:, (k % 4) * P:(k % 4 + 1) * P], xe[:, 0, k * P:(k + 1) * P],
                                           ident[:, :])
                    ins.then_inc(s_o_pe, 1)
                    pe.wait_ge(s_o_dve, 3 * o + 4)
                    for j in range(12):
                        if j == 8:
                            pe.wait_ge(s_o_dve, 3 * o + 5)
                            for q in range(4):
                                ins = pe.transpose(bank[6][:, q * P:(q + 1) * P], hm[:, q * P:(q + 1) * P], ident[:, :])
                            ins.then_inc(s_o_pe, 1)
                            pe.wait_ge(s_o_dve, 3 * o + 6)
                        pe.wait_ge(s_o_raw[j % RING], 48 * o + 16 * (j // RING) + 16)
                        a, k0, nk = (oxT, 2 * (j % 4), KD) if j < 8 else (omT, 2 * (j % 2), FE // P)
                        out = bank[j // 4] if j < 8 else bank[2 + (j - 8) // 2]
                        for kk in range(2):
                            ins = pe.matmul(out[:, :], a[:, k0 + kk], raw[:, j % RING, kk], start=k0 + kk == 0,
                                            stop=k0 + kk == nk - 1)
                        ins.then_inc(s_o_pe, 1)

            def rows3(t):
                pe.wait_ge(s_hn, 2 * NT + t + 1)
                for half in range(2):
                    tr_rows(G_F + 2 * t + half, hn3[:, t % 2, half * W:(half + 1) * W])

            def g_between(t, i):
                if t == 0 and i == 0:
                    rows3(0)
                if i == 0:
                    pe.wait_ge(s_trf, G_F + 2 * t + 2)
                if i == 1 and t + 1 < NT:
                    rows3(t + 1)

            tile_by_tile(U_G, F_G, hh, hl, g_between)
            natural(U_G + 4, 4, F_G + NT, hh, hl)


def kernel(**inputs):
    import concourse.bacc as bacc
    from concourse.bass_utils import run_bass_kernel_spmd

    nc = bacc.Bacc("TRN2", target_bir_lowering=False, num_devices=1)
    arrays, I = {}, {}
    for name, a in inputs.items():
        a = np.ascontiguousarray(a)
        arrays["in_" + name] = a
        I[name] = nc.dram_tensor("in_" + name, a.shape, mybir.dt.from_np(a.dtype), kind="ExternalInput").ap()
    shapes = [(1, TP, D), (B, TS, D), (1, 1, TP, H, HD), (1, 1, TP, H, HD), (1, 1, 2, W),
              (1, B, TS, H, HD), (1, B, TS, H, HD), (1, B, 2, W)]
    O = [nc.dram_tensor(f"out_{i}", s, F32, kind="ExternalOutput").ap() for i, s in enumerate(shapes)]
    program(nc, I, O)
    r = run_bass_kernel_spmd(nc, [arrays], core_ids=[0])
    return tuple(r.results[0][f"out_{i}"] for i in range(len(shapes)))
```
